# Optimizing a Trainium2 kernel written in Bass

```python
import math
import jax, jax.numpy as jnp
from jax import lax
import numpy as np

D_MODEL = 1024
BATCH = 1
SEQ = 512
DEPTH = 1

HEAD_DIM = 64
DIL_GROUPS = ((128, 1), (512, 4), (2048, 16))
N_GROUPS = 3
HEADS_PER_GROUP = 4
N_ATTN_HEADS = N_GROUPS * HEADS_PER_GROUP
ATTN_W = N_ATTN_HEADS * HEAD_DIM
ATTN_OUT_W = HEADS_PER_GROUP * HEAD_DIM
BLK = 128
SGU_CHUNK = 128
SGU_GROUPS = 4
SGU_W = 512
SGU_GROUP_W = SGU_W // SGU_GROUPS
N_BRANCH = 2
IN_W = 3 * ATTN_W + 2 * SGU_W + N_BRANCH * D_MODEL
MEM_LEN = 256
MEM_HEADS = 4
MEM_HEAD_DIM = 128
MEM_W = MEM_HEADS * MEM_HEAD_DIM
D_FF = -(-8 * D_MODEL // (3 * 256)) * 256
EPS = 1e-6


def rmsnorm(x, g):
    xf = x.astype(jnp.float32)
    r = lax.rsqrt(jnp.mean(xf * xf, axis=-1, keepdims=True) + EPS)
    return (xf * r * g.astype(jnp.float32)).astype(x.dtype)

def alibi_slopes_grouped():
    def pow2(n):
        start = 2.0 ** (-8.0 / n)
        return [start ** (i + 1) for i in range(n)]
    n = N_ATTN_HEADS
    if math.log2(n).is_integer():
        s = pow2(n)
    else:
        c = 2 ** int(math.floor(math.log2(n)))
        s = pow2(c) + pow2(2 * c)[0::2][: n - c]
    s = np.array(sorted(s, reverse=True), dtype=np.float32)
    return s.reshape(N_GROUPS, HEADS_PER_GROUP)

def dilated_causal_window_attention(q, k, v, slopes, window, dilation):
    B, S, H, Dh = q.shape
    n_back = window // dilation
    assert n_back <= BLK
    sub_len = -(-S // dilation)
    L = -(-sub_len // BLK) * BLK
    S_pad = L * dilation
    nb = L // BLK

    def to_blocks(t):
        t = jnp.pad(t, ((0, 0), (0, S_pad - S), (0, 0), (0, 0)))
        t = t.reshape(B, nb, BLK, dilation, H, Dh)
        return t.transpose(0, 3, 4, 1, 2, 5)

    def with_prev(t):
        prev = jnp.pad(t, ((0, 0), (0, 0), (0, 0), (1, 0), (0, 0), (0, 0)))[:, :, :, :-1]
        return jnp.concatenate([prev, t], axis=4)

    qb = to_blocks(q)
    kk = with_prev(to_blocks(k))
    vv = with_prev(to_blocks(v))

    s = jnp.einsum('brhnqd,brhnkd->brhnqk', qb, kk).astype(jnp.float32) * (Dh ** -0.5)
    steps = (np.arange(BLK)[:, None] + BLK) - np.arange(2 * BLK)[None, :]
    band = (steps >= 0) & (steps <= n_back)
    no_prev = (np.arange(nb)[:, None, None] == 0) & (np.arange(2 * BLK)[None, None, :] < BLK)
    valid = band[None] & ~no_prev
    dist = jnp.asarray((np.clip(steps, 0, None) * dilation).astype(np.float32))
    bias = -jnp.asarray(slopes)[:, None, None, None] * dist[None, None]
    s = jnp.where(jnp.asarray(valid), s + bias, -jnp.inf)
    mx = jnp.max(s, axis=-1, keepdims=True)
    e = jnp.exp(s - mx)
    den = jnp.sum(e, axis=-1, keepdims=True)
    o = jnp.einsum('brhnqk,brhnkd->brhnqd', e, vv.astype(jnp.float32)) / den
    lse = (mx + jnp.log(den))[..., 0]
    o = o.transpose(0, 3, 4, 1, 2, 5).reshape(B, S_pad, H, Dh)[:, :S]
    lse = lse.transpose(0, 3, 4, 1, 2).reshape(B, S_pad, H)[:, :S]
    return o, lse

def spatial_gating(uv, w_s, b_s, g):
    B, S, _ = uv.shape
    z = jax.nn.gelu(uv)
    u, v = jnp.split(z, 2, axis=-1)
    v = rmsnorm(v, g)
    v = v.reshape(B, S // SGU_CHUNK, SGU_CHUNK, SGU_GROUPS, SGU_GROUP_W)
    mixed = jnp.einsum('gts,bnsgc->bntgc', jnp.tril(w_s), v) + b_s.T[:, :, None]
    return u * mixed.reshape(B, S, SGU_W)

def memory_cross_attention(c, m, w_q, w_kv, w_o):
    B, S, _ = c.shape
    M = m.shape[1]
    q = (c @ w_q).reshape(B, S, MEM_HEADS, MEM_HEAD_DIM)
    kv = (m @ w_kv).reshape(B, M, 2, MEM_HEADS, MEM_HEAD_DIM)
    k, v = kv[:, :, 0], kv[:, :, 1]
    s = jnp.einsum('bshd,bmhd->bhsm', q, k).astype(jnp.float32) * (MEM_HEAD_DIM ** -0.5)
    p = jax.nn.softmax(s, axis=-1)
    o = jnp.einsum('bhsm,bmhd->bshd', p, v.astype(jnp.float32)).astype(c.dtype)
    return o.reshape(B, S, MEM_W) @ w_o

def first_inputs(seed: int = 0) -> dict:
    key = jax.random.key(seed)
    ks = jax.random.split(key, 24)
    f32 = jnp.float32

    def nrm(k, shape, scale):
        return jax.random.normal(k, shape, f32) * scale

    def gain(k, shape):
        return 1.0 + 0.02 * jax.random.normal(k, shape, f32)

    L = DEPTH
    return {
        "x": nrm(ks[0], (BATCH, SEQ, D_MODEL), 1.0),
        "mem": nrm(ks[1], (BATCH, MEM_LEN, D_MODEL), 1.0),
        "g_mix": gain(ks[2], (L, D_MODEL)),
        "w_in": nrm(ks[3], (L, D_MODEL, IN_W), D_MODEL ** -0.5),
        "b_gate": nrm(ks[4], (L, N_BRANCH * D_MODEL), 0.1),
        "w_sgu_spatial": nrm(ks[5], (L, SGU_GROUPS, SGU_CHUNK, SGU_CHUNK), 0.5 * SGU_CHUNK ** -0.5),
        "b_sgu_spatial": 1.0 + nrm(ks[6], (L, SGU_GROUPS, SGU_CHUNK), 0.1),
        "g_sgu": gain(ks[7], (L, SGU_W)),
        "w_branch_attn": nrm(ks[8], (L, ATTN_OUT_W, D_MODEL), ATTN_OUT_W ** -0.5),
        "w_branch_sgu": nrm(ks[9], (L, SGU_W, D_MODEL), SGU_W ** -0.5),
        "w_out": nrm(ks[10], (L, D_MODEL, D_MODEL), D_MODEL ** -0.5),
        "g_cross": gain(ks[11], (L, D_MODEL)),
        "g_mem": gain(ks[12], (L, D_MODEL)),
        "w_q_cross": nrm(ks[13], (L, D_MODEL, MEM_W), D_MODEL ** -0.5),
        "w_kv_cross": nrm(ks[14], (L, D_MODEL, 2 * MEM_W), D_MODEL ** -0.5),
        "w_o_cross": nrm(ks[15], (L, MEM_W, D_MODEL), MEM_W ** -0.5),
        "g_ffn": gain(ks[16], (L, D_MODEL)),
        "w_gate_up": nrm(ks[17], (L, D_MODEL, 2 * D_FF), D_MODEL ** -0.5),
        "w_down": nrm(ks[18], (L, D_FF, D_MODEL), D_FF ** -0.5),
        "g_final": gain(ks[19], (D_MODEL,)),
    }

def first_block(x, mem, g_mix, w_in, b_gate, w_sgu_spatial, b_sgu_spatial, g_sgu,
              w_branch_attn, w_branch_sgu, w_out, g_cross, g_mem, w_q_cross,
              w_kv_cross, w_o_cross, g_ffn, w_gate_up, w_down, g_final):
    B, S, D = x.shape
    slopes = alibi_slopes_grouped()
    h = x
    for l in range(DEPTH):
        a = rmsnorm(h, g_mix[l])
        proj = a @ w_in[l]
        q, k, v, uv, gl = jnp.split(
            proj, [ATTN_W, 2 * ATTN_W, 3 * ATTN_W, 3 * ATTN_W + 2 * SGU_W], axis=-1)
        q = q.reshape(B, S, N_GROUPS, HEADS_PER_GROUP, HEAD_DIM)
        k = k.reshape(B, S, N_GROUPS, HEADS_PER_GROUP, HEAD_DIM)
        v = v.reshape(B, S, N_GROUPS, HEADS_PER_GROUP, HEAD_DIM)
        outs, lses = [], []
        for gi, (win, dil) in enumerate(DIL_GROUPS):
            o, lse = dilated_causal_window_attention(
                q[:, :, gi], k[:, :, gi], v[:, :, gi], slopes[gi], win, dil)
            outs.append(o)
            lses.append(lse)
        outs = jnp.stack(outs)
        alpha = jax.nn.softmax(jnp.stack(lses), axis=0)
        y_attn = jnp.sum(alpha[..., None] * outs, axis=0).reshape(B, S, ATTN_OUT_W).astype(x.dtype)

        y_sgu = spatial_gating(uv, w_sgu_spatial[l], b_sgu_spatial[l], g_sgu[l])

        gates = jax.nn.sigmoid((gl + b_gate[l]).astype(jnp.float32)).astype(x.dtype)
        gates = gates.reshape(B, S, N_BRANCH, D)
        merged = (gates[:, :, 0] * (y_attn @ w_branch_attn[l])
                  + gates[:, :, 1] * (y_sgu @ w_branch_sgu[l]))
        h = h + merged @ w_out[l]

        c = rmsnorm(h, g_cross[l])
        m = rmsnorm(mem, g_mem[l])
        h = h + memory_cross_attention(c, m, w_q_cross[l], w_kv_cross[l], w_o_cross[l])

        f = rmsnorm(h, g_ffn[l])
        gt, up = jnp.split(f @ w_gate_up[l], 2, axis=-1)
        h = h + (jax.nn.silu(gt) * up) @ w_down[l]
    return rmsnorm(h, g_final)


CONV_CH = D_MODEL
CONV_K = 31
HEAD_DIM_2 = 128
N_HEADS = D_MODEL // HEAD_DIM_2
DELTA_W = N_HEADS * HEAD_DIM_2
SHORT_CONV = 5
N_DIR = 2
CHUNK = 64
D_FF_2 = -(-8 * D_MODEL // (3 * 256)) * 256
PLE_DIM = 256
NORM_EPS = 1e-6
LN_EPS = 1e-5
IN_SIZES = (CONV_CH, CONV_CH, DELTA_W, DELTA_W, DELTA_W, DELTA_W,
            N_DIR * N_HEADS, N_DIR * N_HEADS, D_MODEL, D_MODEL)
IN_TOTAL = sum(IN_SIZES)


def rms_norm(x, g):
    xf = x.astype(jnp.float32)
    y = xf * lax.rsqrt(jnp.mean(xf * xf, axis=-1, keepdims=True) + NORM_EPS)
    return (y * g.astype(jnp.float32)).astype(x.dtype)

def layer_norm(x, g, b):
    xf = x.astype(jnp.float32)
    mu = jnp.mean(xf, axis=-1, keepdims=True)
    xc = xf - mu
    y = xc * lax.rsqrt(jnp.mean(xc * xc, axis=-1, keepdims=True) + LN_EPS)
    return (y * g.astype(jnp.float32) + b.astype(jnp.float32)).astype(x.dtype)

def l2_norm(x):
    xf = x.astype(jnp.float32)
    return xf * lax.rsqrt(jnp.sum(xf * xf, axis=-1, keepdims=True) + NORM_EPS)

def depthwise_conv(x, w):
    k = w.shape[0]
    return lax.conv_general_dilated(
        x, w[:, None, :].astype(x.dtype), window_strides=(1,),
        padding=[(k // 2, k // 2)], dimension_numbers=("NWC", "WIO", "NWC"),
        feature_group_count=x.shape[-1])

def split_cols(t, sizes):
    out, start = [], 0
    for s in sizes:
        out.append(t[..., start:start + s])
        start += s
    return out

def gated_delta_rule(q, k, v, g, beta):
    out_dtype = v.dtype
    bsz, t_len, n_h, _ = q.shape
    n_blk = t_len // CHUNK

    def blocks(t):
        t = t.astype(jnp.float32).reshape((bsz, n_blk, CHUNK, n_h) + t.shape[3:])
        return jnp.moveaxis(t, 3, 1)

    q, k, v, g, beta = (blocks(t) for t in (q, k, v, g, beta))
    g = jnp.cumsum(g, axis=-1)
    idx = jnp.arange(CHUNK)
    tri_incl = idx[:, None] >= idx[None, :]
    tri_strict = idx[:, None] > idx[None, :]
    decay = jnp.exp(jnp.where(tri_incl, g[..., :, None] - g[..., None, :], -jnp.inf))
    k_beta = k * beta[..., None]
    lower = jnp.where(tri_strict, jnp.einsum('bhncd,bhnsd->bhncs', k_beta, k) * decay, 0.0)
    dv = v.shape[-1]
    rhs = jnp.concatenate([v * beta[..., None], k_beta * jnp.exp(g)[..., None]], axis=-1)
    sol = lax.linalg.triangular_solve(lower, rhs, left_side=True, lower=True, unit_diagonal=True)
    u, w = sol[..., :dv], sol[..., dv:]
    qk = jnp.einsum('bhncd,bhnsd->bhncs', q, k) * decay
    g_last = g[..., -1]
    q_dec = q * jnp.exp(g)[..., None]
    k_tail = k * jnp.exp(g_last[..., None] - g)[..., None]

    def step(state, xs):
        qd, kt, ui, wi, qki, gl = xs
        v_new = ui - jnp.einsum('bhck,bhkv->bhcv', wi, state)
        o = jnp.einsum('bhck,bhkv->bhcv', qd, state) + jnp.einsum('bhcs,bhsv->bhcv', qki, v_new)
        state = state * jnp.exp(gl)[..., None, None] + jnp.einsum('bhck,bhcv->bhkv', kt, v_new)
        return state, o

    xs = tuple(jnp.moveaxis(t, 2, 0) for t in (q_dec, k_tail, u, w, qk, g_last))
    s0 = jnp.zeros((bsz, n_h, q.shape[-1], dv), jnp.float32)
    _, o = lax.scan(step, s0, xs)
    o = jnp.transpose(o, (1, 0, 3, 2, 4)).reshape(bsz, t_len, n_h, dv)
    return o.astype(out_dtype)

def second_inputs(seed: int = 0) -> dict:
    key = jax.random.key(seed)
    ks = jax.random.split(key, 32)
    f32 = jnp.float32

    def nrm(k, shape, fan_in):
        return jax.random.normal(k, shape, f32) * (fan_in ** -0.5)

    def gain(k, shape):
        return 1.0 + 0.05 * jax.random.normal(k, shape, f32)

    def small(k, shape):
        return 0.01 * jax.random.normal(k, shape, f32)

    a_log = jnp.log(jax.random.uniform(ks[10], (DEPTH, N_DIR, N_HEADS), f32, 1.0, 16.0))
    dt = jnp.exp(jax.random.uniform(ks[11], (DEPTH, N_DIR, N_HEADS), f32,
                                    float(np.log(1e-3)), float(np.log(1e-1))))
    dt_bias = dt + jnp.log(-jnp.expm1(-dt))
    return {
        "x": jax.random.normal(ks[0], (BATCH, SEQ, D_MODEL), f32),
        "p": jax.random.normal(ks[1], (DEPTH, BATCH, SEQ, PLE_DIM), f32),
        "g_mix": gain(ks[2], (DEPTH, D_MODEL)),
        "w_in": nrm(ks[3], (DEPTH, D_MODEL, IN_TOTAL), D_MODEL),
        "conv_dw_w": nrm(ks[4], (DEPTH, CONV_K, CONV_CH), CONV_K),
        "conv_dw_b": small(ks[5], (DEPTH, CONV_CH)),
        "conv_ln_g": gain(ks[6], (DEPTH, CONV_CH)),
        "conv_ln_b": small(ks[7], (DEPTH, CONV_CH)),
        "w_conv_out": nrm(ks[8], (DEPTH, CONV_CH, D_MODEL), CONV_CH),
        "qkv_conv_w": nrm(ks[9], (DEPTH, SHORT_CONV, 3 * DELTA_W), SHORT_CONV),
        "a_log": a_log,
        "dt_bias": dt_bias,
        "delta_norm_g": gain(ks[12], (DEPTH, HEAD_DIM_2)),
        "w_delta_out": nrm(ks[13], (DEPTH, DELTA_W, D_MODEL), DELTA_W),
        "w_o": nrm(ks[14], (DEPTH, D_MODEL, D_MODEL), D_MODEL),
        "g_ffn": gain(ks[15], (DEPTH, D_MODEL)),
        "w_gate_up": nrm(ks[16], (DEPTH, D_MODEL, 2 * D_FF_2), D_MODEL),
        "w_down": nrm(ks[17], (DEPTH, D_FF_2, D_MODEL), D_FF_2),
        "g_pl": gain(ks[18], (DEPTH, D_MODEL)),
        "w_pl_gate": nrm(ks[19], (DEPTH, D_MODEL, D_MODEL), D_MODEL),
        "w_pl_proj": nrm(ks[20], (DEPTH, PLE_DIM, D_MODEL), PLE_DIM),
        "g_pl_proj": gain(ks[21], (DEPTH, D_MODEL)),
        "g_final": gain(ks[22], (D_MODEL,)),
    }

def second_block(x, p, g_mix, w_in, conv_dw_w, conv_dw_b, conv_ln_g, conv_ln_b, w_conv_out,
              qkv_conv_w, a_log, dt_bias, delta_norm_g, w_delta_out, w_o, g_ffn,
              w_gate_up, w_down, g_pl, w_pl_gate, w_pl_proj, g_pl_proj, g_final):
    bsz, t_len, _ = x.shape
    for i in range(DEPTH):
        h = rms_norm(x, g_mix[i])
        proj = h @ w_in[i]
        glu_a, glu_b, q, k, v, z, a_in, b_in, gate_a, gate_b = split_cols(proj, IN_SIZES)

        c = glu_a * jax.nn.sigmoid(glu_b)
        c = depthwise_conv(c, conv_dw_w[i]) + conv_dw_b[i]
        c = jax.nn.silu(layer_norm(c, conv_ln_g[i], conv_ln_b[i]))
        y_conv = c @ w_conv_out[i]

        qkv = jax.nn.silu(depthwise_conv(jnp.concatenate([q, k, v], axis=-1), qkv_conv_w[i]))
        q, k, v = split_cols(qkv, (DELTA_W, DELTA_W, DELTA_W))
        q = l2_norm(q.reshape(bsz, t_len, N_HEADS, HEAD_DIM_2)) * (HEAD_DIM_2 ** -0.5)
        k = l2_norm(k.reshape(bsz, t_len, N_HEADS, HEAD_DIM_2))
        v = v.reshape(bsz, t_len, N_HEADS, HEAD_DIM_2)
        a_in = a_in.astype(jnp.float32).reshape(bsz, t_len, N_DIR, N_HEADS)
        b_in = b_in.astype(jnp.float32).reshape(bsz, t_len, N_DIR, N_HEADS)
        g = -jnp.exp(a_log[i].astype(jnp.float32)) * jax.nn.softplus(a_in + dt_bias[i].astype(jnp.float32))
        beta = jax.nn.sigmoid(b_in)
        o_fwd = gated_delta_rule(q, k, v, g[:, :, 0], beta[:, :, 0])
        rev = lambda t: jnp.flip(t, axis=1)
        o_bwd = rev(gated_delta_rule(rev(q), rev(k), rev(v), rev(g[:, :, 1]), rev(beta[:, :, 1])))
        o = rms_norm(o_fwd + o_bwd, delta_norm_g[i]) * jax.nn.silu(z.reshape(bsz, t_len, N_HEADS, HEAD_DIM_2))
        y_delta = o.reshape(bsz, t_len, DELTA_W).astype(x.dtype) @ w_delta_out[i]

        y = jax.nn.sigmoid(gate_a) * y_conv + jax.nn.sigmoid(gate_b) * y_delta
        x = x + y @ w_o[i]

        h = rms_norm(x, g_ffn[i])
        gt, up = split_cols(h @ w_gate_up[i], (D_FF_2, D_FF_2))
        x = x + (jax.nn.silu(gt) * up) @ w_down[i]

        pl = rms_norm(p[i] @ w_pl_proj[i], g_pl_proj[i])
        x = x + jax.nn.sigmoid(rms_norm(x, g_pl[i]) @ w_pl_gate[i]) * pl
    return rms_norm(x, g_final)


def setup_inputs(seed=0):
    out = dict(first_inputs(seed))
    for name, value in second_inputs(seed + 1).items():
        if name != "x":
            out[name + "_2"] = value
    return out


def reference(
    x, mem, g_mix, w_in, b_gate, w_sgu_spatial, b_sgu_spatial, g_sgu, w_branch_attn,
    w_branch_sgu, w_out, g_cross, g_mem, w_q_cross, w_kv_cross, w_o_cross, g_ffn, w_gate_up,
    w_down, g_final, p_2, g_mix_2, w_in_2, conv_dw_w_2, conv_dw_b_2, conv_ln_g_2, conv_ln_b_2,
    w_conv_out_2, qkv_conv_w_2, a_log_2, dt_bias_2, delta_norm_g_2, w_delta_out_2, w_o_2,
    g_ffn_2, w_gate_up_2, w_down_2, g_pl_2, w_pl_gate_2, w_pl_proj_2, g_pl_proj_2, g_final_2,
):
    x = first_block(
        x, mem, g_mix, w_in, b_gate, w_sgu_spatial, b_sgu_spatial, g_sgu, w_branch_attn,
        w_branch_sgu, w_out, g_cross, g_mem, w_q_cross, w_kv_cross, w_o_cross, g_ffn, w_gate_up,
        w_down, g_final,
    )
    return second_block(
        x, p_2, g_mix_2, w_in_2, conv_dw_w_2, conv_dw_b_2, conv_ln_g_2, conv_ln_b_2,
        w_conv_out_2, qkv_conv_w_2, a_log_2, dt_bias_2, delta_norm_g_2, w_delta_out_2, w_o_2,
        g_ffn_2, w_gate_up_2, w_down_2, g_pl_2, w_pl_gate_2, w_pl_proj_2, g_pl_proj_2,
        g_final_2,
    )


_drawn_inputs = setup_inputs


def setup_inputs(seed=0):
    import zlib

    import numpy as np

    out = dict(_drawn_inputs(seed))
    spreads = {}
    factors = {'g_mix': 4.542,
     'b_gate': 3.007,
     'g_sgu': 8.0,
     'g_cross': 8.0,
     'g_mem': 8.0,
     'g_ffn': 3.646,
     'conv_dw_b_2': 8.0,
     'conv_ln_g_2': 3.219,
     'conv_ln_b_2': 27.012,
     'delta_norm_g_2': 3.763,
     'g_pl_2': 23.326,
     'g_pl_proj_2': 9.692,
     'g_ffn_2': 2.695}
    for name, (base, spread) in spreads.items():
        noise = np.random.default_rng([zlib.crc32(name.encode()), seed]).standard_normal(out[name].shape)
        drawn = base * np.exp(spread * noise) if base else spread * noise
        out[name] = __import__('jax').numpy.asarray(drawn.astype(out[name].dtype))
    for name, factor in factors.items():
        out[name] = (out[name] * factor).astype(out[name].dtype)
    return out
```

```python
from contextlib import ExitStack

import numpy as np

import concourse.bass as bass
from concourse import mybir

F32 = mybir.dt.float32
F32R = mybir.dt.float32r
ALU = mybir.AluOpType
ACT = mybir.ActivationFunctionType
AX_X = mybir.AxisListType.X

P = 128
D = 1024
DC = D // P
T = 512
TC = T // P
RING = 4
LEAD = 3
BLOCK = 1024
ACCS = 4
EPS = 1e-6
LN_EPS = 1e-5
HD = 64
FF = 2816
FC = FF // P
NM = 256
BIG = 1e30
CONV_K = 31
CONV_PAD = CONV_K // 2
SHORT_K = 5
SHORT_PAD = SHORT_K // 2
HEADS = 8
DIRS = 2
LEVELS = 6


def alibi_slopes():
    def pow2(n):
        start = 2.0 ** (-8.0 / n)
        return [start ** (i + 1) for i in range(n)]
    s = pow2(8) + pow2(16)[0::2][:4]
    return np.array(sorted(s, reverse=True), dtype=np.float32).reshape(3, 4)


def shape_constants():
    p = np.arange(P)
    eye = np.eye(P, dtype=np.float32)
    dist = np.full((P, TC, T), BIG, np.float32)
    for r in range(4):
        q = (4 * p + r)[:, None]
        k = np.arange(T)[None, :]
        ok = (q - k >= 0) & (q - k <= 128)
        dist[:, r][ok] = (q - k)[ok]
    steps = (p[:, None] - p[None, :]).astype(np.float32)
    d4 = np.where(steps >= 0, steps * 4, BIG).astype(np.float32)
    d16 = np.where((steps >= 0) & (steps % 4 == 0), steps * 4, BIG).astype(np.float32)
    dist2 = np.stack([d4, d16], 1)
    upper = (p[:, None] <= p[None, :]).astype(np.float32)
    level = np.zeros((P, DIRS, LEVELS + 1, P), np.float32)
    incl = np.zeros((P, DIRS, P), np.float32)
    for l in range(LEVELS + 1):
        w = 2 ** l
        s, c = p[:, None], p[None, :]
        same = (s // (2 * w)) == (c // (2 * w))
        level[:, 0, l] = same & ((s // w) % 2 == 0) & ((c // w) % 2 == 1)
        level[:, 1, l] = same & ((s // w) % 2 == 1) & ((c // w) % 2 == 0)
    incl[:, 0] = p[:, None] <= p[None, :]
    incl[:, 1] = p[:, None] >= p[None, :]
    return {"eye": eye, "dist": dist, "dist2": dist2, "upper": upper, "level": level, "incl": incl}


class Steps:

    def __init__(self, eng, sem):
        self.eng, self.sem, self.n, self.reg, self.per = eng, sem, 0, None, 0

    def did(self, ins):
        ins.then_inc(self.sem, 1)
        self.n += 1
        return self.n

    def wait(self, number=None):
        number = self.n if number is None else number
        self.eng.wait_ge(self.sem, number if self.reg is None else self.reg * self.per + number)

    def enter(self, reg, per):
        self.reg, self.per, self.start = reg, per, self.n

    def leave(self, count):
        assert self.n - self.start == self.per, (self.n - self.start, self.per)
        self.reg, self.n = None, self.start + count * self.per


class Stage:
    def __init__(self, name, w, kc, cols, loops, body, cstep, kind="T", kblocks=1):
        self.name, self.w, self.kc, self.cols, self.kind = name, w, kc, cols, kind
        self.loops, self.body, self.cstep, self.kblocks = loops, body, cstep, kblocks
        self.width = cols // P if kind == "T" else 1
        self.accs = loops * len(body) // kblocks * self.width
        assert loops == 1 or (len(body) % RING == 0 and len(body) // kblocks * self.width % ACCS == 0)
        self.n = self.loops * len(self.body)
        assert kc * cols == BLOCK


def stage_cols(name, w, col0, nchunks, kind="T", kc=8):
    cols = BLOCK // kc
    unroll = 4 if nchunks % 4 == 0 else nchunks
    return Stage(name, w, kc, cols, nchunks // unroll, [(0, col0 + j * cols) for j in range(unroll)], unroll * cols, kind)


def stage_pairs(name, w, colA, colB, pairs):
    assert pairs % 2 == 0
    body = [(0, colA), (0, colB), (0, colA + P), (0, colB + P)]
    return Stage(name, w, 8, P, pairs // 2, body, 2 * P)


def stage_down(name, w):
    body = [(2 * j, n) for n in (0, 512) for j in range(FC // 2)]
    return Stage(name, w, 2, 512, 1, body, 0, kblocks=FC // 2)


STAGES = [
    stage_cols("qk", "w_in", 0, 12),
    stage_cols("v", "w_in", 1536, 6, "N"),
    stage_cols("u", "w_in", 2304, 4),
    stage_cols("vv", "w_in", 2816, 4, "N"),
    stage_cols("branch_attn", "w_branch_attn", 0, 2, kc=2),
    stage_cols("gate_attn", "w_in", 3328, 8),
    stage_cols("branch_sgu", "w_branch_sgu", 0, 4, kc=4),
    stage_cols("gate_sgu", "w_in", 4352, 8),
    stage_cols("out", "w_out", 0, 8),
    stage_cols("mem_k", "w_kv_cross", 0, 4),
    stage_cols("mem_v", "w_kv_cross", 512, 4, "N"),
    stage_cols("cross_q", "w_q_cross", 0, 4),
    stage_cols("cross_o", "w_o_cross", 0, 4, kc=4),
    stage_pairs("gate_up", "w_gate_up", 0, FF, FC),
    stage_down("down", "w_down"),
]
STAGES2 = [
    stage_pairs("glu", "w_in_2", 0, D, 8),
    stage_cols("gate_a", "w_in_2", 6 * D + 32, 8),
    stage_cols("conv_out", "w_conv_out_2", 0, 8),
    Stage("heads", "w_in_2", 8, P, 4, [(0, (2 + s) * D + h * P) for h in range(2) for s in range(4)], 2 * P),
    stage_cols("delta_out", "w_delta_out_2", 0, 8),
    stage_cols("gate_b", "w_in_2", 7 * D + 32, 8),
    stage_cols("o2", "w_o_2", 0, 8),
    stage_pairs("gate_up2", "w_gate_up_2", 0, FF, FC),
    stage_down("down2", "w_down_2"),
    stage_cols("pl_proj", "w_pl_proj_2", 0, 2, kc=2),
    stage_cols("pl_gate", "w_pl_gate_2", 0, 8),
]

VECTORS = [("g_mix", 8), ("b_gate", 16), ("g_cross", 8), ("g_mem", 8), ("g_ffn", 8), ("g_final", 8),
           ("g_mix_2", 8), ("conv_dw_b_2", 8), ("conv_ln_g_2", 8), ("conv_ln_b_2", 8), ("g_ffn_2", 8),
           ("g_pl_2", 8), ("g_pl_proj_2", 8), ("g_final_2", 8), ("delta_norm_g_2", 1)]


def build(nc, ins, out, dump=None, upto=99):
    stages = STAGES + (STAGES2 if upto > 1 else [])
    first_block, n = {}, 0
    for s in stages:
        first_block[s.name] = n
        n += s.n
    NB = n
    first_acc, n = {}, 0
    for s in stages:
        first_acc[s.name] = n
        n += s.accs
    by_name = {s.name: s for s in stages}

    vec_at, n = {}, 0
    for name, rows in VECTORS:
        vec_at[name] = n
        n += rows
    NVEC = n

    with ExitStack() as ctx:
        def sb(name, shape, dt=F32, where=ctx):
            return where.enter_context(nc.sbuf_tensor("s_" + name, shape, dt))

        def sem(name):
            return ctx.enter_context(nc.semaphore(name))

        raw = sb("raw", [P, RING, BLOCK])
        whi = sb("whi", [P, RING, BLOCK], F32R)
        wlo = sb("wlo", [P, RING, BLOCK], F32R)
        X = sb("X", [P, DC, T])
        ah = sb("ah", [P, DC, T], F32R)
        al = sb("al", [P, DC, T], F32R)
        eye = sb("eye", [P, P])
        ones = sb("ones", [P, P])
        vec = sb("vec", [P, NVEC])
        eps = sb("eps", [P, 2])
        rbc = sb("rbc", [P, T])
        lnt = sb("lnt", [P, T])
        sq = sb("sq", [P, 2, T])
        nt = sb("nt", [P, 2, T])
        stg = sb("stg", [P, 4, T])

        psum = ctx.enter_context(nc.psum_tensor("psum", [P, 8, T], F32))

        with ExitStack() as one:
            yh = sb("yh", [P, 6, T], F32R, one)
            yl = sb("yl", [P, 6, T], F32R, one)
            with ExitStack() as a:
                vrows = sb("vrows", [P, P], F32, a)
                xin = sb("xin", [P, TC, D], F32, a)
            with ExitStack() as a:
                qk = sb("qk", [P, 12, T], F32, a)
                vt = sb("vt", [P, 4, 768], F32, a)
                uu = sb("uu", [P, 4, T], F32, a)
                vv = sb("vv", [P, TC, 512], F32, a)
                dist = vv
                dist2 = sb("dist2", [P, 2, P], F32, a)
                upper = sb("upper", [P, P], F32, a)
                wsp = sb("wsp", [P, 4, P], F32, a)
                wspT = sb("wspT", [P, 4, P], F32, a)
                brow = sb("brow", [P, 4, P], F32, a)
                grow = lnt
                sc = sb("sc", [P, 2, 768], F32, a)
                ya = stg[:, 0:2, :].rearrange("p a (b n) -> p (a b) n", n=256)
                pT = stg[:, 2:4, :].rearrange("p a n -> p (a n)")
                ss = sb("ss", [P, 16], F32, a)
                rs = sb("rs", [P, 16], F32, a)
                mx = sb("mx", [P, 16], F32, a)
                nmx = sb("nmx", [P, 16], F32, a)
                den = sb("den", [P, 16], F32, a)
                rden = sb("rden", [P, 16], F32, a)
            with ExitStack() as a:
                m1 = sb("m1", [P, DC, T], F32, a)
                m2 = sb("m2", [P, DC, T], F32, a)
            with ExitStack() as a:
                memin = sb("memin", [P, 2, D], F32, a)
                memT = sb("memT", [P, DC, NM], F32, a)
                mh = sb("mh", [P, DC, NM], F32R, a)
                ml = sb("ml", [P, DC, NM], F32R, a)
                ckT = sb("ckT", [P, 4, NM], F32, a)
                cv = sb("cv", [P, 2, 512], F32, a)
                cq = sb("cq", [P, 4, T], F32, a)
                cs = sb("cs", [P, 4, NM], F32, a)
                cpT = sb("cpT", [P, 2, T], F32, a)
                cmx = sb("cmx", [P, 16], F32, a)
                cden = sb("cden", [P, 16], F32, a)
                crd = sb("crd", [P, 16], F32, a)
        with ExitStack() as a:
            hh = sb("hh", [P, FC, T], F32R, a)
            hl = sb("hl", [P, FC, T], F32R, a)

        conv_w = sb("conv_w", [P, CONV_K * 8])
        short_w = sb("short_w", [P, SHORT_K * 24])
        with ExitStack() as two:
            level = sb("level", [P, DIRS, LEVELS + 1, P], F32, two)
            incl = sb("incl", [P, DIRS, P], F32, two)
            zh = sb("zh", [P, DC, T], F32R, two)
            zl = sb("zl", [P, DC, T], F32R, two)
            yg = sb("yg", [P, DC, T], F32, two)
            coef = sb("coef", [P, 5, TC, 16], F32, two)
            hc = sb("hc", [P, 5, TC, DIRS], F32, two)
            with ExitStack() as a:
                cp = sb("cp", [P, DC, T + CONV_K - 1], F32, a)
                crows = sb("crows", [P, 3, P], F32, a)
                abw = sb("abw", [P, DC, 32], F32, a)
                abh = sb("abh", [P, DC, 32], F32R, a)
                abl = sb("abl", [P, DC, 32], F32R, a)
                arow = sb("arow", [P, 2, 16], F32, a)
                ab = sb("ab", [P, TC, 32], F32, a)
                tmp = sb("tmp", [P, 3, TC, 16], F32, a)
                mu = sb("mu", [P, T], F32, a)
            with ExitStack() as a:
                raw3 = sb("raw3", [P, 3, T + SHORT_K - 1], F32, a)
                tok = sb("tok", [P, 2, TC, P], F32, a)
                E_ = sb("E", [P, DIRS, TC, P], F32, a)
                AT = sb("AT", [P, DIRS, TC, P], F32, a)
                EG = sb("EG", [P, DIRS, TC, P], F32, a)
                KB = sb("KB", [P, DIRS, TC, P], F32, a)
                vnew = sb("vnew", [P, DIRS, 2, P], F32, a)
                St = sb("St", [P, DIRS, P], F32, a)
            with ExitStack() as a:
                d2 = sb("d2", [P, DC, T], F32, a)
        XV = X[:, :, :].rearrange("p (k d) (t n) -> p k d t n", k=4, t=TC)
        Mi, MT, QK, QD = XV[:, 0], XV[:, 1], XV[:, 2], XV[:, 3]
        with ExitStack() as a:
            ph = sb("ph", [P, 2, T], F32R, a)
            pl = sb("pl", [P, 2, T], F32R, a)
            pin = sb("pin", [P, TC, 256], F32, a)
            PL = sb("PL", [P, DC, T], F32, a)
            outt = sb("outt", [P, TC, D], F32, a)
        spill = nc.dram_tensor("x_spill", [P, DC, T], F32).ap()

        sems = {}

        def S(name):
            if name not in sems:
                sems[name] = ctx.enter_context(nc.semaphore(name))
            return sems[name]

        raw_loaded = [S(f"raw_loaded{i}") for i in range(RING)]
        hi_ready = S("hi_ready")
        lo_ready = S("lo_ready")
        block_used = S("block_used")
        acc_free = S("acc_free")
        stage_used = S("stage_used")

        def weight(name):
            w = ins[name]
            if len(w.shape) == 3:
                w = w.rearrange("a k n -> (a k) n")
            return w.rearrange("(c p) n -> p c n", p=P)

        def passes(eng, s):
            if s.loops == 1 or s is stages[-1]:
                for i in range(s.loops):
                    yield i
            else:
                with eng.Fori(0, s.loops) as i:
                    yield i

        def count(s, i, j, extra=0):
            return i * len(s.body) + (first_block[s.name] + j + extra)

        def acc_number(s, i, g, m, extra=0):
            per = len(s.body) // s.kblocks * s.width
            return i * per + (first_acc[s.name] + g * s.width + m + extra)

        def pe_stage(pe, name, act_hi, act_lo, tokens=T, cols_of=None):
            s = by_name[name]
            n_tok = tokens // P
            for i in passes(pe, s):
                for j, (k0, _) in enumerate(s.body):
                    slot = (first_block[name] + j) % RING
                    g, kb = j // s.kblocks, j % s.kblocks
                    pe.wait_ge(lo_ready, count(s, i, j, RING + 1))
                    if s.kind == "T":
                        for m in range(s.width):
                            bank = (first_acc[name] + g * s.width + m) % ACCS
                            if kb == 0:
                                pe.wait_ge(acc_free, acc_number(s, i, g, m, 1))
                            for k in range(s.kc):
                                w = slice(k * s.cols + m * P, k * s.cols + (m + 1) * P)
                                kk = k0 + k
                                o = psum[:, bank, 0:tokens]
                                first, last = kb == 0 and k == 0, kb == s.kblocks - 1 and k == s.kc - 1
                                pe.matmul(o, whi[:, slot, w], act_hi[:, kk, :], start=first, stop=False)
                                pe.matmul(o, whi[:, slot, w], act_lo[:, kk, :], start=False, stop=False)
                                mm = pe.matmul(o, wlo[:, slot, w], act_hi[:, kk, :], start=False, stop=last)
                    else:
                        bank = (first_acc[name] + g) % ACCS
                        pe.wait_ge(acc_free, acc_number(s, i, g, 0, 1))
                        for t in range(n_tok):
                            tok = cols_of(t)
                            o = psum[:, bank, t * P:(t + 1) * P]
                            for k in range(s.kc):
                                w = slice(k * P, (k + 1) * P)
                                pe.matmul(o, act_hi[:, k, tok], whi[:, slot, w], start=k == 0, stop=False)
                                pe.matmul(o, act_hi[:, k, tok], wlo[:, slot, w], start=False, stop=False)
                                mm = pe.matmul(o, act_lo[:, k, tok], whi[:, slot, w], start=False, stop=k == s.kc - 1)
                    mm.then_inc(block_used, 1)

        def act_round(act, b, q, per4):
            slot = q % RING
            act.wait_ge(raw_loaded[slot], per4 * 16 + 16 * (q // RING + 1))
            act.wait_ge(block_used, b + 1)
            act.activation(whi[:, slot, :], raw[:, slot, :], ACT.Copy).then_inc(hi_ready, 1)

        def act_stage(act, name, empty):
            s = by_name[name]
            for i in passes(act, s):
                for j in range(len(s.body)):
                    q = first_block[name] + j + LEAD
                    last = s is stages[-1]
                    if not (last and q + i * len(s.body) >= NB):
                        act_round(act, count(s, i, j, LEAD), q, i * (len(s.body) // RING) if s.loops > 1 else 0) if not (last and s.loops > 1) else \
                            act_round(act, q + i * len(s.body), q + i * len(s.body), 0)
                    if j % s.kblocks == s.kblocks - 1:
                        g = j // s.kblocks
                        act.wait_ge(block_used, count(s, i, j, RING + 1))
                        for m in range(s.width):
                            a = first_acc[name] + g * s.width + m
                            empty(i, g, m, a, a % ACCS).then_inc(acc_free, 1)

        def sem_base(n):
            return 8 * n

        def act_norm(act, mine, n, src, tokens, ready, hilo=None):
            for c in range(DC):
                ready(c)
                act.wait_ge(S("sq_free"), 8 * n + c + 1)
                act.activation(sq[:, c % 2, 0:tokens], src[:, c, :], ACT.Square).then_inc(S("sq_ready"), 1)
            act.wait_ge(S("sq_free"), 8 * n + 8 + 2)
            if n:
                act.wait_ge(S("n_ready"), 8 * n)
            mine.did(act.activation(lnt[:, 0:tokens], psum[:, 4, 0:tokens], ACT.Ln, scale=1.0 / D, bias=eps[:, 0:1]))
            mine.wait()
            act.activation(rbc[:, 0:tokens], lnt[:, 0:tokens], ACT.Exp, scale=-0.5).then_inc(S("r_ready"), 1)
            if hilo is not None:
                for c in range(DC):
                    act.wait_ge(S("n_ready"), 8 * n + c + 1)
                    act.activation(hilo[0][:, c, :], nt[:, c % 2, 0:tokens], ACT.Copy).then_inc(S("nh_ready"), 1)

        def pe_norm(pe, n, tokens):
            if n:
                pe.wait_ge(S("r_ready"), n)
            for c in range(DC):
                pe.wait_ge(S("sq_ready"), 8 * n + c + 1)
                pe.matmul(psum[:, 4, 0:tokens], ones[:, :], sq[:, c % 2, 0:tokens], start=c == 0, stop=c == DC - 1)\
                  .then_inc(S("sq_free"), 1)

        def dve_norm(dve, n, nh, src, gain, tokens, hilo=None):
            g0 = vec_at[gain]
            dve.wait_ge(S("r_ready"), n + 1)

            def low(c):
                dve.wait_ge(S("nh_ready"), 8 * nh + c + 1)
                dve.tensor_tensor(hilo[1][:, c, :], nt[:, c % 2, 0:tokens], hilo[0][:, c, :].bitcast(F32),
                                  ALU.subtract).then_inc(S("normed"), 1)

            for c in range(DC):
                if hilo is not None and c >= 2:
                    dve.wait_ge(S("normed"), 8 * nh + c - 1)
                dst = nt[:, c % 2, 0:tokens] if hilo is not None else src[:, c, :]
                dve.scalar_tensor_tensor(out=dst, in0=src[:, c, :], scalar=vec[:, g0 + c:g0 + c + 1],
                                         in1=rbc[:, 0:tokens], op0=ALU.mult, op1=ALU.mult).then_inc(S("n_ready"), 1)
                if hilo is not None and c >= 1:
                    low(c - 1)
            if hilo is not None:
                low(DC - 1)

        def act_split(act, ready, n0, src, hi, done, chunks):
            for c in range(chunks):
                act.wait_ge(S(ready), n0 + c + 1)
                act.activation(hi[:, c, :], src[:, c, :], ACT.Copy).then_inc(S(done), 1)

        TAPS = 3 * SHORT_K

        def head_semaphore_step(i, j, per, k):
            return i * (2 * per) + (j * per + k)

        V = head_semaphore_step
        chunk_order = [range(TC), range(TC - 1, -1, -1)]

        def pe_heads(pe):
            s = by_name["heads"]
            for i in passes(pe, s):
                for j in range(2):
                    w = lambda name, per, k: pe.wait_ge(S(name), V(i, j, per, k))
                    for b in range(4 * j, 4 * j + 4):
                        slot, bank = (first_block["heads"] + b) % RING, (first_acc["heads"] + b) % ACCS
                        pe.wait_ge(lo_ready, count(s, i, b, RING + 1))
                        pe.wait_ge(acc_free, acc_number(s, i, b, 0, 1))
                        for k in range(DC):
                            wk = slice(k * P, (k + 1) * P)
                            pe.matmul(psum[:, bank, :], whi[:, slot, wk], ah[:, k, :], start=k == 0, stop=False)
                            pe.matmul(psum[:, bank, :], whi[:, slot, wk], al[:, k, :], start=False, stop=False)
                            mm = pe.matmul(psum[:, bank, :], wlo[:, slot, wk], ah[:, k, :], start=False, stop=k == DC - 1)
                        mm.then_inc(block_used, 1)
                    for n in range(2):
                        w("l2_sq", 2, n + 1)
                        pe.matmul(psum[:, 4 + n, :], ones[:], sq[:, n, :], start=True, stop=True).then_inc(S("l2_sum"), 1)
                    w("qk_scaled", 2, 2)
                    for n in range(2):
                        for t in range(TC):
                            mm = pe.transpose(psum[:, 6 + n, t * P:(t + 1) * P], stg[:, 1 + n, t * P:(t + 1) * P], eye[:])
                        mm.then_inc(S("kv_turned"), 1)
                    w("hc_ready", 1, 1)
                    pe.wait_ge(acc_free, acc_number(s, i, 4 * j + 3, 0, ACCS + 1))
                    for d in range(DIRS):
                        for t in range(TC):
                            mm = pe.matmul(psum[:, d, t * P:(t + 1) * P], hc[:, 0, t, d:d + 1].to_broadcast([P, P]),
                                           incl[:, d, :], start=True, stop=True)
                        mm.then_inc(S("g_bc"), 1)
                        for t in range(TC):
                            mm = pe.matmul(psum[:, 2 + d, t * P:(t + 1) * P], hc[:, 1, t, d:d + 1].to_broadcast([P, P]),
                                           eye[:], start=True, stop=True)
                        mm.then_inc(S("b_bc"), 1)
                    for n in range(2):
                        for t in range(TC):
                            tk = slice(t * P, (t + 1) * P)
                            mm = pe.matmul(psum[:, 4 + n, tk], stg[:, 1, tk], stg[:, n, tk], start=True, stop=True)
                        mm.then_inc(S("kq_ready"), 1)
                    for d in range(DIRS):
                        w("mt0_ready", 2, d + 1)
                        w("tok_ready", 2, 2)
                        for t in range(TC):
                            mm = pe.transpose(psum[:, 6 + d, t * P:(t + 1) * P], MT[:, d, t, :], eye[:])
                        mm.then_inc(S("m0_turned"), 1)
                    for l in range(LEVELS):
                        for d in range(DIRS):
                            w("lev_ready", 2 * LEVELS, 2 * l + d + 1)
                            if l == 0:
                                w("m_ready", 2 * LEVELS, d + 1)
                            else:
                                w("m_ready", 2 * LEVELS, 2 * l + d + 1)
                                w("mt_ready", 2 * LEVELS, 2 * l + d - 1)
                            for t in range(TC):
                                mm = pe.matmul(psum[:, 6 + d, t * P:(t + 1) * P], E_[:, d, t, :], Mi[:, d, t, :],
                                               start=True, stop=True)
                            mm.then_inc(S("p_ready"), 1)
                        for d in range(DIRS):
                            w("q_ready", 2 * LEVELS, 2 * l + d + 1)
                            if l == 0:
                                w("kb_ready", 2, d + 1)
                            else:
                                w("m_ready", 2 * LEVELS, 2 * l + d + 1)
                                w("mt_ready", 2 * LEVELS, 2 * l + d - 1)
                            for t in range(TC):
                                if l < LEVELS - 1:
                                    mm = pe.matmul(psum[:, d, t * P:(t + 1) * P], MT[:, d, t, :], EG[:, d, t, :],
                                                   start=True, stop=True)
                            if l < LEVELS - 1:
                                mm.then_inc(S("m_new"), 1)
                            for t in range(TC):
                                mm = pe.matmul(psum[:, 2 + d, t * P:(t + 1) * P], EG[:, d, t, :], MT[:, d, t, :],
                                               start=True, stop=True)
                            mm.then_inc(S("mt_new"), 1)
                    for n in range(TC):
                        for d in range(DIRS):
                            t = chunk_order[d][n]
                            if n:
                                w("s_ready", 2 * TC, 2 * (n - 1) + d + 1)
                                pe.matmul(psum[:, 6 + d, 0:P], KB[:, d, t, :], St[:, d, :], start=True, stop=True)\
                                  .then_inc(S("r_mm"), 1)
                        for d in range(DIRS):
                            t = chunk_order[d][n]
                            if n:
                                w("v_ready", 2 * (TC - 1), 2 * (n - 1) + d + 1)
                                v = vnew[:, d, 0, :]
                            else:
                                w("vb_ready", 2, d + 1)
                                w("mt_ready", 2 * LEVELS, 2 * (LEVELS - 1) + d + 1)
                                v = AT[:, d, t, :]
                            pe.matmul(psum[:, 6 + d, P:2 * P], MT[:, d, t, :], v, start=True, stop=True)\
                              .then_inc(S("vn_mm"), 1)
                        for d in range(DIRS):
                            t = chunk_order[d][n]
                            o = psum[:, 4 + d, t * P:(t + 1) * P]
                            if n:
                                pe.matmul(o, St[:, d, :], QD[:, d, t, :], start=True, stop=False)
                            w("vn_ready", 2 * TC, 2 * n + d + 1)
                            if n == 0:
                                w("qk_masked", 4, 4)
                                w("kt_ready", 2, d + 1)
                            pe.matmul(psum[:, 6 + d, 2 * P:3 * P], E_[:, d, t, :], vnew[:, d, 1, :], start=True, stop=True)\
                              .then_inc(S("s_mm"), 1)
                            mm = pe.matmul(o, vnew[:, d, 1, :], QK[:, d, t, :], start=n == 0, stop=True)
                            if n == TC - 1:
                                mm.then_inc(S("o_ready"), 1)
                            else:
                                mm.then_inc(S("o_part"), 1)
                    w("o_sq", 1, 1)
                    pe.matmul(psum[:, 6, :], ones[:], sq[:, 0, :], start=True, stop=True).then_inc(S("o_sum"), 1)

        def act_heads(act):
            s = by_name["heads"]
            for i in passes(act, s):
                for j in range(2):
                    w = lambda name, per, k: act.wait_ge(S(name), V(i, j, per, k))
                    for b in range(4 * j, 4 * j + 4):
                        act_round(act, count(s, i, b, LEAD), first_block["heads"] + b + LEAD, i * 2)
                        act.wait_ge(block_used, count(s, i, b, RING + 1))
                        bank = (first_acc["heads"] + b) % ACCS
                        n = b % 4
                        if n < 3:
                            act.wait_ge(S("raw_free"), V(i, j, 1, 1))
                            a = act.activation(raw3[:, n, SHORT_PAD:SHORT_PAD + T], psum[:, bank, :], ACT.Copy)
                        else:
                            act.wait_ge(S("z_free"), V(i, j, 1, 1))
                            a = act.activation(stg[:, 3, :], psum[:, bank, :], ACT.Silu)
                        a.then_inc(acc_free, 1)
                    for n in range(3):
                        w("conv3", 3, n + 1)
                        act.activation(stg[:, n, :], stg[:, n, :], ACT.Silu).then_inc(S("qkv_silu"), 1)
                    w("qkv_silu", 3, 2)
                    for n in range(2):
                        act.activation(sq[:, n, :], stg[:, n, :], ACT.Square).then_inc(S("l2_sq"), 1)
                    for n in range(2):
                        w("l2_sum", 2, n + 1)
                        act.activation(nt[:, n, :], psum[:, 4 + n, :], ACT.Ln, bias=eps[:, 0:1]).then_inc(S("l2_ln"), 1)
                    for n in range(2):
                        w("l2_ln", 2, n + 1)
                        act.activation(nt[:, n, :], nt[:, n, :], ACT.Exp, scale=-0.5).then_inc(S("l2_r"), 1)
                    for n in range(2):
                        w("kv_turned", 2, n + 1)
                        act.activation(tok[:, n].rearrange("p t n -> p (t n)"), psum[:, 6 + n, :], ACT.Copy)\
                           .then_inc(S("tok_ready"), 1)
                    for d in range(DIRS):
                        w("e_arg", 2, d + 1)
                        act.activation(E_[:, d], E_[:, d], ACT.Exp).then_inc(S("e_ready"), 1)
                        act.activation(EG[:, d].rearrange("p t n -> p (t n)"), psum[:, d, :], ACT.Exp).then_inc(S("eg_ready"), 1)
                    for d in range(DIRS):
                        w("m0_turned", 2, d + 1)
                        act.activation(Mi[:, d].rearrange("p t n -> p (t n)"), psum[:, 6 + d, :], ACT.Copy)\
                           .then_inc(S("m_ready"), 1)
                    for l in range(LEVELS):
                        for d in range(DIRS):
                            if l < LEVELS - 1:
                                w("m_new", 2 * (LEVELS - 1), 2 * l + d + 1)
                                w("mt_new", 2 * LEVELS, 2 * l + d + 1)
                                act.activation(Mi[:, d].rearrange("p t n -> p (t n)"), psum[:, d, :], ACT.Copy)\
                                   .then_inc(S("m_ready"), 1)
                            w("mt_new", 2 * LEVELS, 2 * l + d + 1)
                            act.activation(MT[:, d].rearrange("p t n -> p (t n)"), psum[:, 2 + d, :], ACT.Copy)\
                               .then_inc(S("mt_ready"), 1)
                    for n in range(TC):
                        for d in range(DIRS):
                            w("vn_mm", 2 * TC, 2 * n + d + 1)
                            if n:
                                w("s_mm", 2 * TC, 2 * (n - 1) + d + 1)
                                w("o_part", 2 * (TC - 1), 2 * (n - 1) + d + 1)
                            act.activation(vnew[:, d, 1, :], psum[:, 6 + d, P:2 * P], ACT.Copy).then_inc(S("vn_ready"), 1)
                    w("o_both", 1, 1)
                    act.activation(sq[:, 0, :], nt[:, 0, :], ACT.Square).then_inc(S("o_sq"), 1)
                    w("o_sum", 1, 1)
                    act.activation(lnt[:], psum[:, 6, :], ACT.Ln, scale=1.0 / P, bias=eps[:, 0:1]).then_inc(S("o_ln"), 1)
                    w("o_ln", 1, 1)
                    act.activation(rbc[:], lnt[:], ACT.Exp, scale=-0.5).then_inc(S("o_r"), 1)
                    w("o_gated", 1, 1)
                    act.activation(zh[:, bass.ds(i * 2 + j, 1), :], nt[:, 1:2, :], ACT.Copy).then_inc(S("o_hi"), 1)

        def dve_heads(dve, mine):
            s = by_name["heads"]
            mine.did(dve.memset(raw3[:, :, 0:SHORT_PAD], 0.0))
            mine.did(dve.memset(raw3[:, :, SHORT_PAD + T:], 0.0))
            mine.wait()
            dve.wait_ge(stage_used, 4 + 48)
            dve.sem_inc(S("raw_free"), 1)
            dve.sem_inc(S("z_free"), 1)
            dve.wait_ge(S("coef_exp"), 2)
            dve.wait_ge(S("beta_ready"), 1)
            g0 = vec_at["delta_norm_g_2"]
            for i in passes(dve, s):
                mine.enter(i, 48)
                for j in range(2):
                    w = lambda name, per, k: dve.wait_ge(S(name), V(i, j, per, k))
                    head = i * 2 + j
                    dve.tensor_copy(hc[:].rearrange("p k t d -> p (k t) d"),
                                    coef[:].rearrange("p k t (d h) -> p (k t) d h", d=DIRS)[:, :, :, bass.ds(head, 1)]
                                    .rearrange("p a d h -> p a (d h)")).then_inc(S("hc_ready"), 1)
                    for n in range(3):
                        dve.wait_ge(acc_free, acc_number(s, i, 4 * j + n, 0, ACCS + 1))
                        for k in range(SHORT_K):
                            tap = short_w[:, bass.ds(head + (k * 24 + n * 8), 1)]
                            src = raw3[:, n, k:k + T]
                            if k == 0:
                                ins_ = dve.tensor_scalar(stg[:, n, :], src, tap, None, ALU.mult)
                            else:
                                mine.wait()
                                ins_ = dve.scalar_tensor_tensor(out=stg[:, n, :], in0=src, scalar=tap, in1=stg[:, n, :],
                                                                op0=ALU.mult, op1=ALU.add)
                            if k < SHORT_K - 1:
                                mine.did(ins_)
                            else:
                                ins_.then_inc(S("conv3"), 1)
                    w("conv3", 3, 3)
                    dve.sem_inc(S("raw_free"), 1)
                    for n in range(2):
                        w("l2_r", 2, n + 1)
                        w("qkv_silu", 3, n + 1)
                        dve.scalar_tensor_tensor(out=stg[:, n, :], in0=stg[:, n, :], scalar=P ** -0.5 if n == 0 else 1.0,
                                                 in1=nt[:, n, :], op0=ALU.mult, op1=ALU.mult).then_inc(S("qk_scaled"), 1)
                    w("qkv_silu", 3, 3)
                    w("hc_ready", 1, 1)
                    for d in range(DIRS):
                        w("g_bc", 2, d + 1)
                        for t in range(TC):
                            ins_ = dve.tensor_scalar(E_[:, d, t, :], psum[:, d, t * P:(t + 1) * P], hc[:, 2, t, d:d + 1], 0.0,
                                                     ALU.add, ALU.min)
                        ins_.then_inc(S("e_arg"), 1)
                    w("qk_scaled", 2, 2)
                    for d in range(DIRS):
                        f = lambda ap: ap.rearrange("p t n -> p (t n)")
                        ps = lambda b: psum[:, b, :].rearrange("p (t n) -> p t n", t=TC)
                        w("e_ready", 2, d + 1)
                        mine.did(dve.tensor_tensor(E_[:, d], E_[:, d], incl[:, d:d + 1, :].to_broadcast([P, TC, P]), ALU.mult))
                        w("kq_ready", 2, 2)
                        mine.wait()
                        dve.tensor_tensor(QK[:, d], E_[:, d], ps(4), ALU.mult).then_inc(S("qk_masked"), 1)
                        dve.tensor_tensor(AT[:, d], E_[:, d], ps(5), ALU.mult).then_inc(S("qk_masked"), 1)
                        w("qk_masked", 4, 2 * d + 2)
                        w("b_bc", 2, d + 1)
                        mine.did(dve.tensor_tensor(AT[:, d], AT[:, d], ps(2 + d), ALU.mult))
                        mine.wait()
                        mine.did(dve.tensor_tensor(E_[:, d], AT[:, d], level[:, d, 0:1, :].to_broadcast([P, TC, P]), ALU.mult))
                        mine.wait()
                        dve.tensor_tensor(MT[:, d], eye[:].rearrange("p (a n) -> p a n", a=1).to_broadcast([P, TC, P]),
                                          E_[:, d], ALU.subtract).then_inc(S("mt0_ready"), 1)
                        w("mt0_ready", 2, d + 1)
                        dve.tensor_tensor(E_[:, d], AT[:, d], level[:, d, 1:2, :].to_broadcast([P, TC, P]), ALU.mult)\
                           .then_inc(S("lev_ready"), 1)
                        w("eg_ready", 2, d + 1)
                        q_ = stg[:, 0, :].rearrange("p (t n) -> p t n", t=TC)
                        k_ = stg[:, 1, :].rearrange("p (t n) -> p t n", t=TC)
                        mine.did(dve.tensor_tensor(QD[:, d], q_, EG[:, d], ALU.mult))
                        mine.did(dve.tensor_tensor(KB[:, d], k_, EG[:, d], ALU.mult))
                        mine.wait()
                        dve.tensor_tensor(KB[:, d], KB[:, d], ps(2 + d), ALU.mult).then_inc(S("kb_ready"), 1)
                    w("kb_ready", 2, 2)
                    mine.wait()
                    for l in range(LEVELS):
                        for d in range(DIRS):
                            w("p_ready", 2 * LEVELS, 2 * l + d + 1)
                            dve.tensor_tensor(EG[:, d], eye[:].rearrange("p (a n) -> p a n", a=1).to_broadcast([P, TC, P]),
                                              ps(6 + d), ALU.subtract).then_inc(S("q_ready"), 1)
                            if l < LEVELS - 1:
                                dve.tensor_tensor(E_[:, d], AT[:, d], level[:, d, l + 2:l + 3, :].to_broadcast([P, TC, P]),
                                                  ALU.mult).then_inc(S("lev_ready"), 1)
                            else:
                                w("lev_ready", 2 * LEVELS, 2 * LEVELS)
                                for t in range(TC):
                                    ins_ = dve.tensor_scalar(E_[:, d, t, :], tok[:, 0, t, :], hc[:, 3, t, d:d + 1], None, ALU.mult)
                                ins_.then_inc(S("kt_ready"), 1)
                                for t in range(TC):
                                    ins_ = dve.tensor_scalar(AT[:, d, t, :], tok[:, 1, t, :], hc[:, 1, t, d:d + 1], None, ALU.mult)
                                ins_.then_inc(S("vb_ready"), 1)
                    w("vb_ready", 2, 2)
                    for n in range(TC):
                        if n:
                            for d in range(DIRS):
                                t = chunk_order[d][n]
                                w("r_mm", 2 * (TC - 1), 2 * (n - 1) + d + 1)
                                dve.tensor_tensor(vnew[:, d, 0, :], AT[:, d, t, :], psum[:, 6 + d, 0:P], ALU.subtract)\
                                   .then_inc(S("v_ready"), 1)
                        for d in range(DIRS):
                            t = chunk_order[d][n]
                            w("s_mm", 2 * TC, 2 * n + d + 1)
                            if n == 0:
                                ins_ = dve.tensor_copy(St[:, d, :], psum[:, 6 + d, 2 * P:3 * P])
                            else:
                                w("s_ready", 2 * TC, 2 * (n - 1) + d + 1)
                                ins_ = dve.scalar_tensor_tensor(out=St[:, d, :], in0=St[:, d, :], scalar=hc[:, 4, t, d:d + 1],
                                                                in1=psum[:, 6 + d, 2 * P:3 * P], op0=ALU.mult, op1=ALU.add)
                            ins_.then_inc(S("s_ready"), 1)
                    w("o_ready", 2, 2)
                    mine.did(dve.tensor_copy(nt[:, 0, :], psum[:, 4, :]))
                    mine.wait()
                    dve.tensor_tensor(nt[:, 0, :], nt[:, 0, :], psum[:, 5, :], ALU.add).then_inc(S("o_both"), 1)
                    w("o_r", 1, 1)
                    w("o_both", 1, 1)
                    mine.did(dve.scalar_tensor_tensor(out=nt[:, 1, :], in0=nt[:, 0, :], scalar=vec[:, g0:g0 + 1], in1=rbc[:],
                                             op0=ALU.mult, op1=ALU.mult))
                    mine.wait()
                    dve.wait_ge(acc_free, acc_number(s, i, 4 * j + 3, 0, ACCS + 1))
                    dve.tensor_tensor(nt[:, 1, :], nt[:, 1, :], stg[:, 3, :], ALU.mult).then_inc(S("o_gated"), 1)
                    w("o_gated", 1, 1)
                    dve.sem_inc(S("z_free"), 1)
                    w("o_hi", 1, 1)
                    dve.tensor_tensor(zl[:, bass.ds(head, 1), :], nt[:, 1:2, :], zh[:, bass.ds(head, 1), :].bitcast(F32),
                                      ALU.subtract).then_inc(S("o_split"), 1)
                    w("o_split", 1, 1)
                mine.leave(s.loops)

        slopes = alibi_slopes()
        w3 = lambda name: ins[name].rearrange("a h d -> (a h) d") if len(ins[name].shape) == 3 else ins[name]
        block = ctx.enter_context(nc.Block())

        @block.sync
        def _(sp):
            sp.dma_start(eye[:], ins["eye"]).then_inc(S("eye_in"), 16)
            sp.dma_start(xin[:], ins["x"].rearrange("a (c p) d -> p (a c) d", p=P)).then_inc(S("x_in"), 16)
            for name, rows in VECTORS:
                v = ins[name]
                v = v.rearrange("a n -> (a n)") if len(v.shape) == 2 else v
                sp.dma_start(vrows[vec_at[name]:vec_at[name] + rows, :], v.rearrange("(c p) -> c p", p=P))\
                  .then_inc(S("vrows_in"), 16)
            for s in stages:
                w = weight(s.w)
                if s.name == "v":
                    sp.wait_ge(S("x_turned"), 8)
                    sp.wait_ge(S("vec_ready"), 1)
                    sp.dma_start(dist2[:], ins["dist2"]).then_inc(S("attn_in"), 16)
                    sp.dma_start(upper[:], ins["upper"]).then_inc(S("attn_in"), 16)
                    sp.dma_start(wsp[:], ins["w_sgu_spatial"].rearrange("a g t s -> t (a g) s")).then_inc(S("attn_in"), 16)
                    sp.dma_start(brow[:], ins["b_sgu_spatial"].rearrange("a g t -> a (g t)").to_broadcast([P, 4 * P])
                                 .rearrange("p (g t) -> p g t", g=4)).then_inc(S("attn_in"), 16)
                    sp.wait_ge(S("r_ready"), 1)
                    sp.dma_start(grow[:], ins["g_sgu"].to_broadcast([P, 512])).then_inc(S("attn_in"), 16)
                for i in passes(sp, s):
                    for j, (k0, col) in enumerate(s.body):
                        q = first_block[s.name] + j
                        slot = q % RING
                        cols = bass.ds(i * s.cstep + col, s.cols) if s.loops > 1 else slice(col, col + s.cols)
                        sp.wait_ge(lo_ready, count(s, i, j, 1))
                        sp.dma_start(raw[:, slot, :].rearrange("p (c n) -> p c n", c=s.kc),
                                     w[:, k0:k0 + s.kc, cols]).then_inc(raw_loaded[slot], 16)
            if not dump:
                for t in range(TC):
                    sp.wait_ge(S("out_ready"), 4 * (t + 1))
                    sp.dma_start(out.rearrange("a (c p) d -> p (a c) d", p=P)[:, t, :], outt[:, t, :]).then_inc(S("out_done"), 16)
                sp.wait_ge(S("out_done"), 16 * TC)
            if dump:
                sp.wait_ge(S(dump[1]), dump[2])
                sp.dma_start(out, dump[0](dict(X=X, ah=ah, qk=qk, vt=vt))).then_inc(S("out_done"), 16)
                sp.wait_ge(S("out_done"), 16)

        @block.gpsimd
        def _(pool):
            pool.sem_inc(lo_ready, RING)
            whole, rest = divmod(NB, RING)

            def low(b, slot, i):
                pool.wait_ge(hi_ready, b + 1)
                pool.tensor_tensor(wlo[:, slot, :], raw[:, slot, :], whi[:, slot, :].bitcast(F32),
                                   ALU.subtract).then_inc(lo_ready, 1)

            with pool.Fori(0, whole) as i:
                for j in range(RING):
                    low(i * RING + j, j, i)
            for j in range(rest):
                low(whole * RING + j, j, whole)

        @block.tensor
        def _(pe):
            pe.sem_inc(block_used, RING)
            pe.sem_inc(S("sq_free"), 2)
            pe.wait_ge(S("eye_in"), 16)
            pe.wait_ge(S("vrows_in"), 16 * len(VECTORS))
            pe.transpose(psum[:, 5, 0:NVEC], vrows[0:NVEC, :], eye[0:NVEC, 0:NVEC]).then_inc(S("vec_turned"), 1)
            pe.wait_ge(S("x_in"), 16)
            for c in range(DC):
                if c >= 2:
                    pe.wait_ge(S("x_turned"), c - 1)
                for t in range(TC):
                    mm = pe.transpose(psum[:, 6 + c % 2, t * P:(t + 1) * P], xin[:, t, c * P:(c + 1) * P], eye[:])
                mm.then_inc(S("x_tp"), 1)
            pe.wait_ge(S("ones_ready"), 1)
            pe_norm(pe, 0, T)
            pe.wait_ge(S("normed"), 8)
            pe_stage(pe, "qk", ah, al)
            pe_stage(pe, "v", ah, al, cols_of=lambda r: slice(r, T, 4))
            pe_stage(pe, "u", ah, al)
            pe_stage(pe, "vv", ah, al, cols_of=lambda t: slice(t * P, (t + 1) * P))

            pe.wait_ge(S("attn_in"), 16 * 5)
            for g in range(4):
                mm = pe.transpose(psum[:, 4, g * P:(g + 1) * P], wsp[:, g, :], eye[:])
            mm.then_inc(S("wsp_turned"), 1)
            pe.wait_ge(S("wspT_ready"), 1)
            pe.wait_ge(S("vv_normed"), TC)
            for g in range(4):
                if g >= 2:
                    pe.wait_ge(S("sgu_done"), g - 1)
                for n in range(TC):
                    mm = pe.matmul(psum[:, 6 + g % 2, n * P:(n + 1) * P], vv[:, n, g * P:(g + 1) * P], wspT[:, g, :],
                                   start=True, stop=True)
                mm.then_inc(S("mixed"), 1)

            pe.wait_ge(S("sgu_done"), 4)
            pe.wait_ge(acc_free, first_acc["branch_attn"] + ACCS)

            def scores(u):
                h, r = divmod(u, 4)
                if u >= 2:
                    pe.wait_ge(S("scored"), u - 1)
                bank = 4 + 2 * (u % 2)
                at = slice(64 * (h % 2), 64 * (h % 2) + 64)
                for gi in range(3):
                    q, k = qk[at, 2 * gi + h // 2, r::4], qk[at, 6 + 2 * gi + h // 2, :]
                    o = psum[:, bank, :] if gi == 0 else psum[:, bank + 1, (gi - 1) * P:gi * P]
                    mm = pe.matmul(o, q, k if gi == 0 else k[:, r::4], start=True, stop=True)
                mm.then_inc(S("scores"), 1)

            def values(u):
                h, r = divmod(u, 4)
                pe.wait_ge(S("probs"), u + 1)
                s_ = sc[:, u % 2, :]
                if u >= 1:
                    pe.wait_ge(S("pT_ready_a"), u)
                    pe.wait_ge(S("pT_ready_b"), u)
                for c in range(4):
                    pe.transpose(psum[:, 0, c * P:(c + 1) * P], s_[:, c:T:4], eye[:])
                for c in range(2):
                    mm = pe.transpose(psum[:, 1, c * P:(c + 1) * P], s_[:, T + c * P:T + (c + 1) * P], eye[:])
                mm.then_inc(S("p_turned"), 1)
                pe.wait_ge(S("pT_ready_a"), u + 1)
                pe.wait_ge(S("pT_ready_b"), u + 1)
                if u >= 2:
                    pe.wait_ge(S("y_ready"), u - 1)
                for c in range(6):
                    gi, tile = (0, c) if c < 4 else (c - 3, r)
                    v0 = (gi * 4 + h) * HD
                    mm = pe.matmul(psum[:, 2 + u % 2, 0:HD], pT[:, c * P:(c + 1) * P], vt[:, tile, v0:v0 + HD],
                                   start=c == 0, stop=c == 5)
                mm.then_inc(S("attended"), 1)

            for u in range(16):
                scores(u)
                if u:
                    values(u - 1)
            values(15)
            pe.wait_ge(S("y_ready"), 16)
            for c in range(2):
                for r in range(4):
                    mm = pe.transpose(psum[:, 4 + c, r * P:(r + 1) * P], ya[:, r, c * P:(c + 1) * P], eye[:])
            mm.then_inc(S("y_turned"), 1)
            pe.wait_ge(S("yT_ready"), 2)
            pe_stage(pe, "branch_attn", yh, yl)
            pe_stage(pe, "gate_attn", ah, al)
            pe_stage(pe, "branch_sgu", yh[:, 2:6, :], yl[:, 2:6, :])
            pe_stage(pe, "gate_sgu", ah, al)
            pe.wait_ge(S("merge_split"), 8)
            pe_stage(pe, "out", ah, al)

            pe.wait_ge(S("mem_in"), 16)
            for c in range(DC):
                if c >= 2:
                    pe.wait_ge(S("mem_turned"), c - 1)
                for t in range(2):
                    mm = pe.transpose(psum[:, 6 + c % 2, t * P:(t + 1) * P], memin[:, t, c * P:(c + 1) * P], eye[:])
                mm.then_inc(S("mem_tp"), 1)
            pe_norm(pe, 1, NM)
            pe.wait_ge(S("normed"), 16)
            pe_stage(pe, "mem_k", mh, ml, NM)
            pe_stage(pe, "mem_v", mh, ml, NM, cols_of=lambda t: slice(t * P, (t + 1) * P))
            pe_norm(pe, 2, T)
            pe.wait_ge(S("normed"), 24)
            pe_stage(pe, "cross_q", ah, al)
            pe.wait_ge(acc_free, first_acc["cross_o"] + ACCS)

            def cscores(u):
                h, t = divmod(u, 4)
                if u >= 2:
                    pe.wait_ge(S("cprobs"), u - 1)
                pe.matmul(psum[:, 4 + u % 2, 0:NM], cq[:, h, t * P:(t + 1) * P], ckT[:, h, :], start=True, stop=True)\
                  .then_inc(S("cscores"), 1)

            def cturn(u):
                h, t = divmod(u, 4)
                pe.wait_ge(S("cnormed"), u + 1)
                if t == 0 and h >= 1:
                    pe.wait_ge(S("cpT_ready"), 2 * h)
                for c in range(2):
                    mm = pe.transpose(psum[:, 6 + c, t * P:(t + 1) * P], cs[:, u % 4, c * P:(c + 1) * P], eye[:])
                mm.then_inc(S("cturned"), 1)

            def cout(h):
                pe.wait_ge(S("cpT_ready"), 2 * h + 2)
                for c in range(2):
                    mm = pe.matmul(psum[:, h, :], cv[:, c, h * P:(h + 1) * P], cpT[:, c, :], start=c == 0, stop=c == 1)
                mm.then_inc(S("cattended"), 1)

            for u in range(17):
                if u < 16:
                    cscores(u)
                if u:
                    cturn(u - 1)
                    if u % 4 == 0:
                        cout(u // 4 - 1)
            pe.wait_ge(S("co_split"), 4)
            pe_stage(pe, "cross_o", yh, yl)
            pe_norm(pe, 3, T)
            pe.wait_ge(S("normed"), 32)
            pe_stage(pe, "gate_up", ah, al)
            pe.wait_ge(S("hid_split"), FC)
            pe_stage(pe, "down", hh, hl)
            if upto == 1:
                return
            pe_norm(pe, 4, T)
            pe.wait_ge(S("crows_in"), 48)
            for k, rows in enumerate((P, CONV_K * 8 - P, SHORT_K * 24)):
                mm = pe.transpose(psum[:, 5, k * P:k * P + rows], crows[0:rows, k, :], eye[0:rows, 0:rows])
            mm.then_inc(S("crows_turned"), 1)
            pe_norm(pe, 5, T)
            pe.wait_ge(S("normed"), 40)
            pe_stage(pe, "glu", ah, al)
            pe_stage(pe, "gate_a", ah, al)
            pe.wait_ge(S("ab_split"), 1)
            for t in range(TC):
                o = psum[:, 5, t * 32:(t + 1) * 32]
                for k in range(DC):
                    tk = slice(t * P, (t + 1) * P)
                    pe.matmul(o, ah[:, k, tk], abh[:, k, :], start=k == 0, stop=False)
                    pe.matmul(o, ah[:, k, tk], abl[:, k, :], start=False, stop=False)
                    mm = pe.matmul(o, al[:, k, tk], abh[:, k, :], start=False, stop=k == DC - 1)
            mm.then_inc(S("ab_ready"), 1)
            pe.wait_ge(S("g_ready"), 1)
            for d in range(DIRS):
                pe.matmul(psum[:, 6, d * 64:(d + 1) * 64], incl[:, d, :], coef[:, 0, :, :].rearrange("p t u -> p (t u)"),
                          start=True, stop=True)
            pe.matmul(psum[:, 6, 128:192], ones[:], coef[:, 0, :, :].rearrange("p t u -> p (t u)"), start=True, stop=True)\
              .then_inc(S("cum_ready"), 1)
            for c in range(DC):
                pe.wait_ge(S("conv_done"), c + 1)
                mm = pe.matmul(psum[:, 4, :], ones[:], X[:, c, :], start=c == 0, stop=c == DC - 1)
            mm.then_inc(S("conv_sum"), 1)
            for c in range(DC):
                pe.wait_ge(S("csq_ready"), c + 1)
                pe.matmul(psum[:, 5, :], ones[:], sq[:, c % 2, :], start=c == 0, stop=c == DC - 1).then_inc(S("csq_used"), 1)
            pe.wait_ge(S("c_split"), DC)
            pe_stage(pe, "conv_out", zh, zl)
            pe_heads(pe)
            pe.wait_ge(S("o_split"), HEADS)
            pe_stage(pe, "delta_out", zh, zl)
            pe_stage(pe, "gate_b", ah, al)
            pe.wait_ge(S("y_split"), DC)
            pe_stage(pe, "o2", zh, zl)
            pe_norm(pe, 6, T)
            pe.wait_ge(S("normed"), 48)
            pe_stage(pe, "gate_up2", ah, al)
            pe.wait_ge(S("hid_split"), 2 * FC)
            pe_stage(pe, "down2", hh, hl)
            pe.wait_ge(S("p_in"), 16)
            for c in range(2):
                for t in range(TC):
                    mm = pe.transpose(psum[:, 6 + c, t * P:(t + 1) * P], pin[:, t, c * P:(c + 1) * P], eye[:])
                mm.then_inc(S("pp_turned"), 1)
            pe.wait_ge(S("pp_split"), 2)
            pe_stage(pe, "pl_proj", ph, pl)
            pe_norm(pe, 7, T)
            pe_norm(pe, 8, T)
            pe.wait_ge(S("normed"), 56)
            pe_stage(pe, "pl_gate", ah, al)
            pe_norm(pe, 9, T)
            for t in range(TC):
                for half in range(2):
                    n = 2 * t + half
                    if t == 0 and half == 0:
                        pe.wait_ge(S("n_ready"), 80)
                    if n >= 2:
                        pe.wait_ge(S("out_ready"), 2 * (n - 1))
                    for c in range(4):
                        mm = pe.transpose(psum[:, 6 + n % 2, c * P:(c + 1) * P], X[:, 4 * half + c, t * P:(t + 1) * P], eye[:])
                    mm.then_inc(S("o_turned"), 1)

        @block.scalar
        def _(act):
            mine = Steps(act, S("act_own"))
            act.sem_inc(acc_free, ACCS)
            for b in range(LEAD):
                act_round(act, b, b, 0)
            act_norm(act, mine, 0, X, T, lambda c: act.wait_ge(S("x_turned"), c + 1), (ah, al))
            act_stage(act, "qk", lambda i, g, m, a, bank: act.activation(
                qk[:, bass.ds(i * 4 + g, 1), :], psum[:, bank:bank + 1, :], ACT.Copy))
            act_stage(act, "v", lambda i, g, m, a, bank: act.activation(
                vt[:, :, g * P:(g + 1) * P], psum[:, bank, :].rearrange("p (r n) -> p r n", r=4), ACT.Copy))
            act_stage(act, "u", lambda i, g, m, a, bank: act.activation(
                uu[:, g, :], psum[:, bank, :], ACT.Gelu_apprx_tanh))
            act_stage(act, "vv", lambda i, g, m, a, bank: act.activation(
                vv[:, :, g * P:(g + 1) * P], psum[:, bank, :].rearrange("p (t n) -> p t n", t=4), ACT.Gelu_apprx_tanh))
            act.wait_ge(acc_free, first_acc["branch_attn"] + ACCS)
            for t in range(TC):
                if t:
                    act.wait_ge(S("ss_ready"), t)
                act.activation(sq[:, 0, :], vv[:, t, :], ACT.Square, accum_out=ss[:, t:t + 1]).then_inc(S("ss_ready"), 1)
            act.wait_ge(S("ss_ready"), TC)
            mine.did(act.activation(ss[:, 8:12], ss[:, 0:4], ACT.Ln, scale=1.0 / 512, bias=eps[:, 0:1]))
            mine.wait()
            act.activation(rs[:, 0:4], ss[:, 8:12], ACT.Exp, scale=-0.5).then_inc(S("rs_ready"), 1)
            for g in range(4):
                act.wait_ge(S("sgu_done"), g + 1)
                act.activation(yh[:, 2 + g, :], nt[:, g % 2, :], ACT.Copy).then_inc(S("sgu_hi"), 1)
            act.wait_ge(S("mixed"), 4)
            act.dma_start(dist[:], ins["dist"]).then_inc(S("dist_in"), 16)

            def soft(u):
                act.wait_ge(S("scored"), u + 1)
                act.activation(sc[:, u % 2, :], sc[:, u % 2, :], ACT.Exp, scale=HD ** -0.5, bias=nmx[:, u:u + 1],
                               accum_out=den[:, u:u + 1]).then_inc(S("probs"), 1)

            def pT_a(u):
                act.wait_ge(S("p_turned"), u + 1)
                if u:
                    act.wait_ge(S("attended"), u)
                act.activation(pT[:, 0:T], psum[:, 0, :], ACT.Copy).then_inc(S("pT_ready_a"), 1)

            soft(0)
            for u in range(16):
                if u < 15:
                    soft(u + 1)
                pT_a(u)
            act.wait_ge(S("y_turned"), 1)
            for c in range(2):
                act.activation(yh[:, c, :].rearrange("p (j r) -> p r j", r=4),
                               psum[:, 4 + c, :].rearrange("p (r j) -> p r j", r=4), ACT.Copy).then_inc(S("y_hi"), 1)

            act.wait_ge(S("y_ready"), 16)
            act.wait_ge(S("yT_ready"), 2)
            act_stage(act, "branch_attn", lambda i, g, m, a, bank: act.activation(
                m1[:, 4 * g + m, :], psum[:, bank, :], ACT.Copy))

            def stage_out(name, staged0, func, bias_of=None):
                s = by_name[name]
                a0 = first_acc[name]

                def empty(i, g, m, a, bank):
                    per = len(s.body) // s.kblocks * s.width
                    act.wait_ge(stage_used, i * per + (staged0 + a - a0 + 1))
                    kw = {} if bias_of is None else {"bias": bias_of(i, a - a0)}
                    return act.activation(stg[:, (staged0 + a - a0) % 4, :], psum[:, bank, :], func, **kw)

                act_stage(act, name, empty)

            bg = vec_at["b_gate"]
            stage_out("gate_attn", 0, ACT.Sigmoid, lambda i, k: vec[:, bass.ds(i * 4 + (bg + k), 1)])
            act_stage(act, "branch_sgu", lambda i, g, m, a, bank: act.activation(
                m2[:, 2 * g + m, :], psum[:, bank, :], ACT.Copy))
            stage_out("gate_sgu", 8, ACT.Sigmoid, lambda i, k: vec[:, bass.ds(i * 4 + (bg + 8 + k), 1)])
            act_split(act, "merged", 8, m1, ah, "merge_hi", 8)
            act.wait_ge(S("merge_split"), 8)
            act.dma_start(memin[:], ins["mem"].rearrange("a (c p) d -> p (a c) d", p=P)).then_inc(S("mem_in"), 16)
            stage_out("out", 16, ACT.Copy)
            act_norm(act, mine, 1, memT, NM, lambda c: act.wait_ge(S("mem_turned"), c + 1), (mh, ml))
            act_stage(act, "mem_k", lambda i, g, m, a, bank: act.activation(
                ckT[:, g, :], psum[:, bank, 0:NM], ACT.Copy))
            act_stage(act, "mem_v", lambda i, g, m, a, bank: act.activation(
                cv[:, :, g * P:(g + 1) * P], psum[:, bank, 0:NM].rearrange("p (t n) -> p t n", t=2), ACT.Copy))
            act_norm(act, mine, 2, X, T, lambda c: act.wait_ge(stage_used, 4 + 16 + c + 1), (ah, al))
            act_stage(act, "cross_q", lambda i, g, m, a, bank: act.activation(
                cq[:, g, :], psum[:, bank, :], ACT.Copy))

            def csoft(u):
                act.wait_ge(S("cmaxed"), u + 1)
                if u >= 4:
                    act.wait_ge(S("cturned"), u - 3)
                act.activation(cs[:, u % 4, :], psum[:, 4 + u % 2, 0:NM], ACT.Exp, scale=P ** -0.5,
                               bias=cmx[:, u:u + 1], accum_out=cden[:, u:u + 1]).then_inc(S("cprobs"), 1)

            def cpT_copy(h):
                act.wait_ge(S("cturned"), 4 * h + 4)
                if h:
                    act.wait_ge(S("cattended"), h)
                for c in range(2):
                    act.activation(cpT[:, c, :], psum[:, 6 + c, :], ACT.Copy).then_inc(S("cpT_ready"), 1)

            def co_hi(h):
                act.wait_ge(S("cattended"), h + 1)
                act.activation(yh[:, h, :], psum[:, h, :], ACT.Copy).then_inc(S("co_hi"), 1)

            for u in range(16):
                csoft(u)
                if u % 4 == 0 and u > 0:
                    cpT_copy(u // 4 - 1)
                if u % 4 == 2 and u > 4:
                    co_hi(u // 4 - 1)
            cpT_copy(3)
            co_hi(3)
            stage_out("cross_o", 24, ACT.Copy)
            act_norm(act, mine, 3, X, T, lambda c: act.wait_ge(stage_used, 4 + 24 + c + 1), (ah, al))

            def swiglu(name, staged, hid0):
                s = by_name[name]
                a0 = first_acc[name]
                act.wait_ge(stage_used, 4 + staged)

                def empty(i, g, m, a, bank):
                    act.wait_ge(S("hid"), i * 2 + (hid0 + g // 2 + 1))
                    return act.activation(stg[:, g, :], psum[:, bank, :], ACT.Silu if g % 2 == 0 else ACT.Copy)

                for i in passes(act, s):
                    for j in range(4):
                        q = first_block[name] + j + LEAD
                        act_round(act, count(s, i, j, LEAD), q, i)
                        act.wait_ge(block_used, count(s, i, j, RING + 1))
                        empty(i, j, 0, a0 + j, (a0 + j) % ACCS).then_inc(acc_free, 1)
                        if j % 2 == 1:
                            act.wait_ge(S("hid"), i * 2 + (hid0 + j // 2 + 3))
                            act.activation(hh[:, bass.ds(i * 2 + j // 2, 1), :], nt[:, j // 2:j // 2 + 1, :], ACT.Copy)\
                               .then_inc(S("hid_hi"), 1)

            swiglu("gate_up", 32, 0)
            stage_out("down", 32, ACT.Copy)
            if upto == 1:
                return
            act_norm(act, mine, 4, X, T, lambda c: act.wait_ge(stage_used, 4 + 32 + c + 1))
            act.dma_start(level[:], ins["level"]).then_inc(S("masks_in"), 16)
            act.dma_start(incl[:], ins["incl"]).then_inc(S("masks_in"), 16)
            cw = ins["conv_dw_w_2"].rearrange("a k (c p) -> (a k c) p", p=P)
            act.dma_start(crows[:, 0, :], cw[0:P, :]).then_inc(S("crows_in"), 16)
            act.dma_start(crows[0:CONV_K * 8 - P, 1, :], cw[P:CONV_K * 8, :]).then_inc(S("crows_in"), 16)
            act.dma_start(crows[0:SHORT_K * 24, 2, :], ins["qkv_conv_w_2"].rearrange("a k (c p) -> (a k c) p", p=P))\
               .then_inc(S("crows_in"), 16)
            act.dma_start(abw[:], ins["w_in_2"].rearrange("a (c p) n -> p (a c) n", p=P)[:, :, 6 * D:6 * D + 32])\
               .then_inc(S("ab_in"), 16)
            act.dma_start(arow[:, 0, :], ins["a_log_2"].rearrange("a d h -> a (d h)").to_broadcast([P, 16])).then_inc(S("arow_in"), 16)
            act.dma_start(arow[:, 1, :], ins["dt_bias_2"].rearrange("a d h -> a (d h)").to_broadcast([P, 16])).then_inc(S("arow_in"), 16)
            act.wait_ge(S("n_ready"), 40)
            act.dma_start(spill, X[:]).then_inc(S("spilled"), 16)
            act_norm(act, mine, 5, X, T, lambda c: None, (ah, al))
            act.wait_ge(S("ab_in"), 16)
            act.activation(abh[:], abw[:], ACT.Copy).then_inc(S("ab_hi"), 1)

            def glu_empty(i, g, m, a, bank):
                act.wait_ge(S("glu_done"), i * 2 + (g // 2 + 1))
                return act.activation(stg[:, g % 4, :], psum[:, bank, :], ACT.Sigmoid if g % 2 else ACT.Copy)

            act.wait_ge(stage_used, 4 + 40)
            act_stage(act, "glu", glu_empty)
            act_stage(act, "gate_a", lambda i, g, m, a, bank: act.activation(
                yg[:, bass.ds(i * 4 + g, 1), :], psum[:, bank:bank + 1, :], ACT.Sigmoid))
            act.wait_ge(S("arow_in"), 32)
            act.activation(arow[:, 0, :], arow[:, 0, :], ACT.Exp).then_inc(S("alog_exp"), 1)
            act.wait_ge(S("ab_sum"), 1)
            act.activation(tmp[:, 1], tmp[:, 0], ACT.Abs).then_inc(S("ab_abs"), 1)
            act.wait_ge(S("ab_abs"), 1)
            act.activation(tmp[:, 2], tmp[:, 1], ACT.Exp, scale=-1.0).then_inc(S("ab_abs"), 1)
            act.wait_ge(S("ab_abs"), 2)
            act.activation(tmp[:, 1], tmp[:, 2], ACT.Ln, bias=1.0).then_inc(S("ab_abs"), 1)
            act.activation(coef[:, 1], ab[:, :, 16:32], ACT.Sigmoid).then_inc(S("beta_ready"), 1)
            act.wait_ge(S("tail_arg"), 1)
            act.activation(coef[:, 3], coef[:, 3], ACT.Exp).then_inc(S("coef_exp"), 1)
            act.activation(coef[:, 4], coef[:, 4], ACT.Exp).then_inc(S("coef_exp"), 1)
            for c in range(DC):
                act.wait_ge(S("centred"), c + 1)
                if c >= 2:
                    act.wait_ge(S("csq_used"), c - 1)
                act.activation(sq[:, c % 2, :], X[:, c, :], ACT.Square).then_inc(S("csq_ready"), 1)
            act.wait_ge(S("csq_used"), DC)
            act.wait_ge(S("n_ready"), 48)
            mine.did(act.activation(lnt[:], psum[:, 5, :], ACT.Ln, scale=1.0 / D, bias=eps[:, 1:2]))
            mine.wait()
            act.activation(rbc[:], lnt[:], ACT.Exp, scale=-0.5).then_inc(S("c_r"), 1)
            lb = vec_at["conv_ln_b_2"]
            for c in range(DC):
                act.wait_ge(S("c_scaled"), c + 1)
                mine.did(act.activation(X[:, c, :], X[:, c, :], ACT.Silu, bias=vec[:, lb + c:lb + c + 1]))
                mine.wait()
                act.activation(zh[:, c, :], X[:, c, :], ACT.Copy).then_inc(S("c_hi"), 1)
            stage_out("conv_out", 40, ACT.Copy)
            act_heads(act)
            act_stage(act, "delta_out", lambda i, g, m, a, bank: act.activation(
                d2[:, bass.ds(i * 4 + g, 1), :], psum[:, bank:bank + 1, :], ACT.Copy))
            act.dma_start(X[:], spill).then_inc(S("x_back"), 16)
            stage_out("gate_b", 48, ACT.Sigmoid)
            act_split(act, "y_sum", 0, yg, zh, "y_hi2", DC)
            stage_out("o2", 56, ACT.Copy)
            act_norm(act, mine, 6, X, T, lambda c: act.wait_ge(stage_used, 4 + 56 + c + 1), (ah, al))
            swiglu("gate_up2", 64, FC)
            stage_out("down2", 64, ACT.Copy)
            act.wait_ge(block_used, RING + first_block["pl_proj"])
            act.dma_start(pin[:], ins["p_2"].rearrange("a b (c p) d -> p (a b c) d", p=P)).then_inc(S("p_in"), 16)
            for c in range(2):
                act.wait_ge(S("pp_turned"), c + 1)
                act.activation(ph[:, c, :], psum[:, 6 + c, :], ACT.Copy).then_inc(S("pp_hi"), 1)
            act_stage(act, "pl_proj", lambda i, g, m, a, bank: act.activation(
                PL[:, 4 * g + m, :], psum[:, bank, :], ACT.Copy))
            act_norm(act, mine, 7, PL, T, lambda c: act.wait_ge(acc_free, ACCS + first_acc["pl_proj"] + 8))
            act_norm(act, mine, 8, X, T, lambda c: act.wait_ge(stage_used, 4 + 72), (ah, al))
            stage_out("pl_gate", 72, ACT.Sigmoid)
            act_norm(act, mine, 9, X, T, lambda c: act.wait_ge(S("x_final"), c + 1))

        @block.vector
        def _(dve):
            mine = Steps(dve, S("dve_own"))
            mine.did(dve.memset(ones[:], 1.0))
            mine.did(dve.memset(eps[:, 0:1], EPS))
            mine.did(dve.memset(eps[:, 1:2], LN_EPS))
            mine.wait()
            dve.wait_ge(S("vec_turned"), 1)
            dve.tensor_copy(vec[:], psum[:, 5, 0:NVEC]).then_inc(S("vec_ready"), 1)
            dve.sem_inc(S("ones_ready"), 1)
            dve.sem_inc(stage_used, 4)
            dve.sem_inc(S("hid"), 2)
            dve.sem_inc(S("glu_done"), 2)
            for c in range(DC):
                dve.wait_ge(S("x_tp"), c + 1)
                dve.tensor_copy(X[:, c, :], psum[:, 6 + c % 2, :]).then_inc(S("x_turned"), 1)
            dve.wait_ge(S("vec_ready"), 1)
            dve_norm(dve, 0, 0, X, "g_mix", T, (ah, al))

            dve.wait_ge(S("attn_in"), 16 * 5)
            dve.wait_ge(S("wsp_turned"), 1)
            for g in range(4):
                ins_ = dve.tensor_tensor(wspT[:, g, :], psum[:, 4, g * P:(g + 1) * P], upper[:], ALU.mult)
            ins_.then_inc(S("wspT_ready"), 1)
            dve.wait_ge(S("rs_ready"), 1)
            for t in range(TC):
                dve.scalar_tensor_tensor(out=vv[:, t, :], in0=vv[:, t, :], scalar=rs[:, t:t + 1], in1=grow[:],
                                         op0=ALU.mult, op1=ALU.mult).then_inc(S("vv_normed"), 1)
            for g in range(4):
                dve.wait_ge(S("mixed"), g + 1)
                if g >= 2:
                    dve.wait_ge(S("sgu_lo"), g - 1)
                b_ = brow[:, g:g + 1, :].to_broadcast([P, TC, P])
                n_ = nt[:, g % 2, :].rearrange("p (t s) -> p t s", t=TC)
                mine.did(dve.tensor_tensor(n_, psum[:, 6 + g % 2, :].rearrange("p (t s) -> p t s", t=TC), b_, ALU.add))
                mine.wait()
                dve.tensor_tensor(nt[:, g % 2, :], nt[:, g % 2, :], uu[:, g, :], ALU.mult).then_inc(S("sgu_done"), 1)
                dve.wait_ge(S("sgu_hi"), g + 1)
                dve.tensor_tensor(yl[:, 2 + g, :], nt[:, g % 2, :], yh[:, 2 + g, :].bitcast(F32), ALU.subtract)\
                   .then_inc(S("sgu_lo"), 1)

            def score(u):
                h, r = divmod(u, 4)
                bank = 4 + 2 * (u % 2)
                dve.wait_ge(S("scores"), u + 1)
                if u >= 2:
                    dve.wait_ge(S("p_turned"), u - 1)
                for gi in range(3):
                    k = -float(slopes[gi, h]) * HD ** 0.5
                    d_ = dist[:, r, :] if gi == 0 else dist2[:, gi - 1, :]
                    src = psum[:, bank, :] if gi == 0 else psum[:, bank + 1, (gi - 1) * P:gi * P]
                    dst = sc[:, u % 2, 0:T] if gi == 0 else sc[:, u % 2, T + (gi - 1) * P:T + gi * P]
                    mine.did(dve.scalar_tensor_tensor(out=dst, in0=d_, scalar=k, in1=src, op0=ALU.mult, op1=ALU.add))
                mine.wait()
                mine.did(dve.tensor_reduce(mx[:, u:u + 1], sc[:, u % 2, :], AX_X, ALU.max))
                mine.wait()
                dve.tensor_scalar(nmx[:, u:u + 1], mx[:, u:u + 1], -(HD ** -0.5), None, ALU.mult).then_inc(S("scored"), 1)

            def pT_b(u):
                dve.wait_ge(S("p_turned"), u + 1)
                if u:
                    dve.wait_ge(S("attended"), u)
                dve.tensor_copy(pT[:, T:768], psum[:, 1, 0:256]).then_inc(S("pT_ready_b"), 1)

            def attend(u):
                h, r = divmod(u, 4)
                dve.wait_ge(S("probs"), u + 1)
                mine.did(dve.reciprocal(rden[:, u:u + 1], den[:, u:u + 1]))
                mine.wait()
                dve.wait_ge(S("attended"), u + 1)
                dve.tensor_scalar(ya[:, r, h * HD:(h + 1) * HD], psum[:, 2 + u % 2, 0:HD], rden[:, u:u + 1], None,
                                  ALU.mult).then_inc(S("y_ready"), 1)

            dve.wait_ge(S("dist_in"), 16)
            score(0)
            for u in range(16):
                if u < 15:
                    score(u + 1)
                pT_b(u)
                attend(u)
            for c in range(2):
                dve.wait_ge(S("y_hi"), c + 1)
                dve.tensor_tensor(yl[:, c, :].rearrange("p (j r) -> p r j", r=4),
                                  psum[:, 4 + c, :].rearrange("p (r j) -> p r j", r=4),
                                  yh[:, c, :].rearrange("p (j r) -> p r j", r=4).bitcast(F32), ALU.subtract)\
                   .then_inc(S("yT_ready"), 1)

            def per_stage(name, fn):
                s = by_name[name]
                per = len(s.body) // s.kblocks * s.width
                for i in passes(dve, s):
                    for k in range(per):
                        dve.wait_ge(acc_free, i * per + (first_acc[name] + k + 1 + ACCS))
                        fn(i, k, per)

            def gate1(i, k, per):
                c = bass.ds(i * per + k, 1)
                dve.tensor_tensor(m1[:, c, :], stg[:, k:k + 1, :], m1[:, c, :], ALU.mult).then_inc(stage_used, 1)

            def gate2(i, k, per):
                c = bass.ds(i * per + k, 1)
                dve.tensor_tensor(m2[:, c, :], stg[:, k:k + 1, :], m2[:, c, :], ALU.mult).then_inc(stage_used, 1)
                dve.wait_ge(stage_used, i * per + (4 + 8 + k + 1))
                dve.tensor_tensor(m1[:, c, :], m1[:, c, :], m2[:, c, :], ALU.add).then_inc(S("merged"), 1)

            per_stage("gate_attn", gate1)
            dve.sem_inc(S("merged"), 8)
            per_stage("gate_sgu", gate2)
            for c in range(8):
                dve.wait_ge(S("merge_hi"), c + 1)
                dve.tensor_tensor(al[:, c, :], m1[:, c, :], ah[:, c, :].bitcast(F32), ALU.subtract)\
                   .then_inc(S("merge_split"), 1)

            def residual(name, staged0):
                def add(i, k, per):
                    c = bass.ds(i * per + k, 1) if per < 8 else slice(k, k + 1)
                    sl = (staged0 + k) % 4
                    dve.tensor_tensor(X[:, c, :], X[:, c, :], stg[:, sl:sl + 1, :], ALU.add).then_inc(stage_used, 1)
                per_stage(name, add)

            residual("out", 16)
            for c in range(DC):
                dve.wait_ge(S("mem_tp"), c + 1)
                dve.tensor_copy(memT[:, c, :], psum[:, 6 + c % 2, 0:NM]).then_inc(S("mem_turned"), 1)
            dve_norm(dve, 1, 1, memT, "g_mem", NM, (mh, ml))
            dve_norm(dve, 2, 2, X, "g_cross", T, (ah, al))

            def cmaxes(u):
                dve.wait_ge(S("cscores"), u + 1)
                mine.did(dve.tensor_reduce(crd[:, u:u + 1], psum[:, 4 + u % 2, 0:NM], AX_X, ALU.max))
                mine.wait()
                dve.tensor_scalar(cmx[:, u:u + 1], crd[:, u:u + 1], -(P ** -0.5), None, ALU.mult).then_inc(S("cmaxed"), 1)

            def cnorm(u):
                dve.wait_ge(S("cprobs"), u + 1)
                mine.did(dve.reciprocal(crd[:, u:u + 1], cden[:, u:u + 1]))
                mine.wait()
                dve.tensor_scalar(cs[:, u % 4, :], cs[:, u % 4, :], crd[:, u:u + 1], None, ALU.mult)\
                   .then_inc(S("cnormed"), 1)

            def co_lo(h):
                dve.wait_ge(S("co_hi"), h + 1)
                dve.tensor_tensor(yl[:, h, :], psum[:, h, :], yh[:, h, :].bitcast(F32), ALU.subtract)\
                   .then_inc(S("co_split"), 1)

            cmaxes(0)
            for u in range(16):
                if u < 15:
                    cmaxes(u + 1)
                cnorm(u)
            for h in range(4):
                co_lo(h)
            residual("cross_o", 24)
            dve_norm(dve, 3, 3, X, "g_ffn", T, (ah, al))

            def swiglu(name, staged, hid0):
                s = by_name[name]
                for i in passes(dve, s):
                    for k in range(2):
                        dve.wait_ge(acc_free, i * 4 + (first_acc[name] + 2 * k + 2 + ACCS))
                        dve.tensor_tensor(nt[:, k, :], stg[:, 2 * k, :], stg[:, 2 * k + 1, :], ALU.mult).then_inc(S("hid"), 1)
                        dve.wait_ge(S("hid_hi"), i * 2 + (hid0 + k + 1))
                        dve.tensor_tensor(hl[:, bass.ds(i * 2 + k, 1), :], nt[:, k:k + 1, :],
                                          hh[:, bass.ds(i * 2 + k, 1), :].bitcast(F32), ALU.subtract)\
                           .then_inc(S("hid_split"), 1)

            swiglu("gate_up", 32, 0)
            residual("down", 32)
            if upto == 1:
                return
            dve_norm(dve, 4, 0, X, "g_final", T)
            dve.wait_ge(S("crows_turned"), 1)
            dve.tensor_copy(conv_w[:], psum[:, 5, 0:CONV_K * 8])
            dve.tensor_copy(short_w[:], psum[:, 5, 2 * P:2 * P + SHORT_K * 24]).then_inc(S("taps_ready"), 1)
            dve_norm(dve, 5, 4, X, "g_mix_2", T, (ah, al))
            dve.wait_ge(S("ab_hi"), 1)
            dve.tensor_tensor(abl[:], abw[:], abh[:].bitcast(F32), ALU.subtract).then_inc(S("ab_split"), 1)
            mine.did(dve.memset(cp[:, :, 0:CONV_PAD], 0.0))
            mine.did(dve.memset(cp[:, :, CONV_PAD + T:], 0.0))

            s = by_name["glu"]
            for i in passes(dve, s):
                for k in range(2):
                    dve.wait_ge(acc_free, i * 4 + (first_acc["glu"] + 2 * k + 2 + ACCS))
                    dve.tensor_tensor(cp[:, bass.ds(i * 2 + k, 1), CONV_PAD:CONV_PAD + T], stg[:, 2 * k:2 * k + 1, :],
                                      stg[:, 2 * k + 1:2 * k + 2, :], ALU.mult).then_inc(S("glu_done"), 1)
            cb = vec_at["conv_dw_b_2"]
            dve.wait_ge(S("taps_ready"), 1)
            dve.wait_ge(S("spilled"), 16)
            mine.wait()
            dve.wait_ge(S("glu_done"), 2 + 8)
            with dve.Fori(0, DC // 2) as i:
                for k in range(CONV_K):
                    for j in range(2):
                        c = i * 2 + j
                        src, dst = cp[:, bass.ds(c, 1), k:k + T], X[:, bass.ds(c, 1), :]
                        w = conv_w[:, bass.ds(c + 8 * k, 1)]
                        if k == 0:
                            ins_ = dve.tensor_scalar(dst, src, w, vec[:, bass.ds(c + cb, 1)], ALU.mult, ALU.add)
                        else:
                            dve.wait_ge(S("tap"), i * (2 * CONV_K - 2) + (2 * (k - 1) + j + 1))
                            ins_ = dve.scalar_tensor_tensor(out=dst, in0=src, scalar=w, in1=dst, op0=ALU.mult, op1=ALU.add)
                        ins_.then_inc(S("tap") if k < CONV_K - 1 else S("conv_done"), 1)

            dve.wait_ge(S("ab_ready"), 1)
            mine.did(dve.tensor_copy(ab[:], psum[:, 5, 0:128].rearrange("p (t u) -> p t u", t=TC)))
            mine.wait()
            dtb = arow[:, 1:2, :].to_broadcast([P, TC, 16])
            dve.wait_ge(S("arow_in"), 32)
            dve.tensor_tensor(tmp[:, 0], ab[:, :, 0:16], dtb, ALU.add).then_inc(S("ab_sum"), 1)
            dve.wait_ge(S("ab_abs"), 3)
            mine.did(dve.scalar_tensor_tensor(out=tmp[:, 2], in0=tmp[:, 0], scalar=0.0, in1=tmp[:, 1], op0=ALU.max, op1=ALU.add))
            mine.wait()
            dve.wait_ge(S("alog_exp"), 1)
            dve.scalar_tensor_tensor(out=coef[:, 0], in0=tmp[:, 2], scalar=-1.0, in1=arow[:, 0:1, :].to_broadcast([P, TC, 16]),
                                     op0=ALU.mult, op1=ALU.mult).then_inc(S("g_ready"), 1)
            dve.wait_ge(S("masks_in"), 32)
            dve.wait_ge(S("cum_ready"), 1)
            cum = [psum[:, 6, d * 64:(d + 1) * 64].rearrange("p (t u) -> p t u", t=TC) for d in range(3)]
            for d in range(DIRS):
                u = slice(8 * d, 8 * d + 8)
                mine.did(dve.tensor_scalar(coef[:, 2, :, u], cum[d][:, :, u], -1.0, None, ALU.mult))
            mine.wait()
            mine.did(dve.tensor_tensor(coef[:, 3], cum[2], coef[:, 2], ALU.add))
            mine.did(dve.tensor_copy(coef[:, 4], cum[2]))
            mine.wait()
            dve.tensor_scalar(coef[:, 3], coef[:, 3], 0.0, None, ALU.min).then_inc(S("tail_arg"), 1)

            dve.wait_ge(S("conv_sum"), 1)
            mine.did(dve.tensor_scalar(mu[:], psum[:, 4, :], 1.0 / D, None, ALU.mult))
            mine.wait()
            dve.wait_ge(S("conv_done"), 8)
            for c in range(DC):
                dve.tensor_tensor(X[:, c, :], X[:, c, :], mu[:], ALU.subtract).then_inc(S("centred"), 1)
            dve.wait_ge(S("c_r"), 1)
            lg = vec_at["conv_ln_g_2"]
            for c in range(DC):
                dve.scalar_tensor_tensor(out=X[:, c, :], in0=X[:, c, :], scalar=vec[:, lg + c:lg + c + 1], in1=rbc[:],
                                         op0=ALU.mult, op1=ALU.mult).then_inc(S("c_scaled"), 1)
            for c in range(DC):
                dve.wait_ge(S("c_hi"), c + 1)
                dve.tensor_tensor(zl[:, c, :], X[:, c, :], zh[:, c, :].bitcast(F32), ALU.subtract).then_inc(S("c_split"), 1)

            def gate_conv(i, k, per):
                c = bass.ds(i * per + k, 1)
                dve.tensor_tensor(yg[:, c, :], stg[:, k:k + 1, :], yg[:, c, :], ALU.mult).then_inc(stage_used, 1)

            per_stage("conv_out", gate_conv)
            dve_heads(dve, mine)

            def gate_delta(i, k, per):
                c = bass.ds(i * per + k, 1)
                dve.tensor_tensor(d2[:, c, :], stg[:, k:k + 1, :], d2[:, c, :], ALU.mult).then_inc(stage_used, 1)
                dve.wait_ge(stage_used, i * per + (4 + 48 + k + 1))
                dve.tensor_tensor(yg[:, c, :], yg[:, c, :], d2[:, c, :], ALU.add).then_inc(S("y_sum"), 1)

            per_stage("gate_b", gate_delta)
            for c in range(8):
                dve.wait_ge(S("y_hi2"), c + 1)
                dve.tensor_tensor(zl[:, c, :], yg[:, c, :], zh[:, c, :].bitcast(F32), ALU.subtract).then_inc(S("y_split"), 1)
            dve.wait_ge(S("x_back"), 16)
            residual("o2", 56)
            dve_norm(dve, 6, 5, X, "g_ffn_2", T, (ah, al))
            swiglu("gate_up2", 64, FC)
            residual("down2", 64)
            for c in range(2):
                dve.wait_ge(S("pp_hi"), c + 1)
                dve.tensor_tensor(pl[:, c, :], psum[:, 6 + c, :], ph[:, c, :].bitcast(F32), ALU.subtract)\
                   .then_inc(S("pp_split"), 1)
            dve_norm(dve, 7, 0, PL, "g_pl_proj_2", T)
            dve_norm(dve, 8, 6, X, "g_pl_2", T, (ah, al))

            def gate_pl(i, k, per):
                c = i * per + k
                dve.tensor_tensor(PL[:, c, :], stg[:, k, :], PL[:, c, :], ALU.mult).then_inc(stage_used, 1)
                dve.wait_ge(stage_used, 4 + 72 + c + 1)
                dve.tensor_tensor(X[:, c, :], X[:, c, :], PL[:, c, :], ALU.add).then_inc(S("x_final"), 1)

            per_stage("pl_gate", gate_pl)
            dve.wait_ge(S("x_final"), 8)
            dve_norm(dve, 9, 0, X, "g_final_2", T)
            for n in range(8):
                t, half = divmod(n, 2)
                dve.wait_ge(S("o_turned"), n + 1)
                for q in range(2):
                    dve.tensor_copy(outt[:, t, half * 512 + q * 256:half * 512 + (q + 1) * 256],
                                    psum[:, 6 + n % 2, q * 256:(q + 1) * 256]).then_inc(S("out_ready"), 1)



_INS = ["x", "mem", "g_mix", "w_in", "b_gate", "w_sgu_spatial", "b_sgu_spatial", "g_sgu", "w_branch_attn",
        "w_branch_sgu", "w_out", "g_cross", "g_mem", "w_q_cross", "w_kv_cross", "w_o_cross", "g_ffn", "w_gate_up",
        "w_down", "g_final", "p_2", "g_mix_2", "w_in_2", "conv_dw_w_2", "conv_dw_b_2", "conv_ln_g_2", "conv_ln_b_2",
        "w_conv_out_2", "qkv_conv_w_2", "a_log_2", "dt_bias_2", "delta_norm_g_2", "w_delta_out_2", "w_o_2",
        "g_ffn_2", "w_gate_up_2", "w_down_2", "g_pl_2", "w_pl_gate_2", "w_pl_proj_2", "g_pl_proj_2", "g_final_2"]


def kernel(**inputs):
    import concourse.bacc as bacc
    from concourse.bass_utils import run_bass_kernel_spmd

    nc = bacc.Bacc("TRN2", target_bir_lowering=False, num_devices=1)
    arrays, aps = {}, {}
    for name, a in [(n, inputs[n]) for n in _INS] + list(shape_constants().items()):
        a = np.ascontiguousarray(a)
        arrays[f"in_{name}"] = a
        aps[name] = nc.dram_tensor(f"in_{name}", a.shape, mybir.dt.from_np(a.dtype), kind="ExternalInput").ap()
    out = nc.dram_tensor("out_0", (1, T, D), F32, kind="ExternalOutput").ap()
    build(nc, aps, out)
    r = run_bass_kernel_spmd(nc, [arrays], core_ids=[0])
    return r.results[0]["out_0"]
```

```python
from contextlib import ExitStack

import numpy as np

import concourse.bass as bass
from concourse import mybir

F32 = mybir.dt.float32
F32R = mybir.dt.float32r
ALU = mybir.AluOpType
ACT = mybir.ActivationFunctionType
AX_X = mybir.AxisListType.X

P = 128
D = 1024
DC = D // P
T = 512
TC = T // P
RING = 4
LEAD = 3
BLOCK = 1024
ACCS = 4
EPS = 1e-6
LN_EPS = 1e-5
HD = 64
FF = 2816
FC = FF // P
NM = 256
BIG = 1e30
CONV_K = 31
CONV_PAD = CONV_K // 2
SHORT_K = 5
SHORT_PAD = SHORT_K // 2
HEADS = 8
DIRS = 2
LEVELS = 6
LEVEL_FILL = [(3, 0), (3, 1), (7, None), (3, 2), (7, None), (4, None)]
CONV_TAPS_SOLVE = sum(taps for taps, _ in LEVEL_FILL)
HEAD_STEPS = 2 * (3 * (SHORT_K - 1) + CONV_K - 1 + 2 + 2 + 2 + 4 + 1 + 1)


def alibi_slopes():
    def pow2(n):
        start = 2.0 ** (-8.0 / n)
        return [start ** (i + 1) for i in range(n)]
    s = pow2(8) + pow2(16)[0::2][:4]
    return np.array(sorted(s, reverse=True), dtype=np.float32).reshape(3, 4)


def shape_constants():
    p = np.arange(P)
    eye = np.eye(P, dtype=np.float32)
    dist = np.full((P, TC, T), BIG, np.float32)
    for r in range(4):
        q = (4 * p + r)[:, None]
        k = np.arange(T)[None, :]
        ok = (q - k >= 0) & (q - k <= 128)
        dist[:, r][ok] = (q - k)[ok]
    steps = (p[:, None] - p[None, :]).astype(np.float32)
    d4 = np.where(steps >= 0, steps * 4, BIG).astype(np.float32)
    d16 = np.where((steps >= 0) & (steps % 4 == 0), steps * 4, BIG).astype(np.float32)
    dist2 = np.stack([d4, d16], 1)
    upper = (p[:, None] <= p[None, :]).astype(np.float32)
    level = np.zeros((P, DIRS, LEVELS + 1, P), np.float32)
    incl = np.zeros((P, DIRS, P), np.float32)
    for l in range(LEVELS + 1):
        w = 2 ** l
        s, c = p[:, None], p[None, :]
        same = (s // (2 * w)) == (c // (2 * w))
        level[:, 0, l] = same & ((s // w) % 2 == 0) & ((c // w) % 2 == 1)
        level[:, 1, l] = same & ((s // w) % 2 == 1) & ((c // w) % 2 == 0)
    incl[:, 0] = p[:, None] <= p[None, :]
    incl[:, 1] = p[:, None] >= p[None, :]
    return {"eye": eye, "dist": dist, "dist2": dist2, "upper": upper, "level": level, "incl": incl}


class Steps:

    def __init__(self, eng, sem):
        self.eng, self.sem, self.n, self.reg, self.per = eng, sem, 0, None, 0

    def did(self, ins):
        ins.then_inc(self.sem, 1)
        self.n += 1
        return self.n

    def wait(self, number=None):
        number = self.n if number is None else number
        self.eng.wait_ge(self.sem, number if self.reg is None else self.reg * self.per + number)

    def enter(self, reg, per):
        self.reg, self.per, self.start = reg, per, self.n

    def leave(self, count):
        assert self.n - self.start == self.per, (self.n - self.start, self.per)
        self.reg, self.n = None, self.start + count * self.per


class Stage:
    def __init__(self, name, w, kc, cols, loops, body, cstep, kind="T", kblocks=1):
        self.name, self.w, self.kc, self.cols, self.kind = name, w, kc, cols, kind
        self.loops, self.body, self.cstep, self.kblocks = loops, body, cstep, kblocks
        self.width = cols // P if kind == "T" else 1
        self.accs = loops * len(body) // kblocks * self.width
        assert loops == 1 or (len(body) % RING == 0 and len(body) // kblocks * self.width % ACCS == 0)
        self.n = self.loops * len(self.body)
        assert kc * cols == BLOCK


def stage_cols(name, w, col0, nchunks, kind="T", kc=8):
    cols = BLOCK // kc
    unroll = 4 if nchunks % 4 == 0 else nchunks
    return Stage(name, w, kc, cols, nchunks // unroll, [(0, col0 + j * cols) for j in range(unroll)], unroll * cols, kind)


def stage_pairs(name, w, colA, colB, pairs):
    assert pairs % 2 == 0
    body = [(0, colA), (0, colB), (0, colA + P), (0, colB + P)]
    return Stage(name, w, 8, P, pairs // 2, body, 2 * P)


def stage_down(name, w):
    body = [(2 * j, n) for n in (0, 512) for j in range(FC // 2)]
    return Stage(name, w, 2, 512, 1, body, 0, kblocks=FC // 2)


STAGES = [
    stage_cols("qk", "w_in", 0, 12),
    stage_cols("v", "w_in", 1536, 6, "N"),
    stage_cols("u", "w_in", 2304, 4),
    stage_cols("vv", "w_in", 2816, 4, "N"),
    stage_cols("branch_attn", "w_branch_attn", 0, 2, kc=2),
    stage_cols("gate_attn", "w_in", 3328, 8),
    stage_cols("branch_sgu", "w_branch_sgu", 0, 4, kc=4),
    stage_cols("gate_sgu", "w_in", 4352, 8),
    stage_cols("out", "w_out", 0, 8),
    stage_cols("mem_k", "w_kv_cross", 0, 4),
    stage_cols("mem_v", "w_kv_cross", 512, 4, "N"),
    stage_cols("cross_q", "w_q_cross", 0, 4),
    stage_cols("cross_o", "w_o_cross", 0, 4, kc=4),
    stage_pairs("gate_up", "w_gate_up", 0, FF, FC),
    stage_down("down", "w_down"),
]
STAGES2 = [
    stage_pairs("glu", "w_in_2", 0, D, 8),
    Stage("heads", "w_in_2", 8, P, 4, [(0, (2 + s) * D + h * P) for h in range(2) for s in range(4)], 2 * P),
    stage_cols("gate_a", "w_in_2", 6 * D + 32, 8),
    stage_cols("gate_b", "w_in_2", 7 * D + 32, 8),
    stage_cols("delta_out", "w_delta_out_2", 0, 8),
    stage_cols("conv_out", "w_conv_out_2", 0, 8),
    stage_cols("o2", "w_o_2", 0, 8),
    stage_pairs("gate_up2", "w_gate_up_2", 0, FF, FC),
    stage_down("down2", "w_down_2"),
    stage_cols("pl_proj", "w_pl_proj_2", 0, 2, kc=2),
    stage_cols("pl_gate", "w_pl_gate_2", 0, 8),
]

VECTORS = [("g_mix", 8), ("b_gate", 16), ("g_cross", 8), ("g_mem", 8), ("g_ffn", 8), ("g_final", 8),
           ("g_mix_2", 8), ("conv_dw_b_2", 8), ("conv_ln_g_2", 8), ("conv_ln_b_2", 8), ("g_ffn_2", 8),
           ("g_pl_2", 8), ("g_pl_proj_2", 8), ("g_final_2", 8), ("delta_norm_g_2", 1)]


def build(nc, ins, out, dump=None, upto=99):
    stages = STAGES + (STAGES2 if upto > 1 else [])
    first_block, n = {}, 0
    for s in stages:
        first_block[s.name] = n
        n += s.n
    NB = n
    first_acc, n = {}, 0
    for s in stages:
        first_acc[s.name] = n
        n += s.accs
    by_name = {s.name: s for s in stages}

    vec_at, n = {}, 0
    for name, rows in VECTORS:
        vec_at[name] = n
        n += rows
    NVEC = n

    with ExitStack() as ctx:
        def sb(name, shape, dt=F32, where=ctx):
            return where.enter_context(nc.sbuf_tensor("s_" + name, shape, dt))

        def sem(name):
            return ctx.enter_context(nc.semaphore(name))

        raw = sb("raw", [P, RING, BLOCK])
        whi = sb("whi", [P, RING, BLOCK], F32R)
        wlo = sb("wlo", [P, RING, BLOCK], F32R)
        X = sb("X", [P, DC, T])
        ah = sb("ah", [P, DC, T], F32R)
        al = sb("al", [P, DC, T], F32R)
        eye = sb("eye", [P, P])
        ones = sb("ones", [P, P])
        vec = sb("vec", [P, NVEC])
        eps = sb("eps", [P, 2])
        rbc = sb("rbc", [P, T])
        lnt = sb("lnt", [P, T])
        sq = sb("sq", [P, 2, T])
        nt = sb("nt", [P, 2, T])
        stg = sb("stg", [P, 4, T])

        psum = ctx.enter_context(nc.psum_tensor("psum", [P, 8, T], F32))

        with ExitStack() as one:
            yh = sb("yh", [P, 6, T], F32R, one)
            yl = sb("yl", [P, 6, T], F32R, one)
            with ExitStack() as a:
                vrows = sb("vrows", [P, P], F32, a)
                xin = sb("xin", [P, TC, D], F32, a)
            with ExitStack() as a:
                qk = sb("qk", [P, 12, T], F32, a)
                vt = sb("vt", [P, 4, 768], F32, a)
                uu = sb("uu", [P, 4, T], F32, a)
                vv = sb("vv", [P, TC, 512], F32, a)
                dist = vv
                dist2 = sb("dist2", [P, 2, P], F32, a)
                upper = sb("upper", [P, P], F32, a)
                wsp = sb("wsp", [P, 4, P], F32, a)
                wspT = sb("wspT", [P, 4, P], F32, a)
                brow = sb("brow", [P, 4, P], F32, a)
                grow = lnt
                sc = sb("sc", [P, 2, 768], F32, a)
                ya = stg[:, 0:2, :].rearrange("p a (b n) -> p (a b) n", n=256)
                pT = stg[:, 2:4, :].rearrange("p a n -> p (a n)")
                ss = sb("ss", [P, 16], F32, a)
                rs = sb("rs", [P, 16], F32, a)
                mx = sb("mx", [P, 16], F32, a)
                nmx = sb("nmx", [P, 16], F32, a)
                den = sb("den", [P, 16], F32, a)
                rden = sb("rden", [P, 16], F32, a)
            with ExitStack() as a:
                m1 = sb("m1", [P, DC, T], F32, a)
                m2 = sb("m2", [P, DC, T], F32, a)
            with ExitStack() as a:
                memin = sb("memin", [P, 2, D], F32, a)
                memT = sb("memT", [P, DC, NM], F32, a)
                mh = sb("mh", [P, DC, NM], F32R, a)
                ml = sb("ml", [P, DC, NM], F32R, a)
                ckT = sb("ckT", [P, 4, NM], F32, a)
                cv = sb("cv", [P, 2, 512], F32, a)
                cq = sb("cq", [P, 4, T], F32, a)
                cs = sb("cs", [P, 4, NM], F32, a)
                cpT = sb("cpT", [P, 2, T], F32, a)
                cmx = sb("cmx", [P, 16], F32, a)
                cden = sb("cden", [P, 16], F32, a)
                crd = sb("crd", [P, 16], F32, a)
        with ExitStack() as a:
            hh = sb("hh", [P, FC, T], F32R, a)
            hl = sb("hl", [P, FC, T], F32R, a)

        conv_w = sb("conv_w", [P, CONV_K * 8])
        short_w = sb("short_w", [P, SHORT_K * 24])
        with ExitStack() as two:
            coef = sb("coef", [P, 5, TC, 16], F32, two)
            hc = sb("hc", [P, 5, TC, DIRS], F32, two)
            of = sb("of", [P, DC, T], F32, two)
            cc = sb("cc", [P, DC, T], F32, two)
            with ExitStack() as b:
                level = sb("level", [P, DIRS, LEVELS + 1, P], F32, b)
                incl = sb("incl", [P, DIRS, P], F32, b)
                cp = sb("cp", [P, DC, T + CONV_K - 1], F32, b)
                with ExitStack() as a:
                    crows = sb("crows", [P, 3, P], F32, a)
                    abw = sb("abw", [P, DC, 32], F32, a)
                    abh = sb("abh", [P, DC, 32], F32R, a)
                    abl = sb("abl", [P, DC, 32], F32R, a)
                    arow = sb("arow", [P, 2, 16], F32, a)
                    ab = sb("ab", [P, TC, 32], F32, a)
                    tmp = sb("tmp", [P, 3, TC, 16], F32, a)
                with ExitStack() as a:
                    raw3 = sb("raw3", [P, 3, T + SHORT_K - 1], F32, a)
                    tok = sb("tok", [P, 2, TC, P], F32, a)
                    E_ = sb("E", [P, DIRS, TC, P], F32, a)
                    AT = sb("AT", [P, DIRS, TC, P], F32, a)
                    EG = sb("EG", [P, DIRS, TC, P], F32, a)
                    KB = sb("KB", [P, DIRS, TC, P], F32, a)
                    vnew = sb("vnew", [P, DIRS, 2, P], F32, a)
                    St = sb("St", [P, DIRS, P], F32, a)
            with ExitStack() as b:
                zh = sb("zh", [P, DC, T], F32R, b)
                zl = sb("zl", [P, DC, T], F32R, b)
                gb = sb("gb", [P, DC, T], F32, b)
        ga = X
        mu = nt[:, 1, :]
        XV = X[:, :, :].rearrange("p (k d) (t n) -> p k d t n", k=4, t=TC)
        Mi, MT, QK, QD = XV[:, 0], XV[:, 1], XV[:, 2], XV[:, 3]
        with ExitStack() as a:
            ph = sb("ph", [P, 2, T], F32R, a)
            pl = sb("pl", [P, 2, T], F32R, a)
            pin = sb("pin", [P, TC, 256], F32, a)
            PL = sb("PL", [P, DC, T], F32, a)
            outt = sb("outt", [P, TC, D], F32, a)
        spill = nc.dram_tensor("x_spill", [P, DC, T], F32).ap()

        sems = {}

        def S(name):
            if name not in sems:
                sems[name] = ctx.enter_context(nc.semaphore(name))
            return sems[name]

        raw_loaded = [S(f"raw_loaded{i}") for i in range(RING)]
        hi_ready = S("hi_ready")
        lo_ready = S("lo_ready")
        block_used = S("block_used")
        acc_free = S("acc_free")
        stage_used = S("stage_used")

        def weight(name):
            w = ins[name]
            if len(w.shape) == 3:
                w = w.rearrange("a k n -> (a k) n")
            return w.rearrange("(c p) n -> p c n", p=P)

        def passes(eng, s):
            if s.loops == 1 or s is stages[-1]:
                for i in range(s.loops):
                    yield i
            else:
                with eng.Fori(0, s.loops) as i:
                    yield i

        def count(s, i, j, extra=0):
            return i * len(s.body) + (first_block[s.name] + j + extra)

        def acc_number(s, i, g, m, extra=0):
            per = len(s.body) // s.kblocks * s.width
            return i * per + (first_acc[s.name] + g * s.width + m + extra)

        def pe_stage(pe, name, act_hi, act_lo, tokens=T, cols_of=None):
            s = by_name[name]
            n_tok = tokens // P
            for i in passes(pe, s):
                for j, (k0, _) in enumerate(s.body):
                    slot = (first_block[name] + j) % RING
                    g, kb = j // s.kblocks, j % s.kblocks
                    pe.wait_ge(lo_ready, count(s, i, j, RING + 1))
                    if s.kind == "T":
                        for m in range(s.width):
                            bank = (first_acc[name] + g * s.width + m) % ACCS
                            if kb == 0:
                                pe.wait_ge(acc_free, acc_number(s, i, g, m, 1))
                            for k in range(s.kc):
                                w = slice(k * s.cols + m * P, k * s.cols + (m + 1) * P)
                                kk = k0 + k
                                o = psum[:, bank, 0:tokens]
                                first, last = kb == 0 and k == 0, kb == s.kblocks - 1 and k == s.kc - 1
                                pe.matmul(o, whi[:, slot, w], act_hi[:, kk, :], start=first, stop=False)
                                pe.matmul(o, whi[:, slot, w], act_lo[:, kk, :], start=False, stop=False)
                                mm = pe.matmul(o, wlo[:, slot, w], act_hi[:, kk, :], start=False, stop=last)
                    else:
                        bank = (first_acc[name] + g) % ACCS
                        pe.wait_ge(acc_free, acc_number(s, i, g, 0, 1))
                        for t in range(n_tok):
                            tok = cols_of(t)
                            o = psum[:, bank, t * P:(t + 1) * P]
                            for k in range(s.kc):
                                w = slice(k * P, (k + 1) * P)
                                pe.matmul(o, act_hi[:, k, tok], whi[:, slot, w], start=k == 0, stop=False)
                                pe.matmul(o, act_hi[:, k, tok], wlo[:, slot, w], start=False, stop=False)
                                mm = pe.matmul(o, act_lo[:, k, tok], whi[:, slot, w], start=False, stop=k == s.kc - 1)
                    mm.then_inc(block_used, 1)

        def act_round(act, b, q, per4):
            slot = q % RING
            act.wait_ge(raw_loaded[slot], per4 * 16 + 16 * (q // RING + 1))
            act.wait_ge(block_used, b + 1)
            act.activation(whi[:, slot, :], raw[:, slot, :], ACT.Copy).then_inc(hi_ready, 1)

        def act_stage(act, name, empty):
            s = by_name[name]
            for i in passes(act, s):
                for j in range(len(s.body)):
                    q = first_block[name] + j + LEAD
                    last = s is stages[-1]
                    if not (last and q + i * len(s.body) >= NB):
                        act_round(act, count(s, i, j, LEAD), q, i * (len(s.body) // RING) if s.loops > 1 else 0) if not (last and s.loops > 1) else \
                            act_round(act, q + i * len(s.body), q + i * len(s.body), 0)
                    if j % s.kblocks == s.kblocks - 1:
                        g = j // s.kblocks
                        act.wait_ge(block_used, count(s, i, j, RING + 1))
                        for m in range(s.width):
                            a = first_acc[name] + g * s.width + m
                            empty(i, g, m, a, a % ACCS).then_inc(acc_free, 1)

        def sem_base(n):
            return 8 * n

        def act_norm(act, mine, n, src, tokens, ready, hilo=None):
            for c in range(DC):
                ready(c)
                act.wait_ge(S("sq_free"), 8 * n + c + 1)
                act.activation(sq[:, c % 2, 0:tokens], src[:, c, :], ACT.Square).then_inc(S("sq_ready"), 1)
            act.wait_ge(S("sq_free"), 8 * n + 8 + 2)
            if n:
                act.wait_ge(S("n_ready"), 8 * n)
            mine.did(act.activation(lnt[:, 0:tokens], psum[:, 4, 0:tokens], ACT.Ln, scale=1.0 / D, bias=eps[:, 0:1]))
            mine.wait()
            act.activation(rbc[:, 0:tokens], lnt[:, 0:tokens], ACT.Exp, scale=-0.5).then_inc(S("r_ready"), 1)
            if hilo is not None:
                for c in range(DC):
                    act.wait_ge(S("n_ready"), 8 * n + c + 1)
                    act.activation(hilo[0][:, c, :], nt[:, c % 2, 0:tokens], ACT.Copy).then_inc(S("nh_ready"), 1)

        def pe_norm(pe, n, tokens):
            if n:
                pe.wait_ge(S("r_ready"), n)
            for c in range(DC):
                pe.wait_ge(S("sq_ready"), 8 * n + c + 1)
                pe.matmul(psum[:, 4, 0:tokens], ones[:, :], sq[:, c % 2, 0:tokens], start=c == 0, stop=c == DC - 1)\
                  .then_inc(S("sq_free"), 1)

        def dve_norm(dve, n, nh, src, gain, tokens, hilo=None):
            g0 = vec_at[gain]
            dve.wait_ge(S("r_ready"), n + 1)

            def low(c):
                dve.wait_ge(S("nh_ready"), 8 * nh + c + 1)
                dve.tensor_tensor(hilo[1][:, c, :], nt[:, c % 2, 0:tokens], hilo[0][:, c, :].bitcast(F32),
                                  ALU.subtract).then_inc(S("normed"), 1)

            for c in range(DC):
                if hilo is not None and c >= 2:
                    dve.wait_ge(S("normed"), 8 * nh + c - 1)
                dst = nt[:, c % 2, 0:tokens] if hilo is not None else src[:, c, :]
                dve.scalar_tensor_tensor(out=dst, in0=src[:, c, :], scalar=vec[:, g0 + c:g0 + c + 1],
                                         in1=rbc[:, 0:tokens], op0=ALU.mult, op1=ALU.mult).then_inc(S("n_ready"), 1)
                if hilo is not None and c >= 1:
                    low(c - 1)
            if hilo is not None:
                low(DC - 1)

        def act_split(act, ready, n0, src, hi, done, chunks):
            for c in range(chunks):
                act.wait_ge(S(ready), n0 + c + 1)
                act.activation(hi[:, c, :], src[:, c, :], ACT.Copy).then_inc(S(done), 1)

        def head_step(i, j, per, k):
            return i * (2 * per) + (j * per + k)

        chunk_order = [range(TC), range(TC - 1, -1, -1)]
        PASSES = HEADS // 2
        heads = by_name["heads"]

        def head_passes(eng):
            with eng.Fori(0, PASSES - 1) as i:
                yield i, False
            yield PASSES - 1, True

        def flat(ap):
            return ap.rearrange("p t n -> p (t n)")

        def head_block(i, j, n, extra):
            return count(heads, i, 4 * j + n, extra)

        def head_acc(i, j, n, extra=0):
            return acc_number(heads, i, 4 * j + n, 0, ACCS + 1 + extra)

        def pe_heads(pe):
            def project(i, j, n, part, parts):
                slot, bank = (first_block["heads"] + 4 * j + n) % RING, 4 + n % 2
                if part == 0:
                    pe.wait_ge(lo_ready, head_block(i, j, n, RING + 1))
                    pe.wait_ge(acc_free, head_acc(i, j, n, -2))
                for k in range(part * DC // parts, (part + 1) * DC // parts):
                    wk = slice(k * P, (k + 1) * P)
                    pe.matmul(psum[:, bank, :], whi[:, slot, wk], ah[:, k, :], start=k == 0, stop=False)
                    pe.matmul(psum[:, bank, :], whi[:, slot, wk], al[:, k, :], start=False, stop=False)
                    mm = pe.matmul(psum[:, bank, :], wlo[:, slot, wk], ah[:, k, :], start=False, stop=k == DC - 1)
                if part == parts - 1:
                    mm.then_inc(block_used, 1)

            def lengths(i, j):
                for n in range(2):
                    pe.wait_ge(S("l2_sq"), head_step(i, j, 2, n + 1))
                    pe.wait_ge(acc_free, head_acc(i, j, 2 + n))
                    pe.matmul(psum[:, 4 + n, :], ones[:], sq[:, n, :], start=True, stop=True).then_inc(S("l2_sum"), 1)

            def start(i, j, before, after):
                w = lambda name, per, k: pe.wait_ge(S(name), head_step(i, j, per, k))
                w1 = lambda name, per, k: pe.wait_ge(S(name), head_step(i, j - 1, per, k))
                w("hc_ready", 1, 1)
                for d in range(DIRS):
                    for t in range(TC):
                        mm = pe.matmul(psum[:, d, t * P:(t + 1) * P], hc[:, 0, t, d:d + 1].to_broadcast([P, P]),
                                       incl[:, d, :], start=True, stop=True)
                    mm.then_inc(S("g_bc"), 1)
                for d in range(DIRS):
                    for t in range(TC):
                        mm = pe.matmul(psum[:, 2 + d, t * P:(t + 1) * P], hc[:, 1, t, d:d + 1].to_broadcast([P, P]),
                                       eye[:], start=True, stop=True)
                    mm.then_inc(S("b_bc"), 1)
                w("qk_scaled", 2, 2)
                if before:
                    w1("o_both", 1, 1)
                for n in range(2):
                    for t in range(TC):
                        tk = slice(t * P, (t + 1) * P)
                        mm = pe.matmul(psum[:, 4 + n, tk], stg[:, 1, tk], stg[:, n, tk], start=True, stop=True)
                    mm.then_inc(S("kq_ready"), 1)
                w("qkv_silu", 3, 3)
                if before:
                    w1("s_ready", 2 * TC, 2 * TC)
                for n in range(2):
                    for t in range(TC):
                        mm = pe.transpose(psum[:, 6 + n, t * P:(t + 1) * P], stg[:, 1 + n, t * P:(t + 1) * P], eye[:])
                    mm.then_inc(S("kv_turned"), 1)
                if before:
                    w("tok_ready", 2, 2)
                    w1("o_sq", 1, 1)
                    pe.matmul(psum[:, 7, :], ones[:], sq[:, 0, :], start=True, stop=True).then_inc(S("o_sum"), 1)
                if after:
                    w("qk_masked", 4, 4)
                    project(i, j + 1, 0, 0, 1)
                for d in range(DIRS):
                    w("mt0_ready", 2, d + 1)
                    w("tok_ready", 2, 2)
                    if before and d == 1:
                        w1("o_ln", 1, 1)
                    for t in range(TC):
                        mm = pe.transpose(psum[:, 6 + d, t * P:(t + 1) * P], MT[:, d, t, :], eye[:])
                    mm.then_inc(S("m0_turned"), 1)
                if after:
                    project(i, j + 1, 1, 0, 1)

            def solve(i, j, after):
                w = lambda name, per, k: pe.wait_ge(S(name), head_step(i, j, per, k))
                for l in range(LEVELS):
                    for d in range(DIRS):
                        w("lev_ready", 2 * LEVELS, 2 * l + d + 1)
                        w("m_ready", 2 * LEVELS, 2 * l + d + 1)
                        if l:
                            w("mt_ready", 2 * LEVELS, 2 * l + d - 1)
                        for t in range(TC):
                            mm = pe.matmul(psum[:, 6 + d, t * P:(t + 1) * P], E_[:, d, t, :], Mi[:, d, t, :],
                                           start=True, stop=True)
                        mm.then_inc(S("p_ready"), 1)
                    if after and l < 4:
                        project(i, j + 1, 2 + l // 2, l % 2, 2)
                    if after and l == 4:
                        lengths(i, j + 1)
                    for d in range(DIRS):
                        w("q_ready", 2 * LEVELS, 2 * l + d + 1)
                        if l == 0:
                            w("kb_ready", 2, d + 1)
                        for t in range(TC):
                            if l < LEVELS - 1:
                                mm = pe.matmul(psum[:, d, t * P:(t + 1) * P], MT[:, d, t, :], EG[:, d, t, :],
                                               start=True, stop=True)
                        if l < LEVELS - 1:
                            mm.then_inc(S("m_new"), 1)
                        for t in range(TC):
                            mm = pe.matmul(psum[:, 2 + d, t * P:(t + 1) * P], EG[:, d, t, :], MT[:, d, t, :],
                                           start=True, stop=True)
                        mm.then_inc(S("mt_new"), 1)

            def recur(i, j, after):
                w = lambda name, per, k: pe.wait_ge(S(name), head_step(i, j, per, k))
                for n in range(TC):
                    for d in range(DIRS):
                        t = chunk_order[d][n]
                        if n:
                            w("s_ready", 2 * TC, 2 * (n - 1) + d + 1)
                            pe.matmul(psum[:, 6 + d, 0:P], KB[:, d, t, :], St[:, d, :], start=True, stop=True)\
                              .then_inc(S("r_mm"), 1)
                    for d in range(DIRS):
                        t = chunk_order[d][n]
                        if n:
                            w("v_ready", 2 * (TC - 1), 2 * (n - 1) + d + 1)
                            v = vnew[:, d, 0, :]
                        else:
                            w("vb_ready", 2, d + 1)
                            w("mt_ready", 2 * LEVELS, 2 * (LEVELS - 1) + d + 1)
                            v = AT[:, d, t, :]
                        pe.matmul(psum[:, 6 + d, P:2 * P], MT[:, d, t, :], v, start=True, stop=True)\
                          .then_inc(S("vn_mm"), 1)
                    for d in range(DIRS):
                        t = chunk_order[d][n]
                        o = psum[:, 4 + d, t * P:(t + 1) * P]
                        if n:
                            pe.matmul(o, St[:, d, :], QD[:, d, t, :], start=True, stop=False)
                        w("vn_ready", 2 * TC, 2 * n + d + 1)
                        if n == 0:
                            w("kt_ready", 2, d + 1)
                            if after:
                                pe.wait_ge(S("l2_ln"), head_step(i, j + 1, 2, 2))
                            else:
                                w("qk_masked", 4, 4)
                        pe.matmul(psum[:, 6 + d, 2 * P:3 * P], E_[:, d, t, :], vnew[:, d, 1, :], start=True, stop=True)\
                          .then_inc(S("s_mm"), 1)
                        mm = pe.matmul(o, vnew[:, d, 1, :], QK[:, d, t, :], start=n == 0, stop=True)
                        if n == TC - 1:
                            mm.then_inc(S("o_ready"), 1)
                        else:
                            mm.then_inc(S("o_part"), 1)

            pe.wait_ge(acc_free, first_acc["heads"] + ACCS)
            for n in range(4):
                project(0, 0, n, 0, 1)
            lengths(0, 0)
            start(0, 0, False, True)
            for i, last in head_passes(pe):
                for j in range(2):
                    after = not (last and j == 1)
                    solve(i, j, after)
                    recur(i, j, after)
                    if after:
                        start(i, j + 1, True, not last)
            pe.wait_ge(S("o_sq"), HEADS)
            pe.matmul(psum[:, 7, :], ones[:], sq[:, 0, :], start=True, stop=True).then_inc(S("o_sum"), 1)

        def act_heads(act):
            def take(i, j, n):
                b = 4 * j + n
                act_round(act, count(heads, i, b, LEAD), first_block["heads"] + b + LEAD, i * 2)
                act.wait_ge(block_used, head_block(i, j, n, RING + 1))
                bank = 4 + n % 2
                if n < 3:
                    act.wait_ge(S("raw_free"), head_step(i, j, 1, 1))
                    a = act.activation(raw3[:, n, SHORT_PAD:SHORT_PAD + T], psum[:, bank, :], ACT.Copy)
                else:
                    a = act.activation(of[:, bass.ds(i * 2 + j, 1), :], psum[:, bank:bank + 1, :], ACT.Silu)
                a.then_inc(acc_free, 1)

            def silu(i, j, n):
                act.wait_ge(S("conv3"), head_step(i, j, 3, n + 1))
                act.activation(stg[:, n, :], stg[:, n, :], ACT.Silu).then_inc(S("qkv_silu"), 1)

            def squares(i, j):
                for n in range(2):
                    act.wait_ge(S("qkv_silu"), head_step(i, j, 3, n + 1))
                    act.activation(sq[:, n, :], stg[:, n, :], ACT.Square).then_inc(S("l2_sq"), 1)

            def inverse_lengths(i, j):
                for n in range(2):
                    act.wait_ge(S("l2_sum"), head_step(i, j, 2, n + 1))
                    act.activation(nt[:, n, :], psum[:, 4 + n, :], ACT.Ln, bias=eps[:, 0:1]).then_inc(S("l2_ln"), 1)
                for n in range(2):
                    act.wait_ge(S("l2_ln"), head_step(i, j, 2, n + 1))
                    act.activation(nt[:, n, :], nt[:, n, :], ACT.Exp, scale=-0.5).then_inc(S("l2_r"), 1)

            def o_squares(i, j):
                act.wait_ge(S("o_both"), head_step(i, j, 1, 1))
                act.activation(sq[:, 0, :], stg[:, 3, :], ACT.Square).then_inc(S("o_sq"), 1)

            def o_inverse(i, j):
                act.wait_ge(S("o_sum"), head_step(i, j, 1, 1))
                act.activation(lnt[:], psum[:, 7, :], ACT.Ln, scale=1.0 / P, bias=eps[:, 0:1]).then_inc(S("o_ln"), 1)
                act.wait_ge(S("o_ln"), head_step(i, j, 1, 1))
                act.activation(rbc[:], lnt[:], ACT.Exp, scale=-0.5).then_inc(S("o_r"), 1)

            def start(i, j, before, after):
                w = lambda name, per, k: act.wait_ge(S(name), head_step(i, j, per, k))
                for d in range(DIRS):
                    w("e_arg", 2, d + 1)
                    act.activation(E_[:, d], E_[:, d], ACT.Exp).then_inc(S("e_ready"), 1)
                for d in range(DIRS):
                    act.activation(flat(EG[:, d]), psum[:, d, :], ACT.Exp).then_inc(S("eg_ready"), 1)
                for n in range(2):
                    w("kv_turned", 2, n + 1)
                    act.activation(flat(tok[:, n]), psum[:, 6 + n, :], ACT.Copy).then_inc(S("tok_ready"), 1)
                if before:
                    o_squares(i, j - 1)
                    o_inverse(i, j - 1)
                if after:
                    take(i, j + 1, 0)
                for d in range(DIRS):
                    w("m0_turned", 2, d + 1)
                    act.activation(flat(Mi[:, d]), psum[:, 6 + d, :], ACT.Copy).then_inc(S("m_ready"), 1)
                if after:
                    take(i, j + 1, 1)

            def solve(i, j, after):
                w = lambda name, per, k: act.wait_ge(S(name), head_step(i, j, per, k))
                for l in range(LEVELS):
                    if after and l == 1:
                        take(i, j + 1, 2)
                    if after and l == 2:
                        silu(i, j + 1, 0)
                        silu(i, j + 1, 1)
                        squares(i, j + 1)
                    if after and l == 3:
                        take(i, j + 1, 3)
                    if after and l == 4:
                        silu(i, j + 1, 2)
                    if after and l == 5:
                        inverse_lengths(i, j + 1)
                    for d in range(DIRS):
                        w("mt_new", 2 * LEVELS, 2 * l + d + 1)
                        if l < LEVELS - 1:
                            w("m_new", 2 * (LEVELS - 1), 2 * l + d + 1)
                            act.activation(flat(Mi[:, d]), psum[:, d, :], ACT.Copy).then_inc(S("m_ready"), 1)
                        act.activation(flat(MT[:, d]), psum[:, 2 + d, :], ACT.Copy).then_inc(S("mt_ready"), 1)

            def recur(i, j):
                w = lambda name, per, k: act.wait_ge(S(name), head_step(i, j, per, k))
                for n in range(TC):
                    for d in range(DIRS):
                        w("vn_mm", 2 * TC, 2 * n + d + 1)
                        if n:
                            w("s_mm", 2 * TC, 2 * (n - 1) + d + 1)
                            w("o_part", 2 * (TC - 1), 2 * (n - 1) + d + 1)
                        act.activation(vnew[:, d, 1, :], psum[:, 6 + d, P:2 * P], ACT.Copy).then_inc(S("vn_ready"), 1)

            for n in range(4):
                take(0, 0, n)
            for n in range(3):
                silu(0, 0, n)
            squares(0, 0)
            inverse_lengths(0, 0)
            start(0, 0, False, True)
            for i, last in head_passes(act):
                for j in range(2):
                    after = not (last and j == 1)
                    solve(i, j, after)
                    recur(i, j)
                    if after:
                        start(i, j + 1, True, not last)
            o_squares(PASSES - 1, 1)
            o_inverse(PASSES - 1, 1)

        def dve_heads(dve, mine):
            g0 = vec_at["delta_norm_g_2"]
            cb = vec_at["conv_dw_b_2"]
            eyes = eye[:].rearrange("p (a n) -> p a n", a=1).to_broadcast([P, TC, P])

            def banked(b):
                return psum[:, b, :].rearrange("p (t n) -> p t n", t=TC)

            def conv_tap(head, k, before):
                dst = cc[:, bass.ds(head, 1), :]
                src, tap = cp[:, bass.ds(head, 1), k:k + T], conv_w[:, bass.ds(head + 8 * k, 1)]
                if k == 0:
                    return mine.did(dve.tensor_scalar(dst, src, tap, vec[:, bass.ds(head + cb, 1)], ALU.mult, ALU.add))
                mine.wait(before)
                ins_ = dve.scalar_tensor_tensor(out=dst, in0=src, scalar=tap, in1=dst, op0=ALU.mult, op1=ALU.add)
                if k < CONV_K - 1:
                    return mine.did(ins_)
                ins_.then_inc(S("conv_done"), 1)

            def convolve(i, j, taps, before, short=None):
                taps = list(taps)
                if short is not None:
                    head = i * 2 + (j + 1)
                    dve.wait_ge(acc_free, head_acc(i, j + 1, short))
                for k in range(max(len(taps), 0 if short is None else SHORT_K)):
                    if short is not None and k < SHORT_K:
                        tap = short_w[:, bass.ds(head + (k * 24 + short * 8), 1)]
                        src, dst = raw3[:, short, k:k + T], stg[:, short, :]
                        if k == 0:
                            own = mine.did(dve.tensor_scalar(dst, src, tap, None, ALU.mult))
                        else:
                            mine.wait(own)
                            ins_ = dve.scalar_tensor_tensor(out=dst, in0=src, scalar=tap, in1=dst, op0=ALU.mult, op1=ALU.add)
                            if k < SHORT_K - 1:
                                own = mine.did(ins_)
                            else:
                                ins_.then_inc(S("conv3"), 1)
                    if k < len(taps):
                        before = conv_tap(i * 2 + j, taps[k], before)
                if short == 2:
                    dve.wait_ge(S("conv3"), head_step(i, j + 1, 3, 3))
                    dve.sem_inc(S("raw_free"), 1)
                return before

            def start(i, j, before, conv=None):
                w = lambda name, per, k: dve.wait_ge(S(name), head_step(i, j, per, k))
                head = i * 2 + j
                dve.tensor_copy(hc[:].rearrange("p k t d -> p (k t) d"),
                                coef[:].rearrange("p k t (d h) -> p (k t) d h", d=DIRS)[:, :, :, bass.ds(head, 1)]
                                .rearrange("p a d h -> p a (d h)")).then_inc(S("hc_ready"), 1)
                for n in range(2):
                    w("l2_r", 2, n + 1)
                    w("qkv_silu", 3, n + 1)
                    dve.scalar_tensor_tensor(out=stg[:, n, :], in0=stg[:, n, :], scalar=P ** -0.5 if n == 0 else 1.0,
                                             in1=nt[:, n, :], op0=ALU.mult, op1=ALU.mult).then_inc(S("qk_scaled"), 1)
                if before:
                    o_sum_up(i, j - 1)
                w("hc_ready", 1, 1)
                for d in range(DIRS):
                    w("g_bc", 2, d + 1)
                    for t in range(TC):
                        ins_ = dve.tensor_scalar(E_[:, d, t, :], psum[:, d, t * P:(t + 1) * P], hc[:, 2, t, d:d + 1], 0.0,
                                                 ALU.add, ALU.min)
                    ins_.then_inc(S("e_arg"), 1)
                if before:
                    convolve(i, j - 1, range(CONV_TAPS_SOLVE, CONV_K), conv)
                for d in range(DIRS):
                    w("e_ready", 2, d + 1)
                    masked = mine.did(dve.tensor_tensor(E_[:, d], E_[:, d], incl[:, d:d + 1, :].to_broadcast([P, TC, P]), ALU.mult))
                w("kq_ready", 2, 2)
                mine.wait(masked)
                for d in range(DIRS):
                    dve.tensor_tensor(QK[:, d], E_[:, d], banked(4), ALU.mult).then_inc(S("qk_masked"), 1)
                    dve.tensor_tensor(AT[:, d], E_[:, d], banked(5), ALU.mult).then_inc(S("qk_masked"), 1)
                for d in range(DIRS):
                    w("qk_masked", 4, 2 * d + 2)
                    w("b_bc", 2, d + 1)
                    lower = mine.did(dve.tensor_tensor(AT[:, d], AT[:, d], banked(2 + d), ALU.mult))
                for d in range(DIRS):
                    mine.wait(lower)
                    mine.wait(mine.did(dve.tensor_tensor(E_[:, d], AT[:, d], level[:, d, 0:1, :].to_broadcast([P, TC, P]), ALU.mult)))
                    dve.tensor_tensor(MT[:, d], eyes, E_[:, d], ALU.subtract).then_inc(S("mt0_ready"), 1)
                for d in range(DIRS):
                    w("mt0_ready", 2, d + 1)
                    dve.tensor_tensor(E_[:, d], AT[:, d], level[:, d, 1:2, :].to_broadcast([P, TC, P]), ALU.mult)\
                       .then_inc(S("lev_ready"), 1)
                for d in range(DIRS):
                    w("eg_ready", 2, d + 1)
                    q_ = stg[:, 0, :].rearrange("p (t n) -> p t n", t=TC)
                    k_ = stg[:, 1, :].rearrange("p (t n) -> p t n", t=TC)
                    w("qk_scaled", 2, 2)
                    decayed = mine.did(dve.tensor_tensor(KB[:, d], k_, EG[:, d], ALU.mult))
                    decayed_q = mine.did(dve.tensor_tensor(QD[:, d], q_, EG[:, d], ALU.mult))
                    mine.wait(decayed)
                    dve.tensor_tensor(KB[:, d], KB[:, d], banked(2 + d), ALU.mult).then_inc(S("kb_ready"), 1)
                if before:
                    o_gate(i, j - 1)
                w("kb_ready", 2, 2)
                mine.wait(decayed_q)

            def solve(i, j, after):
                w = lambda name, per, k: dve.wait_ge(S(name), head_step(i, j, per, k))
                conv, tap = None, 0
                for l in range(LEVELS):
                    for d in range(DIRS):
                        w("p_ready", 2 * LEVELS, 2 * l + d + 1)
                        dve.tensor_tensor(EG[:, d], eyes, banked(6 + d), ALU.subtract).then_inc(S("q_ready"), 1)
                        if l < LEVELS - 1:
                            dve.tensor_tensor(E_[:, d], AT[:, d], level[:, d, l + 2:l + 3, :].to_broadcast([P, TC, P]),
                                              ALU.mult).then_inc(S("lev_ready"), 1)
                        else:
                            w("lev_ready", 2 * LEVELS, 2 * LEVELS)
                            w("tok_ready", 2, 2)
                            for t in range(TC):
                                ins_ = dve.tensor_scalar(E_[:, d, t, :], tok[:, 0, t, :], hc[:, 3, t, d:d + 1], None, ALU.mult)
                            ins_.then_inc(S("kt_ready"), 1)
                            for t in range(TC):
                                ins_ = dve.tensor_scalar(AT[:, d, t, :], tok[:, 1, t, :], hc[:, 1, t, d:d + 1], None, ALU.mult)
                            ins_.then_inc(S("vb_ready"), 1)
                    taps, short = LEVEL_FILL[l]
                    conv = convolve(i, j, range(tap, tap + taps), conv, short if after else None)
                    tap += taps
                w("vb_ready", 2, 2)
                return conv

            def recur(i, j):
                w = lambda name, per, k: dve.wait_ge(S(name), head_step(i, j, per, k))
                for n in range(TC):
                    if n:
                        for d in range(DIRS):
                            t = chunk_order[d][n]
                            w("r_mm", 2 * (TC - 1), 2 * (n - 1) + d + 1)
                            dve.tensor_tensor(vnew[:, d, 0, :], AT[:, d, t, :], psum[:, 6 + d, 0:P], ALU.subtract)\
                               .then_inc(S("v_ready"), 1)
                    for d in range(DIRS):
                        t = chunk_order[d][n]
                        w("s_mm", 2 * TC, 2 * n + d + 1)
                        if n == 0:
                            ins_ = dve.tensor_copy(St[:, d, :], psum[:, 6 + d, 2 * P:3 * P])
                        else:
                            w("s_ready", 2 * TC, 2 * (n - 1) + d + 1)
                            ins_ = dve.scalar_tensor_tensor(out=St[:, d, :], in0=St[:, d, :], scalar=hc[:, 4, t, d:d + 1],
                                                            in1=psum[:, 6 + d, 2 * P:3 * P], op0=ALU.mult, op1=ALU.add)
                        ins_.then_inc(S("s_ready"), 1)
                w("s_ready", 2 * TC, 2 * TC)

            def o_sum_up(i, j):
                dve.wait_ge(S("o_ready"), head_step(i, j, 2, 2))
                mine.wait(mine.did(dve.tensor_copy(stg[:, 3, :], psum[:, 4, :])))
                dve.tensor_tensor(stg[:, 3, :], stg[:, 3, :], psum[:, 5, :], ALU.add).then_inc(S("o_both"), 1)

            def o_gate(i, j):
                dve.wait_ge(S("o_r"), head_step(i, j, 1, 1))
                mine.wait(mine.did(dve.scalar_tensor_tensor(out=stg[:, 3, :], in0=stg[:, 3, :], scalar=vec[:, g0:g0 + 1],
                                                            in1=rbc[:], op0=ALU.mult, op1=ALU.mult)))
                o_ = of[:, bass.ds(i * 2 + j, 1), :]
                dve.tensor_tensor(o_, stg[:, 3:4, :], o_, ALU.mult).then_inc(S("o_gated"), 1)
                dve.wait_ge(S("o_gated"), head_step(i, j, 1, 1))

            mine.did(dve.memset(raw3[:, :, 0:SHORT_PAD], 0.0))
            mine.did(dve.memset(raw3[:, :, SHORT_PAD + T:], 0.0))
            mine.wait()
            dve.wait_ge(S("coef_exp"), 2)
            dve.wait_ge(S("beta_ready"), 1)
            dve.sem_inc(S("raw_free"), 1)
            for n in range(3):
                convolve(0, -1, (), None, n)
            start(0, 0, False)
            for i, last in head_passes(dve):
                if not last:
                    mine.enter(i, HEAD_STEPS)
                for j in range(2):
                    after = not (last and j == 1)
                    conv = solve(i, j, after)
                    recur(i, j)
                    if after:
                        start(i, j + 1, True, conv)
                if not last:
                    mine.leave(PASSES - 1)
            o_sum_up(PASSES - 1, 1)
            convolve(PASSES - 1, 1, range(CONV_TAPS_SOLVE, CONV_K), conv)
            o_gate(PASSES - 1, 1)

        slopes = alibi_slopes()
        w3 = lambda name: ins[name].rearrange("a h d -> (a h) d") if len(ins[name].shape) == 3 else ins[name]
        block = ctx.enter_context(nc.Block())

        @block.sync
        def _(sp):
            sp.dma_start(eye[:], ins["eye"]).then_inc(S("eye_in"), 16)
            sp.dma_start(xin[:], ins["x"].rearrange("a (c p) d -> p (a c) d", p=P)).then_inc(S("x_in"), 16)
            for name, rows in VECTORS:
                v = ins[name]
                v = v.rearrange("a n -> (a n)") if len(v.shape) == 2 else v
                sp.dma_start(vrows[vec_at[name]:vec_at[name] + rows, :], v.rearrange("(c p) -> c p", p=P))\
                  .then_inc(S("vrows_in"), 16)
            for s in stages:
                w = weight(s.w)
                if s.name == "v":
                    sp.wait_ge(S("x_turned"), 8)
                    sp.wait_ge(S("vec_ready"), 1)
                    sp.dma_start(dist2[:], ins["dist2"]).then_inc(S("attn_in"), 16)
                    sp.dma_start(upper[:], ins["upper"]).then_inc(S("attn_in"), 16)
                    sp.dma_start(wsp[:], ins["w_sgu_spatial"].rearrange("a g t s -> t (a g) s")).then_inc(S("attn_in"), 16)
                    sp.dma_start(brow[:], ins["b_sgu_spatial"].rearrange("a g t -> a (g t)").to_broadcast([P, 4 * P])
                                 .rearrange("p (g t) -> p g t", g=4)).then_inc(S("attn_in"), 16)
                    sp.wait_ge(S("r_ready"), 1)
                    sp.dma_start(grow[:], ins["g_sgu"].to_broadcast([P, 512])).then_inc(S("attn_in"), 16)
                for i in passes(sp, s):
                    for j, (k0, col) in enumerate(s.body):
                        q = first_block[s.name] + j
                        slot = q % RING
                        cols = bass.ds(i * s.cstep + col, s.cols) if s.loops > 1 else slice(col, col + s.cols)
                        sp.wait_ge(lo_ready, count(s, i, j, 1))
                        sp.dma_start(raw[:, slot, :].rearrange("p (c n) -> p c n", c=s.kc),
                                     w[:, k0:k0 + s.kc, cols]).then_inc(raw_loaded[slot], 16)
            if not dump:
                for t in range(TC):
                    sp.wait_ge(S("out_ready"), 4 * (t + 1))
                    sp.dma_start(out.rearrange("a (c p) d -> p (a c) d", p=P)[:, t, :], outt[:, t, :]).then_inc(S("out_done"), 16)
                sp.wait_ge(S("out_done"), 16 * TC)
            if dump:
                sp.wait_ge(S(dump[1]), dump[2])
                sp.dma_start(out, dump[0](dict(X=X, ah=ah, qk=qk, vt=vt))).then_inc(S("out_done"), 16)
                sp.wait_ge(S("out_done"), 16)

        @block.gpsimd
        def _(pool):
            pool.sem_inc(lo_ready, RING)
            whole, rest = divmod(NB, RING)

            def low(b, slot, i):
                pool.wait_ge(hi_ready, b + 1)
                pool.tensor_tensor(wlo[:, slot, :], raw[:, slot, :], whi[:, slot, :].bitcast(F32),
                                   ALU.subtract).then_inc(lo_ready, 1)

            with pool.Fori(0, whole) as i:
                for j in range(RING):
                    low(i * RING + j, j, i)
            for j in range(rest):
                low(whole * RING + j, j, whole)

        @block.tensor
        def _(pe):
            pe.sem_inc(block_used, RING)
            pe.sem_inc(S("sq_free"), 2)
            pe.wait_ge(S("eye_in"), 16)
            pe.wait_ge(S("vrows_in"), 16 * len(VECTORS))
            pe.transpose(psum[:, 5, 0:NVEC], vrows[0:NVEC, :], eye[0:NVEC, 0:NVEC]).then_inc(S("vec_turned"), 1)
            pe.wait_ge(S("x_in"), 16)
            for c in range(DC):
                if c >= 2:
                    pe.wait_ge(S("x_turned"), c - 1)
                for t in range(TC):
                    mm = pe.transpose(psum[:, 6 + c % 2, t * P:(t + 1) * P], xin[:, t, c * P:(c + 1) * P], eye[:])
                mm.then_inc(S("x_tp"), 1)
            pe.wait_ge(S("ones_ready"), 1)
            pe_norm(pe, 0, T)
            pe.wait_ge(S("normed"), 8)
            pe_stage(pe, "qk", ah, al)
            pe_stage(pe, "v", ah, al, cols_of=lambda r: slice(r, T, 4))
            pe_stage(pe, "u", ah, al)
            pe_stage(pe, "vv", ah, al, cols_of=lambda t: slice(t * P, (t + 1) * P))

            pe.wait_ge(S("attn_in"), 16 * 5)
            for g in range(4):
                mm = pe.transpose(psum[:, 4, g * P:(g + 1) * P], wsp[:, g, :], eye[:])
            mm.then_inc(S("wsp_turned"), 1)
            pe.wait_ge(S("wspT_ready"), 1)
            pe.wait_ge(S("vv_normed"), TC)
            for g in range(4):
                if g >= 2:
                    pe.wait_ge(S("sgu_done"), g - 1)
                for n in range(TC):
                    mm = pe.matmul(psum[:, 6 + g % 2, n * P:(n + 1) * P], vv[:, n, g * P:(g + 1) * P], wspT[:, g, :],
                                   start=True, stop=True)
                mm.then_inc(S("mixed"), 1)

            pe.wait_ge(S("sgu_done"), 4)
            pe.wait_ge(acc_free, first_acc["branch_attn"] + ACCS)

            def scores(u):
                h, r = divmod(u, 4)
                if u >= 2:
                    pe.wait_ge(S("scored"), u - 1)
                bank = 4 + 2 * (u % 2)
                at = slice(64 * (h % 2), 64 * (h % 2) + 64)
                for gi in range(3):
                    q, k = qk[at, 2 * gi + h // 2, r::4], qk[at, 6 + 2 * gi + h // 2, :]
                    o = psum[:, bank, :] if gi == 0 else psum[:, bank + 1, (gi - 1) * P:gi * P]
                    mm = pe.matmul(o, q, k if gi == 0 else k[:, r::4], start=True, stop=True)
                mm.then_inc(S("scores"), 1)

            def turn(u):
                pe.wait_ge(S("probs"), u + 1)
                s_ = sc[:, u % 2, :]
                if u >= 1:
                    pe.wait_ge(S("pT_ready"), 2 * u)
                for c in range(4):
                    pe.transpose(psum[:, 0, c * P:(c + 1) * P], s_[:, c:T:4], eye[:])
                for c in range(2):
                    mm = pe.transpose(psum[:, 1, c * P:(c + 1) * P], s_[:, T + c * P:T + (c + 1) * P], eye[:])
                mm.then_inc(S("p_turned"), 1)

            def values(u):
                h, r = divmod(u, 4)
                pe.wait_ge(S("pT_ready"), 2 * u + 2)
                if u >= 2:
                    pe.wait_ge(S("y_ready"), u - 1)
                for c in range(6):
                    gi, tile = (0, c) if c < 4 else (c - 3, r)
                    v0 = (gi * 4 + h) * HD
                    mm = pe.matmul(psum[:, 2 + u % 2, 0:HD], pT[:, c * P:(c + 1) * P], vt[:, tile, v0:v0 + HD],
                                   start=c == 0, stop=c == 5)
                mm.then_inc(S("attended"), 1)

            scores(0)
            scores(1)
            for u in range(16):
                turn(u)
                if u < 14:
                    scores(u + 2)
                values(u)
            pe.wait_ge(S("y_ready"), 16)
            for c in range(2):
                for r in range(4):
                    mm = pe.transpose(psum[:, 4 + c, r * P:(r + 1) * P], ya[:, r, c * P:(c + 1) * P], eye[:])
            mm.then_inc(S("y_turned"), 1)
            pe.wait_ge(S("yT_ready"), 2)
            pe_stage(pe, "branch_attn", yh, yl)
            pe_stage(pe, "gate_attn", ah, al)
            pe_stage(pe, "branch_sgu", yh[:, 2:6, :], yl[:, 2:6, :])
            pe_stage(pe, "gate_sgu", ah, al)
            pe.wait_ge(S("merge_split"), 8)
            pe_stage(pe, "out", ah, al)

            pe.wait_ge(S("mem_in"), 16)
            for c in range(DC):
                if c >= 2:
                    pe.wait_ge(S("mem_turned"), c - 1)
                for t in range(2):
                    mm = pe.transpose(psum[:, 6 + c % 2, t * P:(t + 1) * P], memin[:, t, c * P:(c + 1) * P], eye[:])
                mm.then_inc(S("mem_tp"), 1)
            pe_norm(pe, 1, NM)
            pe.wait_ge(S("normed"), 16)
            pe_stage(pe, "mem_k", mh, ml, NM)
            pe_stage(pe, "mem_v", mh, ml, NM, cols_of=lambda t: slice(t * P, (t + 1) * P))
            pe_norm(pe, 2, T)
            pe.wait_ge(S("normed"), 24)
            pe_stage(pe, "cross_q", ah, al)
            pe.wait_ge(acc_free, first_acc["cross_o"] + ACCS)

            def cscores(u):
                h, t = divmod(u, 4)
                if u >= 2:
                    pe.wait_ge(S("cprobs"), u - 1)
                pe.matmul(psum[:, 4 + u % 2, 0:NM], cq[:, h, t * P:(t + 1) * P], ckT[:, h, :], start=True, stop=True)\
                  .then_inc(S("cscores"), 1)

            def cturn(u):
                h, t = divmod(u, 4)
                pe.wait_ge(S("cnormed"), u + 1)
                if t == 0 and h >= 1:
                    pe.wait_ge(S("cpT_ready"), 2 * h)
                for c in range(2):
                    mm = pe.transpose(psum[:, 6 + c, t * P:(t + 1) * P], cs[:, u % 4, c * P:(c + 1) * P], eye[:])
                mm.then_inc(S("cturned"), 1)

            def cout(h):
                pe.wait_ge(S("cpT_ready"), 2 * h + 2)
                for c in range(2):
                    mm = pe.matmul(psum[:, h, :], cv[:, c, h * P:(h + 1) * P], cpT[:, c, :], start=c == 0, stop=c == 1)
                mm.then_inc(S("cattended"), 1)

            for u in range(18):
                if u < 16:
                    cscores(u)
                if u >= 2:
                    cturn(u - 2)
                    if u % 4 == 1:
                        cout(u // 4 - 1)
            pe.wait_ge(S("co_split"), 4)
            pe_stage(pe, "cross_o", yh, yl)
            pe_norm(pe, 3, T)
            pe.wait_ge(S("normed"), 32)
            pe_stage(pe, "gate_up", ah, al)
            pe.wait_ge(S("hid_split"), FC)
            pe_stage(pe, "down", hh, hl)
            if upto == 1:
                return
            pe_norm(pe, 4, T)
            pe.wait_ge(S("crows_in"), 48)
            for k, rows in enumerate((P, CONV_K * 8 - P, SHORT_K * 24)):
                mm = pe.transpose(psum[:, 5, k * P:k * P + rows], crows[0:rows, k, :], eye[0:rows, 0:rows])
            mm.then_inc(S("crows_turned"), 1)
            pe_norm(pe, 5, T)
            pe.wait_ge(S("normed"), 40)
            pe_stage(pe, "glu", ah, al)
            pe.wait_ge(S("ab_split"), 1)
            for t in range(TC):
                o = psum[:, 5, t * 32:(t + 1) * 32]
                for k in range(DC):
                    tk = slice(t * P, (t + 1) * P)
                    pe.matmul(o, ah[:, k, tk], abh[:, k, :], start=k == 0, stop=False)
                    pe.matmul(o, ah[:, k, tk], abl[:, k, :], start=False, stop=False)
                    mm = pe.matmul(o, al[:, k, tk], abh[:, k, :], start=False, stop=k == DC - 1)
            mm.then_inc(S("ab_ready"), 1)
            pe.wait_ge(S("g_ready"), 1)
            for d in range(DIRS):
                pe.matmul(psum[:, 6, d * 64:(d + 1) * 64], incl[:, d, :], coef[:, 0, :, :].rearrange("p t u -> p (t u)"),
                          start=True, stop=True)
            pe.matmul(psum[:, 6, 128:192], ones[:], coef[:, 0, :, :].rearrange("p t u -> p (t u)"), start=True, stop=True)\
              .then_inc(S("cum_ready"), 1)
            pe_heads(pe)
            pe_stage(pe, "gate_a", ah, al)
            for c in range(DC):
                pe.wait_ge(S("conv_done"), c + 1)
                mm = pe.matmul(psum[:, 4, :], ones[:], cc[:, c, :], start=c == 0, stop=c == DC - 1)
            mm.then_inc(S("conv_sum"), 1)
            pe_stage(pe, "gate_b", ah, al)
            for c in range(DC):
                pe.wait_ge(S("csq_ready"), c + 1)
                pe.matmul(psum[:, 5, :], ones[:], sq[:, c % 2, :], start=c == 0, stop=c == DC - 1).then_inc(S("csq_used"), 1)
            pe.wait_ge(S("of_split"), DC)
            pe_stage(pe, "delta_out", zh, zl)
            pe.wait_ge(S("c_split"), DC)
            pe_stage(pe, "conv_out", ah, al)
            pe.wait_ge(S("y_split"), DC)
            pe_stage(pe, "o2", zh, zl)
            pe_norm(pe, 6, T)
            pe.wait_ge(S("normed"), 48)
            pe_stage(pe, "gate_up2", ah, al)
            pe.wait_ge(S("hid_split"), 2 * FC)
            pe_stage(pe, "down2", hh, hl)
            pe.wait_ge(S("p_in"), 16)
            for c in range(2):
                for t in range(TC):
                    mm = pe.transpose(psum[:, 6 + c, t * P:(t + 1) * P], pin[:, t, c * P:(c + 1) * P], eye[:])
                mm.then_inc(S("pp_turned"), 1)
            pe.wait_ge(S("pp_split"), 2)
            pe_stage(pe, "pl_proj", ph, pl)
            pe_norm(pe, 7, T)
            pe_norm(pe, 8, T)
            pe.wait_ge(S("normed"), 56)
            pe_stage(pe, "pl_gate", ah, al)
            pe_norm(pe, 9, T)
            for t in range(TC):
                for half in range(2):
                    n = 2 * t + half
                    if t == 0 and half == 0:
                        pe.wait_ge(S("n_ready"), 80)
                    if n >= 2:
                        pe.wait_ge(S("out_ready"), 2 * (n - 1))
                    for c in range(4):
                        mm = pe.transpose(psum[:, 6 + n % 2, c * P:(c + 1) * P], X[:, 4 * half + c, t * P:(t + 1) * P], eye[:])
                    mm.then_inc(S("o_turned"), 1)

        @block.scalar
        def _(act):
            mine = Steps(act, S("act_own"))
            act.sem_inc(acc_free, ACCS)
            for b in range(LEAD):
                act_round(act, b, b, 0)
            act_norm(act, mine, 0, X, T, lambda c: act.wait_ge(S("x_turned"), c + 1), (ah, al))
            act_stage(act, "qk", lambda i, g, m, a, bank: act.activation(
                qk[:, bass.ds(i * 4 + g, 1), :], psum[:, bank:bank + 1, :], ACT.Copy))
            act_stage(act, "v", lambda i, g, m, a, bank: act.activation(
                vt[:, :, g * P:(g + 1) * P], psum[:, bank, :].rearrange("p (r n) -> p r n", r=4), ACT.Copy))
            act_stage(act, "u", lambda i, g, m, a, bank: act.activation(
                uu[:, g, :], psum[:, bank, :], ACT.Gelu_apprx_tanh))
            act_stage(act, "vv", lambda i, g, m, a, bank: act.activation(
                vv[:, :, g * P:(g + 1) * P], psum[:, bank, :].rearrange("p (t n) -> p t n", t=4), ACT.Gelu_apprx_tanh))
            act.wait_ge(acc_free, first_acc["branch_attn"] + ACCS)
            for t in range(TC):
                if t:
                    act.wait_ge(S("ss_ready"), t)
                act.activation(sq[:, 0, :], vv[:, t, :], ACT.Square, accum_out=ss[:, t:t + 1]).then_inc(S("ss_ready"), 1)
            act.wait_ge(S("ss_ready"), TC)
            mine.did(act.activation(ss[:, 8:12], ss[:, 0:4], ACT.Ln, scale=1.0 / 512, bias=eps[:, 0:1]))
            mine.wait()
            act.activation(rs[:, 0:4], ss[:, 8:12], ACT.Exp, scale=-0.5).then_inc(S("rs_ready"), 1)
            for g in range(4):
                act.wait_ge(S("sgu_done"), g + 1)
                act.activation(yh[:, 2 + g, :], nt[:, g % 2, :], ACT.Copy).then_inc(S("sgu_hi"), 1)
            act.wait_ge(S("mixed"), 4)
            act.dma_start(dist[:], ins["dist"]).then_inc(S("dist_in"), 16)

            def soft(u):
                act.wait_ge(S("scored"), u + 1)
                act.activation(sc[:, u % 2, :], sc[:, u % 2, :], ACT.Exp, scale=HD ** -0.5, bias=nmx[:, u:u + 1],
                               accum_out=den[:, u:u + 1]).then_inc(S("probs"), 1)

            def pT_copy(u):
                act.wait_ge(S("p_turned"), u + 1)
                if u:
                    act.wait_ge(S("attended"), u)
                act.activation(pT[:, 0:T], psum[:, 0, :], ACT.Copy).then_inc(S("pT_ready"), 1)
                act.activation(pT[:, T:768], psum[:, 1, 0:256], ACT.Copy).then_inc(S("pT_ready"), 1)

            soft(0)
            soft(1)
            for u in range(16):
                pT_copy(u)
                if u < 14:
                    soft(u + 2)
            act.wait_ge(S("y_turned"), 1)
            for c in range(2):
                act.activation(yh[:, c, :].rearrange("p (j r) -> p r j", r=4),
                               psum[:, 4 + c, :].rearrange("p (r j) -> p r j", r=4), ACT.Copy).then_inc(S("y_hi"), 1)

            act.wait_ge(S("y_ready"), 16)
            act.wait_ge(S("yT_ready"), 2)
            act_stage(act, "branch_attn", lambda i, g, m, a, bank: act.activation(
                m1[:, 4 * g + m, :], psum[:, bank, :], ACT.Copy))

            def stage_out(name, staged0, func, bias_of=None):
                s = by_name[name]
                a0 = first_acc[name]

                def empty(i, g, m, a, bank):
                    per = len(s.body) // s.kblocks * s.width
                    act.wait_ge(stage_used, i * per + (staged0 + a - a0 + 1))
                    kw = {} if bias_of is None else {"bias": bias_of(i, a - a0)}
                    return act.activation(stg[:, (staged0 + a - a0) % 4, :], psum[:, bank, :], func, **kw)

                act_stage(act, name, empty)

            bg = vec_at["b_gate"]
            stage_out("gate_attn", 0, ACT.Sigmoid, lambda i, k: vec[:, bass.ds(i * 4 + (bg + k), 1)])
            act_stage(act, "branch_sgu", lambda i, g, m, a, bank: act.activation(
                m2[:, 2 * g + m, :], psum[:, bank, :], ACT.Copy))
            stage_out("gate_sgu", 8, ACT.Sigmoid, lambda i, k: vec[:, bass.ds(i * 4 + (bg + 8 + k), 1)])
            act_split(act, "merged", 8, m1, ah, "merge_hi", 8)
            act.wait_ge(S("merge_split"), 8)
            act.dma_start(memin[:], ins["mem"].rearrange("a (c p) d -> p (a c) d", p=P)).then_inc(S("mem_in"), 16)
            stage_out("out", 16, ACT.Copy)
            act_norm(act, mine, 1, memT, NM, lambda c: act.wait_ge(S("mem_turned"), c + 1), (mh, ml))
            act_stage(act, "mem_k", lambda i, g, m, a, bank: act.activation(
                ckT[:, g, :], psum[:, bank, 0:NM], ACT.Copy))
            act_stage(act, "mem_v", lambda i, g, m, a, bank: act.activation(
                cv[:, :, g * P:(g + 1) * P], psum[:, bank, 0:NM].rearrange("p (t n) -> p t n", t=2), ACT.Copy))
            act_norm(act, mine, 2, X, T, lambda c: act.wait_ge(stage_used, 4 + 16 + c + 1), (ah, al))
            act_stage(act, "cross_q", lambda i, g, m, a, bank: act.activation(
                cq[:, g, :], psum[:, bank, :], ACT.Copy))

            def csoft(u):
                act.wait_ge(S("cmaxed"), u + 1)
                if u >= 4:
                    act.wait_ge(S("cturned"), u - 3)
                act.activation(cs[:, u % 4, :], psum[:, 4 + u % 2, 0:NM], ACT.Exp, scale=P ** -0.5,
                               bias=cmx[:, u:u + 1], accum_out=cden[:, u:u + 1]).then_inc(S("cprobs"), 1)

            def cpT_copy(h):
                act.wait_ge(S("cturned"), 4 * h + 4)
                if h:
                    act.wait_ge(S("cattended"), h)
                for c in range(2):
                    act.activation(cpT[:, c, :], psum[:, 6 + c, :], ACT.Copy).then_inc(S("cpT_ready"), 1)

            def co_hi(h):
                act.wait_ge(S("cattended"), h + 1)
                act.activation(yh[:, h, :], psum[:, h, :], ACT.Copy).then_inc(S("co_hi"), 1)

            for u in range(16):
                csoft(u)
                if u % 4 == 0 and u > 0:
                    cpT_copy(u // 4 - 1)
                if u % 4 == 2 and u > 4:
                    co_hi(u // 4 - 1)
            cpT_copy(3)
            co_hi(3)
            stage_out("cross_o", 24, ACT.Copy)
            act_norm(act, mine, 3, X, T, lambda c: act.wait_ge(stage_used, 4 + 24 + c + 1), (ah, al))

            def swiglu(name, staged, hid0):
                s = by_name[name]
                a0 = first_acc[name]
                act.wait_ge(stage_used, 4 + staged)

                def empty(i, g, m, a, bank):
                    act.wait_ge(S("hid"), i * 2 + (hid0 + g // 2 + 1))
                    return act.activation(stg[:, g, :], psum[:, bank, :], ACT.Silu if g % 2 == 0 else ACT.Copy)

                for i in passes(act, s):
                    for j in range(4):
                        q = first_block[name] + j + LEAD
                        act_round(act, count(s, i, j, LEAD), q, i)
                        act.wait_ge(block_used, count(s, i, j, RING + 1))
                        empty(i, j, 0, a0 + j, (a0 + j) % ACCS).then_inc(acc_free, 1)
                        if j % 2 == 1:
                            act.wait_ge(S("hid"), i * 2 + (hid0 + j // 2 + 3))
                            act.activation(hh[:, bass.ds(i * 2 + j // 2, 1), :], nt[:, j // 2:j // 2 + 1, :], ACT.Copy)\
                               .then_inc(S("hid_hi"), 1)

            swiglu("gate_up", 32, 0)
            stage_out("down", 32, ACT.Copy)
            if upto == 1:
                return
            act_norm(act, mine, 4, X, T, lambda c: act.wait_ge(stage_used, 4 + 32 + c + 1))
            act.dma_start(level[:], ins["level"]).then_inc(S("masks_in"), 16)
            act.dma_start(incl[:], ins["incl"]).then_inc(S("masks_in"), 16)
            cw = ins["conv_dw_w_2"].rearrange("a k (c p) -> (a k c) p", p=P)
            act.dma_start(crows[:, 0, :], cw[0:P, :]).then_inc(S("crows_in"), 16)
            act.dma_start(crows[0:CONV_K * 8 - P, 1, :], cw[P:CONV_K * 8, :]).then_inc(S("crows_in"), 16)
            act.dma_start(crows[0:SHORT_K * 24, 2, :], ins["qkv_conv_w_2"].rearrange("a k (c p) -> (a k c) p", p=P))\
               .then_inc(S("crows_in"), 16)
            act.dma_start(abw[:], ins["w_in_2"].rearrange("a (c p) n -> p (a c) n", p=P)[:, :, 6 * D:6 * D + 32])\
               .then_inc(S("ab_in"), 16)
            act.dma_start(arow[:, 0, :], ins["a_log_2"].rearrange("a d h -> a (d h)").to_broadcast([P, 16])).then_inc(S("arow_in"), 16)
            act.dma_start(arow[:, 1, :], ins["dt_bias_2"].rearrange("a d h -> a (d h)").to_broadcast([P, 16])).then_inc(S("arow_in"), 16)
            act.wait_ge(S("n_ready"), 40)
            act.dma_start(spill, X[:]).then_inc(S("spilled"), 16)
            act_norm(act, mine, 5, X, T, lambda c: None, (ah, al))
            act.wait_ge(S("ab_in"), 16)
            act.activation(abh[:], abw[:], ACT.Copy).then_inc(S("ab_hi"), 1)

            def glu_empty(i, g, m, a, bank):
                act.wait_ge(S("glu_done"), i * 2 + (g // 2 + 1))
                return act.activation(stg[:, g % 4, :], psum[:, bank, :], ACT.Sigmoid if g % 2 else ACT.Copy)

            act.wait_ge(stage_used, 4 + 40)
            act_stage(act, "glu", glu_empty)
            act.wait_ge(S("arow_in"), 32)
            act.activation(arow[:, 0, :], arow[:, 0, :], ACT.Exp).then_inc(S("alog_exp"), 1)
            act.wait_ge(S("ab_sum"), 1)
            act.activation(tmp[:, 1], tmp[:, 0], ACT.Abs).then_inc(S("ab_abs"), 1)
            act.wait_ge(S("ab_abs"), 1)
            act.activation(tmp[:, 2], tmp[:, 1], ACT.Exp, scale=-1.0).then_inc(S("ab_abs"), 1)
            act.wait_ge(S("ab_abs"), 2)
            act.activation(tmp[:, 1], tmp[:, 2], ACT.Ln, bias=1.0).then_inc(S("ab_abs"), 1)
            act.activation(coef[:, 1], ab[:, :, 16:32], ACT.Sigmoid).then_inc(S("beta_ready"), 1)
            act.wait_ge(S("tail_arg"), 1)
            act.activation(coef[:, 3], coef[:, 3], ACT.Exp).then_inc(S("coef_exp"), 1)
            act.activation(coef[:, 4], coef[:, 4], ACT.Exp).then_inc(S("coef_exp"), 1)
            act_heads(act)
            for c in range(DC):
                act.wait_ge(S("o_gated"), HEADS)
                act.wait_ge(S("conv_done"), DC)
                act.activation(zh[:, c, :], of[:, c, :], ACT.Copy).then_inc(S("of_hi"), 1)
            for name, dst in (("gate_a", ga), ("gate_b", gb)):
                act_stage(act, name, lambda i, g, m, a, bank, dst=dst: act.activation(
                    dst[:, bass.ds(i * 4 + g, 1), :], psum[:, bank:bank + 1, :], ACT.Sigmoid))
            for c in range(DC):
                act.wait_ge(S("centred"), c + 1)
                if c >= 2:
                    act.wait_ge(S("csq_used"), c - 1)
                act.activation(sq[:, c % 2, :], cc[:, c, :], ACT.Square).then_inc(S("csq_ready"), 1)
            act.wait_ge(S("csq_used"), DC)
            mine.did(act.activation(lnt[:], psum[:, 5, :], ACT.Ln, scale=1.0 / D, bias=eps[:, 1:2]))
            mine.wait()
            act.activation(rbc[:], lnt[:], ACT.Exp, scale=-0.5).then_inc(S("c_r"), 1)
            lb = vec_at["conv_ln_b_2"]
            for c in range(DC):
                act.wait_ge(S("c_scaled"), c + 1)
                mine.did(act.activation(cc[:, c, :], cc[:, c, :], ACT.Silu, bias=vec[:, lb + c:lb + c + 1]))
                mine.wait()
                act.activation(ah[:, c, :], cc[:, c, :], ACT.Copy).then_inc(S("c_hi"), 1)
            stage_out("delta_out", 40, ACT.Copy)
            stage_out("conv_out", 48, ACT.Copy)
            act.wait_ge(S("y_sum"), DC)
            act.dma_start(X[:], spill).then_inc(S("x_back"), 16)
            act_split(act, "y_sum", 0, gb, zh, "y_hi2", DC)
            stage_out("o2", 56, ACT.Copy)
            act_norm(act, mine, 6, X, T, lambda c: act.wait_ge(stage_used, 4 + 56 + c + 1), (ah, al))
            swiglu("gate_up2", 64, FC)
            stage_out("down2", 64, ACT.Copy)
            act.wait_ge(block_used, RING + first_block["pl_proj"])
            act.dma_start(pin[:], ins["p_2"].rearrange("a b (c p) d -> p (a b c) d", p=P)).then_inc(S("p_in"), 16)
            for c in range(2):
                act.wait_ge(S("pp_turned"), c + 1)
                act.activation(ph[:, c, :], psum[:, 6 + c, :], ACT.Copy).then_inc(S("pp_hi"), 1)
            act_stage(act, "pl_proj", lambda i, g, m, a, bank: act.activation(
                PL[:, 4 * g + m, :], psum[:, bank, :], ACT.Copy))
            act_norm(act, mine, 7, PL, T, lambda c: act.wait_ge(acc_free, ACCS + first_acc["pl_proj"] + 8))
            act_norm(act, mine, 8, X, T, lambda c: act.wait_ge(stage_used, 4 + 72), (ah, al))
            stage_out("pl_gate", 72, ACT.Sigmoid)
            act_norm(act, mine, 9, X, T, lambda c: act.wait_ge(S("x_final"), c + 1))

        @block.vector
        def _(dve):
            mine = Steps(dve, S("dve_own"))
            mine.did(dve.memset(ones[:], 1.0))
            mine.did(dve.memset(eps[:, 0:1], EPS))
            mine.did(dve.memset(eps[:, 1:2], LN_EPS))
            mine.wait()
            dve.wait_ge(S("vec_turned"), 1)
            dve.tensor_copy(vec[:], psum[:, 5, 0:NVEC]).then_inc(S("vec_ready"), 1)
            dve.sem_inc(S("ones_ready"), 1)
            dve.sem_inc(stage_used, 4)
            dve.sem_inc(S("hid"), 2)
            dve.sem_inc(S("glu_done"), 2)
            for c in range(DC):
                dve.wait_ge(S("x_tp"), c + 1)
                dve.tensor_copy(X[:, c, :], psum[:, 6 + c % 2, :]).then_inc(S("x_turned"), 1)
            dve.wait_ge(S("vec_ready"), 1)
            dve_norm(dve, 0, 0, X, "g_mix", T, (ah, al))

            dve.wait_ge(S("attn_in"), 16 * 5)
            dve.wait_ge(S("wsp_turned"), 1)
            for g in range(4):
                ins_ = dve.tensor_tensor(wspT[:, g, :], psum[:, 4, g * P:(g + 1) * P], upper[:], ALU.mult)
            ins_.then_inc(S("wspT_ready"), 1)
            dve.wait_ge(S("rs_ready"), 1)
            for t in range(TC):
                dve.scalar_tensor_tensor(out=vv[:, t, :], in0=vv[:, t, :], scalar=rs[:, t:t + 1], in1=grow[:],
                                         op0=ALU.mult, op1=ALU.mult).then_inc(S("vv_normed"), 1)
            for g in range(4):
                dve.wait_ge(S("mixed"), g + 1)
                if g >= 2:
                    dve.wait_ge(S("sgu_lo"), g - 1)
                b_ = brow[:, g:g + 1, :].to_broadcast([P, TC, P])
                n_ = nt[:, g % 2, :].rearrange("p (t s) -> p t s", t=TC)
                mine.did(dve.tensor_tensor(n_, psum[:, 6 + g % 2, :].rearrange("p (t s) -> p t s", t=TC), b_, ALU.add))
                mine.wait()
                dve.tensor_tensor(nt[:, g % 2, :], nt[:, g % 2, :], uu[:, g, :], ALU.mult).then_inc(S("sgu_done"), 1)
                dve.wait_ge(S("sgu_hi"), g + 1)
                dve.tensor_tensor(yl[:, 2 + g, :], nt[:, g % 2, :], yh[:, 2 + g, :].bitcast(F32), ALU.subtract)\
                   .then_inc(S("sgu_lo"), 1)

            def score(u):
                h, r = divmod(u, 4)
                bank = 4 + 2 * (u % 2)
                dve.wait_ge(S("scores"), u + 1)
                if u >= 2:
                    dve.wait_ge(S("p_turned"), u - 1)
                for gi in range(3):
                    k = -float(slopes[gi, h]) * HD ** 0.5
                    d_ = dist[:, r, :] if gi == 0 else dist2[:, gi - 1, :]
                    src = psum[:, bank, :] if gi == 0 else psum[:, bank + 1, (gi - 1) * P:gi * P]
                    dst = sc[:, u % 2, 0:T] if gi == 0 else sc[:, u % 2, T + (gi - 1) * P:T + gi * P]
                    mine.did(dve.scalar_tensor_tensor(out=dst, in0=d_, scalar=k, in1=src, op0=ALU.mult, op1=ALU.add))
                mine.wait()
                mine.did(dve.tensor_reduce(mx[:, u:u + 1], sc[:, u % 2, :], AX_X, ALU.max))
                mine.wait()
                dve.tensor_scalar(nmx[:, u:u + 1], mx[:, u:u + 1], -(HD ** -0.5), None, ALU.mult).then_inc(S("scored"), 1)

            def attend(u):
                h, r = divmod(u, 4)
                dve.wait_ge(S("probs"), u + 1)
                mine.did(dve.reciprocal(rden[:, u:u + 1], den[:, u:u + 1]))
                mine.wait()
                dve.wait_ge(S("attended"), u + 1)
                dve.tensor_scalar(ya[:, r, h * HD:(h + 1) * HD], psum[:, 2 + u % 2, 0:HD], rden[:, u:u + 1], None,
                                  ALU.mult).then_inc(S("y_ready"), 1)

            dve.wait_ge(S("dist_in"), 16)
            score(0)
            score(1)
            for u in range(16):
                if u < 14:
                    score(u + 2)
                attend(u)
            for c in range(2):
                dve.wait_ge(S("y_hi"), c + 1)
                dve.tensor_tensor(yl[:, c, :].rearrange("p (j r) -> p r j", r=4),
                                  psum[:, 4 + c, :].rearrange("p (r j) -> p r j", r=4),
                                  yh[:, c, :].rearrange("p (j r) -> p r j", r=4).bitcast(F32), ALU.subtract)\
                   .then_inc(S("yT_ready"), 1)

            def per_stage(name, fn):
                s = by_name[name]
                per = len(s.body) // s.kblocks * s.width
                for i in passes(dve, s):
                    for k in range(per):
                        dve.wait_ge(acc_free, i * per + (first_acc[name] + k + 1 + ACCS))
                        fn(i, k, per)

            def gate1(i, k, per):
                c = bass.ds(i * per + k, 1)
                dve.tensor_tensor(m1[:, c, :], stg[:, k:k + 1, :], m1[:, c, :], ALU.mult).then_inc(stage_used, 1)

            def gate2(i, k, per):
                c = bass.ds(i * per + k, 1)
                dve.tensor_tensor(m2[:, c, :], stg[:, k:k + 1, :], m2[:, c, :], ALU.mult).then_inc(stage_used, 1)
                dve.wait_ge(stage_used, i * per + (4 + 8 + k + 1))
                dve.tensor_tensor(m1[:, c, :], m1[:, c, :], m2[:, c, :], ALU.add).then_inc(S("merged"), 1)

            per_stage("gate_attn", gate1)
            dve.sem_inc(S("merged"), 8)
            per_stage("gate_sgu", gate2)
            for c in range(8):
                dve.wait_ge(S("merge_hi"), c + 1)
                dve.tensor_tensor(al[:, c, :], m1[:, c, :], ah[:, c, :].bitcast(F32), ALU.subtract)\
                   .then_inc(S("merge_split"), 1)

            def residual(name, staged0):
                def add(i, k, per):
                    c = bass.ds(i * per + k, 1) if per < 8 else slice(k, k + 1)
                    sl = (staged0 + k) % 4
                    dve.tensor_tensor(X[:, c, :], X[:, c, :], stg[:, sl:sl + 1, :], ALU.add).then_inc(stage_used, 1)
                per_stage(name, add)

            residual("out", 16)
            for c in range(DC):
                dve.wait_ge(S("mem_tp"), c + 1)
                dve.tensor_copy(memT[:, c, :], psum[:, 6 + c % 2, 0:NM]).then_inc(S("mem_turned"), 1)
            dve_norm(dve, 1, 1, memT, "g_mem", NM, (mh, ml))
            dve_norm(dve, 2, 2, X, "g_cross", T, (ah, al))

            def cmaxes(u):
                dve.wait_ge(S("cscores"), u + 1)
                mine.did(dve.tensor_reduce(crd[:, u:u + 1], psum[:, 4 + u % 2, 0:NM], AX_X, ALU.max))
                mine.wait()
                dve.tensor_scalar(cmx[:, u:u + 1], crd[:, u:u + 1], -(P ** -0.5), None, ALU.mult).then_inc(S("cmaxed"), 1)

            def cnorm(u):
                dve.wait_ge(S("cprobs"), u + 1)
                mine.did(dve.reciprocal(crd[:, u:u + 1], cden[:, u:u + 1]))
                mine.wait()
                dve.tensor_scalar(cs[:, u % 4, :], cs[:, u % 4, :], crd[:, u:u + 1], None, ALU.mult)\
                   .then_inc(S("cnormed"), 1)

            def co_lo(h):
                dve.wait_ge(S("co_hi"), h + 1)
                dve.tensor_tensor(yl[:, h, :], psum[:, h, :], yh[:, h, :].bitcast(F32), ALU.subtract)\
                   .then_inc(S("co_split"), 1)

            cmaxes(0)
            for u in range(16):
                if u < 15:
                    cmaxes(u + 1)
                cnorm(u)
            for h in range(4):
                co_lo(h)
            residual("cross_o", 24)
            dve_norm(dve, 3, 3, X, "g_ffn", T, (ah, al))

            def swiglu(name, staged, hid0):
                s = by_name[name]
                for i in passes(dve, s):
                    for k in range(2):
                        dve.wait_ge(acc_free, i * 4 + (first_acc[name] + 2 * k + 2 + ACCS))
                        dve.tensor_tensor(nt[:, k, :], stg[:, 2 * k, :], stg[:, 2 * k + 1, :], ALU.mult).then_inc(S("hid"), 1)
                        dve.wait_ge(S("hid_hi"), i * 2 + (hid0 + k + 1))
                        dve.tensor_tensor(hl[:, bass.ds(i * 2 + k, 1), :], nt[:, k:k + 1, :],
                                          hh[:, bass.ds(i * 2 + k, 1), :].bitcast(F32), ALU.subtract)\
                           .then_inc(S("hid_split"), 1)

            swiglu("gate_up", 32, 0)
            residual("down", 32)
            if upto == 1:
                return
            dve_norm(dve, 4, 0, X, "g_final", T)
            dve.wait_ge(S("crows_turned"), 1)
            dve.tensor_copy(conv_w[:], psum[:, 5, 0:CONV_K * 8])
            dve.tensor_copy(short_w[:], psum[:, 5, 2 * P:2 * P + SHORT_K * 24]).then_inc(S("taps_ready"), 1)
            dve_norm(dve, 5, 4, X, "g_mix_2", T, (ah, al))
            dve.wait_ge(S("ab_hi"), 1)
            dve.tensor_tensor(abl[:], abw[:], abh[:].bitcast(F32), ALU.subtract).then_inc(S("ab_split"), 1)
            mine.did(dve.memset(cp[:, :, 0:CONV_PAD], 0.0))
            mine.did(dve.memset(cp[:, :, CONV_PAD + T:], 0.0))

            s = by_name["glu"]
            for i in passes(dve, s):
                for k in range(2):
                    dve.wait_ge(acc_free, i * 4 + (first_acc["glu"] + 2 * k + 2 + ACCS))
                    dve.tensor_tensor(cp[:, bass.ds(i * 2 + k, 1), CONV_PAD:CONV_PAD + T], stg[:, 2 * k:2 * k + 1, :],
                                      stg[:, 2 * k + 1:2 * k + 2, :], ALU.mult).then_inc(S("glu_done"), 1)
            dve.wait_ge(S("taps_ready"), 1)
            dve.wait_ge(S("spilled"), 16)
            mine.wait()
            dve.wait_ge(S("glu_done"), 2 + 8)
            dve.wait_ge(S("ab_ready"), 1)
            mine.did(dve.tensor_copy(ab[:], psum[:, 5, 0:128].rearrange("p (t u) -> p t u", t=TC)))
            mine.wait()
            dtb = arow[:, 1:2, :].to_broadcast([P, TC, 16])
            dve.wait_ge(S("arow_in"), 32)
            dve.tensor_tensor(tmp[:, 0], ab[:, :, 0:16], dtb, ALU.add).then_inc(S("ab_sum"), 1)
            dve.wait_ge(S("ab_abs"), 3)
            mine.did(dve.scalar_tensor_tensor(out=tmp[:, 2], in0=tmp[:, 0], scalar=0.0, in1=tmp[:, 1], op0=ALU.max, op1=ALU.add))
            mine.wait()
            dve.wait_ge(S("alog_exp"), 1)
            dve.scalar_tensor_tensor(out=coef[:, 0], in0=tmp[:, 2], scalar=-1.0, in1=arow[:, 0:1, :].to_broadcast([P, TC, 16]),
                                     op0=ALU.mult, op1=ALU.mult).then_inc(S("g_ready"), 1)
            dve.wait_ge(S("masks_in"), 32)
            dve.wait_ge(S("cum_ready"), 1)
            cum = [psum[:, 6, d * 64:(d + 1) * 64].rearrange("p (t u) -> p t u", t=TC) for d in range(3)]
            for d in range(DIRS):
                u = slice(8 * d, 8 * d + 8)
                mine.did(dve.tensor_scalar(coef[:, 2, :, u], cum[d][:, :, u], -1.0, None, ALU.mult))
            mine.wait()
            mine.did(dve.tensor_tensor(coef[:, 3], cum[2], coef[:, 2], ALU.add))
            mine.did(dve.tensor_copy(coef[:, 4], cum[2]))
            mine.wait()
            dve.tensor_scalar(coef[:, 3], coef[:, 3], 0.0, None, ALU.min).then_inc(S("tail_arg"), 1)

            dve_heads(dve, mine)
            for c in range(8):
                dve.wait_ge(S("of_hi"), c + 1)
                dve.tensor_tensor(zl[:, c, :], of[:, c, :], zh[:, c, :].bitcast(F32), ALU.subtract).then_inc(S("of_split"), 1)
            dve.wait_ge(S("conv_sum"), 1)
            mine.did(dve.tensor_scalar(mu, psum[:, 4, :], 1.0 / D, None, ALU.mult))
            mine.wait()
            for c in range(DC):
                dve.tensor_tensor(cc[:, c, :], cc[:, c, :], mu, ALU.subtract).then_inc(S("centred"), 1)
            dve.wait_ge(S("c_r"), 1)
            lg = vec_at["conv_ln_g_2"]
            for c in range(DC):
                dve.scalar_tensor_tensor(out=cc[:, c, :], in0=cc[:, c, :], scalar=vec[:, lg + c:lg + c + 1], in1=rbc[:],
                                         op0=ALU.mult, op1=ALU.mult).then_inc(S("c_scaled"), 1)
            for c in range(DC):
                dve.wait_ge(S("c_hi"), c + 1)
                dve.tensor_tensor(al[:, c, :], cc[:, c, :], ah[:, c, :].bitcast(F32), ALU.subtract).then_inc(S("c_split"), 1)

            def gate_delta(i, k, per):
                c = bass.ds(i * per + k, 1)
                dve.tensor_tensor(gb[:, c, :], stg[:, k:k + 1, :], gb[:, c, :], ALU.mult).then_inc(stage_used, 1)

            def gate_conv(i, k, per):
                c = bass.ds(i * per + k, 1)
                dve.tensor_tensor(ga[:, c, :], stg[:, k:k + 1, :], ga[:, c, :], ALU.mult).then_inc(stage_used, 1)
                dve.wait_ge(stage_used, i * per + (4 + 48 + k + 1))
                dve.tensor_tensor(gb[:, c, :], gb[:, c, :], ga[:, c, :], ALU.add).then_inc(S("y_sum"), 1)

            per_stage("delta_out", gate_delta)
            per_stage("conv_out", gate_conv)
            for c in range(8):
                dve.wait_ge(S("y_hi2"), c + 1)
                dve.tensor_tensor(zl[:, c, :], gb[:, c, :], zh[:, c, :].bitcast(F32), ALU.subtract).then_inc(S("y_split"), 1)
            dve.wait_ge(S("x_back"), 16)
            residual("o2", 56)
            dve_norm(dve, 6, 5, X, "g_ffn_2", T, (ah, al))
            swiglu("gate_up2", 64, FC)
            residual("down2", 64)
            for c in range(2):
                dve.wait_ge(S("pp_hi"), c + 1)
                dve.tensor_tensor(pl[:, c, :], psum[:, 6 + c, :], ph[:, c, :].bitcast(F32), ALU.subtract)\
                   .then_inc(S("pp_split"), 1)
            dve_norm(dve, 7, 0, PL, "g_pl_proj_2", T)
            dve_norm(dve, 8, 6, X, "g_pl_2", T, (ah, al))

            def gate_pl(i, k, per):
                c = i * per + k
                dve.tensor_tensor(PL[:, c, :], stg[:, k, :], PL[:, c, :], ALU.mult).then_inc(stage_used, 1)
                dve.wait_ge(stage_used, 4 + 72 + c + 1)
                dve.tensor_tensor(X[:, c, :], X[:, c, :], PL[:, c, :], ALU.add).then_inc(S("x_final"), 1)

            per_stage("pl_gate", gate_pl)
            dve.wait_ge(S("x_final"), 8)
            dve_norm(dve, 9, 0, X, "g_final_2", T)
            for n in range(8):
                t, half = divmod(n, 2)
                dve.wait_ge(S("o_turned"), n + 1)
                for q in range(2):
                    dve.tensor_copy(outt[:, t, half * 512 + q * 256:half * 512 + (q + 1) * 256],
                                    psum[:, 6 + n % 2, q * 256:(q + 1) * 256]).then_inc(S("out_ready"), 1)



_INS = ["x", "mem", "g_mix", "w_in", "b_gate", "w_sgu_spatial", "b_sgu_spatial", "g_sgu", "w_branch_attn",
        "w_branch_sgu", "w_out", "g_cross", "g_mem", "w_q_cross", "w_kv_cross", "w_o_cross", "g_ffn", "w_gate_up",
        "w_down", "g_final", "p_2", "g_mix_2", "w_in_2", "conv_dw_w_2", "conv_dw_b_2", "conv_ln_g_2", "conv_ln_b_2",
        "w_conv_out_2", "qkv_conv_w_2", "a_log_2", "dt_bias_2", "delta_norm_g_2", "w_delta_out_2", "w_o_2",
        "g_ffn_2", "w_gate_up_2", "w_down_2", "g_pl_2", "w_pl_gate_2", "w_pl_proj_2", "g_pl_proj_2", "g_final_2"]


def kernel(**inputs):
    import concourse.bacc as bacc
    from concourse.bass_utils import run_bass_kernel_spmd

    nc = bacc.Bacc("TRN2", target_bir_lowering=False, num_devices=1)
    arrays, aps = {}, {}
    for name, a in [(n, inputs[n]) for n in _INS] + list(shape_constants().items()):
        a = np.ascontiguousarray(a)
        arrays[f"in_{name}"] = a
        aps[name] = nc.dram_tensor(f"in_{name}", a.shape, mybir.dt.from_np(a.dtype), kind="ExternalInput").ap()
    out = nc.dram_tensor("out_0", (1, T, D), F32, kind="ExternalOutput").ap()
    build(nc, aps, out)
    r = run_bass_kernel_spmd(nc, [arrays], core_ids=[0])
    return r.results[0]["out_0"]
```

```python
from contextlib import ExitStack

import numpy as np

import concourse.bass as bass
from concourse import mybir

F32 = mybir.dt.float32
F32R = mybir.dt.float32r
ALU = mybir.AluOpType
ACT = mybir.ActivationFunctionType
AX_X = mybir.AxisListType.X

P = 128
D = 1024
DC = D // P
T = 512
TC = T // P
RING = 4
LEAD = 3
BLOCK = 1024
ACCS = 4
EPS = 1e-6
LN_EPS = 1e-5
X_PARTS = 4
HD = 64
FF = 2816
FC = FF // P
NM = 256
BIG = 1e30
CONV_K = 31
CONV_PAD = CONV_K // 2
SHORT_K = 5
SHORT_PAD = SHORT_K // 2
HEADS = 8
DIRS = 2
LEVELS = 6
TAPS_FIRST = (CONV_K + 1) // 2
LEVEL_FILL = [(1, 0), (2, 1), (3, None), (2, 2), (3, None), (2, None)]
TAPS_SOLVE = sum(taps for taps, _ in LEVEL_FILL)
HEAD_STEPS = 2 * (3 * (SHORT_K - 1) + CONV_K - 1 + 2 + 2 + 2 + 4 + 1 + 1)


def alibi_slopes():
    def pow2(n):
        start = 2.0 ** (-8.0 / n)
        return [start ** (i + 1) for i in range(n)]
    s = pow2(8) + pow2(16)[0::2][:4]
    return np.array(sorted(s, reverse=True), dtype=np.float32).reshape(3, 4)


def shape_constants():
    p = np.arange(P)
    eye = np.eye(P, dtype=np.float32)
    dist = np.full((P, TC, T), BIG, np.float32)
    for r in range(4):
        q = (4 * p + r)[:, None]
        k = np.arange(T)[None, :]
        ok = (q - k >= 0) & (q - k <= 128)
        dist[:, r][ok] = (q - k)[ok]
    steps = (p[:, None] - p[None, :]).astype(np.float32)
    d4 = np.where(steps >= 0, steps * 4, BIG).astype(np.float32)
    d16 = np.where((steps >= 0) & (steps % 4 == 0), steps * 4, BIG).astype(np.float32)
    dist2 = np.stack([d4, d16], 1)
    upper = (p[:, None] <= p[None, :]).astype(np.float32)
    level = np.zeros((P, DIRS, LEVELS + 1, P), np.float32)
    incl = np.zeros((P, DIRS, P), np.float32)
    for l in range(LEVELS + 1):
        w = 2 ** l
        s, c = p[:, None], p[None, :]
        same = (s // (2 * w)) == (c // (2 * w))
        level[:, 0, l] = same & ((s // w) % 2 == 0) & ((c // w) % 2 == 1)
        level[:, 1, l] = same & ((s // w) % 2 == 1) & ((c // w) % 2 == 0)
    incl[:, 0] = p[:, None] <= p[None, :]
    incl[:, 1] = p[:, None] >= p[None, :]
    return {"eye": eye, "dist": dist, "dist2": dist2, "upper": upper, "level": level, "incl": incl}


class Steps:

    def __init__(self, eng, sem):
        self.eng, self.sem, self.n, self.reg, self.per = eng, sem, 0, None, 0

    def did(self, ins):
        ins.then_inc(self.sem, 1)
        self.n += 1
        return self.n

    def wait(self, number=None):
        number = self.n if number is None else number
        self.eng.wait_ge(self.sem, number if self.reg is None else self.reg * self.per + number)

    def enter(self, reg, per):
        self.reg, self.per, self.start = reg, per, self.n

    def leave(self, count):
        assert self.n - self.start == self.per, (self.n - self.start, self.per)
        self.reg, self.n = None, self.start + count * self.per


class Stage:
    def __init__(self, name, w, kc, cols, loops, body, cstep, kind="T", kblocks=1, width=None):
        self.name, self.w, self.kc, self.cols, self.kind = name, w, kc, cols, kind
        self.loops, self.body, self.cstep, self.kblocks = loops, body, cstep, kblocks
        self.width = width or cols // P
        self.accs = loops * len(body) // kblocks * self.width
        assert loops == 1 or (len(body) % RING == 0 and len(body) // kblocks * self.width % ACCS == 0)
        self.n = self.loops * len(self.body)
        assert kc * cols == BLOCK


def stage_tokens(name, w, col0, ncols, tokens):
    body = [(k0, col0 + c) for c in range(0, ncols, 256) for k0 in (0, 4)]
    return Stage(name, w, 4, 256, 1, body, 0, "N", kblocks=2, width=tokens // (2 * P))


def stage_cols(name, w, col0, nchunks, kc=8, looped=True):
    cols = BLOCK // kc
    unroll = 4 if nchunks % 4 == 0 and looped else nchunks
    return Stage(name, w, kc, cols, nchunks // unroll, [(0, col0 + j * cols) for j in range(unroll)], unroll * cols)


def stage_pairs(name, w, colA, colB, pairs):
    assert pairs % 2 == 0
    body = [(0, colA), (0, colB), (0, colA + P), (0, colB + P)]
    return Stage(name, w, 8, P, pairs // 2, body, 2 * P)


def stage_down(name, w):
    body = [(2 * j, n) for n in (0, 512) for j in range(FC // 2)]
    return Stage(name, w, 2, 512, 1, body, 0, kblocks=FC // 2)


STAGES = [
    stage_cols("u", "w_in", 2304, 4),
    stage_tokens("vv", "w_in", 2816, 512, T),
    stage_cols("qk", "w_in", 0, 12),
    stage_tokens("v", "w_in", 1536, 768, T),
    stage_cols("branch_attn", "w_branch_attn", 0, 2, kc=2),
    stage_cols("gate_attn", "w_in", 3328, 8),
    stage_cols("branch_sgu", "w_branch_sgu", 0, 4, kc=4),
    stage_cols("gate_sgu", "w_in", 4352, 8),
    stage_cols("out", "w_out", 0, 8, looped=False),
    stage_cols("cross_q", "w_q_cross", 0, 4),
    stage_cols("mem_k", "w_kv_cross", 0, 4),
    stage_tokens("mem_v", "w_kv_cross", 512, 512, NM),
    stage_cols("cross_o", "w_o_cross", 0, 4, kc=4),
    stage_pairs("gate_up", "w_gate_up", 0, FF, FC),
    stage_down("down", "w_down"),
]
STAGES2 = [
    stage_pairs("glu", "w_in_2", 0, D, 8),
    Stage("heads", "w_in_2", 8, P, 4, [(0, (2 + s) * D + h * P) for h in range(2) for s in range(4)], 2 * P),
    stage_cols("gate_a", "w_in_2", 6 * D + 32, 8),
    stage_cols("gate_b", "w_in_2", 7 * D + 32, 8),
    stage_cols("delta_out", "w_delta_out_2", 0, 8),
    stage_cols("conv_out", "w_conv_out_2", 0, 8),
    stage_cols("o2", "w_o_2", 0, 8, looped=False),
    stage_pairs("gate_up2", "w_gate_up_2", 0, FF, FC),
    stage_down("down2", "w_down_2"),
    stage_cols("pl_proj", "w_pl_proj_2", 0, 2, kc=2),
    stage_cols("pl_gate", "w_pl_gate_2", 0, 8, looped=False),
]

VECTORS = [("g_mix", 8), ("b_gate", 16), ("g_cross", 8), ("g_mem", 8), ("g_ffn", 8), ("g_final", 8),
           ("g_mix_2", 8), ("conv_dw_b_2", 8), ("conv_ln_g_2", 8), ("conv_ln_b_2", 8), ("g_ffn_2", 8),
           ("g_pl_2", 8), ("g_pl_proj_2", 8), ("g_final_2", 8), ("delta_norm_g_2", 1)]


def build(nc, ins, out):
    stages = STAGES + STAGES2
    first_block, n = {}, 0
    for s in stages:
        first_block[s.name] = n
        n += s.n
    NB = n
    first_acc, n = {}, 0
    for s in stages:
        first_acc[s.name] = n
        n += s.accs
    by_name = {s.name: s for s in stages}

    vec_at, n = {}, 0
    for name, rows in VECTORS:
        vec_at[name] = n
        n += rows
    NVEC = n

    with ExitStack() as ctx:
        def sb(name, shape, dt=F32, where=ctx):
            return where.enter_context(nc.sbuf_tensor("s_" + name, shape, dt))

        def sem(name):
            return ctx.enter_context(nc.semaphore(name))

        raw = sb("raw", [P, RING, BLOCK])
        whi = sb("whi", [P, RING, BLOCK], F32R)
        wlo = sb("wlo", [P, RING, BLOCK], F32R)
        X = sb("X", [P, DC, T])
        ah = sb("ah", [P, DC, T], F32R)
        al = sb("al", [P, DC, T], F32R)
        eye = sb("eye", [P, P])
        ones = sb("ones", [P, P])
        vec = sb("vec", [P, NVEC])
        eps = sb("eps", [P, 2])
        rbc = sb("rbc", [P, T])
        lnt = sb("lnt", [P, T])
        sq = sb("sq", [P, 2, T])
        nt = sb("nt", [P, 2, T])
        stg = sb("stg", [P, 4, T])

        psum = ctx.enter_context(nc.psum_tensor("psum", [P, 8, T], F32))

        with ExitStack() as one:
            yh = sb("yh", [P, 6, T], F32R, one)
            yl = sb("yl", [P, 6, T], F32R, one)
            with ExitStack() as a:
                vrows = sb("vrows", [P, P], F32, a)
                xin = sb("xin", [P, TC, D], F32, a)
            with ExitStack() as a:
                qk = sb("qk", [P, 12, T], F32, a)
                vt = sb("vt", [P, 4, 768], F32, a)
                uu = sb("uu", [P, 4, T], F32, a)
                vv = sb("vv", [P, TC, 512], F32, a)
                dist = vv
                dist2 = sb("dist2", [P, 2, P], F32, a)
                upper = sb("upper", [P, P], F32, a)
                wsp = sb("wsp", [P, 4, P], F32, a)
                wspT = sb("wspT", [P, 4, P], F32, a)
                brow = sb("brow", [P, 4, P], F32, a)
                grow = lnt
                sc = sb("sc", [P, 2, 768], F32, a)
                ya = stg[:, 0:2, :].rearrange("p a (b n) -> p (a b) n", n=256)
                pT = stg[:, 2:4, :].rearrange("p a n -> p (a n)")
                ss = sb("ss", [P, 16], F32, a)
                rs = sb("rs", [P, 16], F32, a)
                mx = sb("mx", [P, 16], F32, a)
                nmx = sb("nmx", [P, 16], F32, a)
                den = sb("den", [P, 16], F32, a)
                rden = sb("rden", [P, 16], F32, a)
            with ExitStack() as a:
                m1 = sb("m1", [P, DC, T], F32, a)
                m2 = sb("m2", [P, DC, T], F32, a)
            with ExitStack() as a:
                memin = sb("memin", [P, 2, D], F32, a)
                memT = sb("memT", [P, DC, NM], F32, a)
                mh = sb("mh", [P, DC, NM], F32R, a)
                ml = sb("ml", [P, DC, NM], F32R, a)
                ckT = sb("ckT", [P, 4, NM], F32, a)
                cv = sb("cv", [P, 2, 512], F32, a)
                cq = sb("cq", [P, 4, T], F32, a)
                cs = sb("cs", [P, 4, NM], F32, a)
                cpT = sb("cpT", [P, 2, T], F32, a)
                cmx = sb("cmx", [P, 16], F32, a)
                cden = sb("cden", [P, 16], F32, a)
                crd = sb("crd", [P, 16], F32, a)
        with ExitStack() as a:
            hh = sb("hh", [P, FC, T], F32R, a)
            hl = sb("hl", [P, FC, T], F32R, a)

        conv_w = sb("conv_w", [P, CONV_K * 8])
        short_w = sb("short_w", [P, SHORT_K * 24])
        with ExitStack() as two:
            coef = sb("coef", [P, 5, TC, 16], F32, two)
            hc = sb("hc", [P, 5, TC, DIRS], F32, two)
            of = sb("of", [P, DC, T], F32, two)
            cc = sb("cc", [P, DC, T], F32, two)
            with ExitStack() as b:
                level = sb("level", [P, DIRS, LEVELS + 1, P], F32, b)
                incl = sb("incl", [P, DIRS, P], F32, b)
                cp = sb("cp", [P, DC, T + CONV_K - 1], F32, b)
                with ExitStack() as a:
                    crows = sb("crows", [P, 3, P], F32, a)
                    abw = sb("abw", [P, DC, 32], F32, a)
                    abh = sb("abh", [P, DC, 32], F32R, a)
                    abl = sb("abl", [P, DC, 32], F32R, a)
                    arow = sb("arow", [P, 2, 16], F32, a)
                    ab = sb("ab", [P, TC, 32], F32, a)
                    tmp = sb("tmp", [P, 3, TC, 16], F32, a)
                with ExitStack() as a:
                    raw3 = sb("raw3", [P, 3, T + SHORT_K - 1], F32, a)
                    tok = sb("tok", [P, 2, TC, P], F32, a)
                    E_ = sb("E", [P, DIRS, TC, P], F32, a)
                    AT = sb("AT", [P, DIRS, TC, P], F32, a)
                    EG = sb("EG", [P, DIRS, TC, P], F32, a)
                    KB = sb("KB", [P, DIRS, TC, P], F32, a)
                    vnew = sb("vnew", [P, DIRS, 2, P], F32, a)
                    St = sb("St", [P, DIRS, P], F32, a)
            with ExitStack() as b:
                zh = sb("zh", [P, DC, T], F32R, b)
                zl = sb("zl", [P, DC, T], F32R, b)
                gb = sb("gb", [P, DC, T], F32, b)
        ga = X
        mu = nt[:, 1, :]
        XV = X[:, :, :].rearrange("p (k d) (t n) -> p k d t n", k=4, t=TC)
        Mi, MT, QK, QD = XV[:, 0], XV[:, 1], XV[:, 2], XV[:, 3]
        with ExitStack() as a:
            ph = sb("ph", [P, 2, T], F32R, a)
            pl = sb("pl", [P, 2, T], F32R, a)
            pin = sb("pin", [P, TC, 256], F32, a)
            PL = sb("PL", [P, DC, T], F32, a)
            outt = sb("outt", [P, TC, D], F32, a)
        spill = nc.dram_tensor("x_spill", [P, DC, T], F32).ap()

        sems = {}

        def S(name):
            if name not in sems:
                sems[name] = ctx.enter_context(nc.semaphore(name))
            return sems[name]

        raw_loaded = [S(f"raw_loaded{i}") for i in range(RING)]
        hi_ready = S("hi_ready")
        lo_ready = S("lo_ready")
        block_used = S("block_used")
        acc_free = S("acc_free")
        stage_used = S("stage_used")

        def weight(name):
            w = ins[name]
            if len(w.shape) == 3:
                w = w.rearrange("a k n -> (a k) n")
            return w.rearrange("(c p) n -> p c n", p=P)

        def passes(eng, s, first_alone=False):
            if s.loops == 1 or first_alone:
                yield 0
            if s.loops > 1:
                with eng.Fori(1 if first_alone else 0, s.loops) as i:
                    yield i

        def count(s, i, j, extra=0):
            return i * len(s.body) + (first_block[s.name] + j + extra)

        def acc_number(s, i, g, m, extra=0):
            per = len(s.body) // s.kblocks * s.width
            return i * per + (first_acc[s.name] + g * s.width + m + extra)

        def pe_stage(pe, name, act_hi, act_lo, tokens=T, cols_of=None, normed=None, between={}):
            s = by_name[name]
            n_tok = tokens // P
            for i in passes(pe, s, normed is not None):
                opening = normed is not None and isinstance(i, int)
                if opening:
                    for j in range(2):
                        pe.wait_ge(lo_ready, count(s, 0, j, RING + 1))
                        pe.wait_ge(acc_free, acc_number(s, 0, j, 0, 1))
                    for k in range(DC):
                        pe.wait_ge(S("normed"), normed + k + 1)
                        for j in range(2):
                            slot, bank = (first_block[name] + j) % RING, (first_acc[name] + j) % ACCS
                            w, o = slice(k * P, (k + 1) * P), psum[:, bank, 0:tokens]
                            pe.matmul(o, whi[:, slot, w], act_hi[:, k, :], start=k == 0, stop=False)
                            pe.matmul(o, whi[:, slot, w], act_lo[:, k, :], start=False, stop=False)
                            mm = pe.matmul(o, wlo[:, slot, w], act_hi[:, k, :], start=False, stop=k == DC - 1)
                            if k == DC - 1:
                                mm.then_inc(block_used, 1)
                    if 1 in between:
                        between[1]()
                for j, (k0, _) in enumerate(s.body):
                    if opening and j < 2:
                        continue
                    slot = (first_block[name] + j) % RING
                    g, kb = j // s.kblocks, j % s.kblocks
                    pe.wait_ge(lo_ready, count(s, i, j, RING + 1))
                    if s.kind == "T":
                        for m in range(s.width):
                            bank = (first_acc[name] + g * s.width + m) % ACCS
                            if kb == 0:
                                pe.wait_ge(acc_free, acc_number(s, i, g, m, 1))
                            for k in range(s.kc):
                                w = slice(k * s.cols + m * P, k * s.cols + (m + 1) * P)
                                kk = k0 + k
                                o = psum[:, bank, 0:tokens]
                                first, last = kb == 0 and k == 0, kb == s.kblocks - 1 and k == s.kc - 1
                                pe.matmul(o, whi[:, slot, w], act_hi[:, kk, :], start=first, stop=False)
                                pe.matmul(o, whi[:, slot, w], act_lo[:, kk, :], start=False, stop=False)
                                mm = pe.matmul(o, wlo[:, slot, w], act_hi[:, kk, :], start=False, stop=last)
                    else:
                        if kb == 0:
                            continue
                        for t in range(n_tok):
                            tok = cols_of(t)
                            bank = (first_acc[name] + g * s.width + t // 2) % ACCS
                            if t % 2 == 0:
                                pe.wait_ge(acc_free, acc_number(s, i, g, t // 2, 1))
                            o = psum[:, bank, t % 2 * s.cols:(t % 2 + 1) * s.cols]
                            for k in range(DC):
                                at = (slot - 1 + k // s.kc) % RING
                                w = slice(k % s.kc * s.cols, (k % s.kc + 1) * s.cols)
                                pe.matmul(o, act_hi[:, k, tok], whi[:, at, w], start=k == 0, stop=False)
                                pe.matmul(o, act_hi[:, k, tok], wlo[:, at, w], start=False, stop=False)
                                mm = pe.matmul(o, act_lo[:, k, tok], whi[:, at, w], start=False, stop=k == DC - 1)
                    mm.then_inc(block_used, 1 if s.kind == "T" else s.kblocks)
                    if j in between:
                        between[j]()

        def act_round(act, b, q, per4):
            slot = q % RING
            act.wait_ge(raw_loaded[slot], per4 * 16 + 16 * (q // RING + 1))
            act.wait_ge(block_used, b + 1)
            act.activation(whi[:, slot, :], raw[:, slot, :], ACT.Copy).then_inc(hi_ready, 1)

        def act_stage(act, name, empty, after=None):
            s = by_name[name]
            for i in passes(act, s):
                for j in range(len(s.body)):
                    q = first_block[name] + j + LEAD
                    if s is not stages[-1] or q < NB:
                        act_round(act, count(s, i, j, LEAD), q, i * (len(s.body) // RING) if s.loops > 1 else 0)
                    if j % s.kblocks == s.kblocks - 1:
                        g = j // s.kblocks
                        act.wait_ge(block_used, count(s, i, j, RING + 1))
                        for m in range(s.width):
                            a = first_acc[name] + g * s.width + m
                            empty(i, g, m, a, a % ACCS).then_inc(acc_free, 1)
                            if after:
                                after(g * s.width + m)

        def act_square(act, n, c, src, tokens=T):
            if c == 0 and n:
                act.wait_ge(S("r_ready"), n)
            if c >= 3:
                act.wait_ge(S("sq_summed"), 7 * n + c - 2)
            dst = lnt[:, 0:tokens] if c == 0 else sq[:, c % 2, 0:tokens]
            act.activation(dst, src[:, c, :], ACT.Square).then_inc(S("sq_ready"), 1)

        def dve_sum(dve, n, c, tokens=T):
            dve.wait_ge(S("sq_ready"), 8 * n + c + 1)
            if c >= 2:
                dve.wait_ge(S("sq_summed"), 7 * n + c - 1)
            dve.tensor_tensor(lnt[:, 0:tokens], lnt[:, 0:tokens], sq[:, c % 2, 0:tokens], ALU.add)\
               .then_inc(S("sq_summed"), 1)

        def pe_norm(pe, n, tokens=T):
            if n:
                pe.wait_ge(S("r_ready"), n)
            pe.wait_ge(S("sq_summed"), 7 * (n + 1))
            pe.matmul(psum[:, 4, 0:tokens], ones[:, :], lnt[:, 0:tokens], start=True, stop=True).then_inc(S("sq_total"), 1)

        def act_inverse(act, mine, n, tokens=T):
            act.wait_ge(S("sq_total"), n + 1)
            if n:
                act.wait_ge(S("n_ready"), 8 * n)
            mine.did(act.activation(lnt[:, 0:tokens], psum[:, 4, 0:tokens], ACT.Ln, scale=1.0 / D, bias=eps[:, 0:1]))
            mine.wait()
            act.activation(rbc[:, 0:tokens], lnt[:, 0:tokens], ACT.Exp, scale=-0.5).then_inc(S("r_ready"), 1)

        def act_norm_hi(act, n, hi, tokens=T):
            for c in range(DC):
                act.wait_ge(S("n_ready"), 8 * n + c + 1)
                act.activation(hi[:, c, :], nt[:, c % 2, 0:tokens], ACT.Copy).then_inc(S("nh_ready"), 1)

        def dve_norm(dve, n, nh, src, gain, tokens=T, hilo=None, after=None):
            g0 = vec_at[gain]
            dve.wait_ge(S("r_ready"), n + 1)

            def low(c):
                dve.wait_ge(S("nh_ready"), 8 * nh + c + 1)
                dve.tensor_tensor(hilo[1][:, c, :], nt[:, c % 2, 0:tokens], hilo[0][:, c, :].bitcast(F32),
                                  ALU.subtract).then_inc(S("normed"), 1)

            for c in range(DC):
                if hilo is not None and c >= 2:
                    dve.wait_ge(S("normed"), 8 * nh + c - 1)
                dst = nt[:, c % 2, 0:tokens] if hilo is not None else src[:, c, :]
                dve.scalar_tensor_tensor(out=dst, in0=src[:, c, :], scalar=vec[:, g0 + c:g0 + c + 1],
                                         in1=rbc[:, 0:tokens], op0=ALU.mult, op1=ALU.mult).then_inc(S("n_ready"), 1)
                if hilo is not None and c >= 1:
                    low(c - 1)
                if after:
                    after(c)
            if hilo is not None:
                low(DC - 1)

        def act_split(act, ready, n0, src, hi, done, chunks):
            for c in range(chunks):
                act.wait_ge(S(ready), n0 + c + 1)
                act.activation(hi[:, c, :], src[:, c, :], ACT.Copy).then_inc(S(done), 1)

        def head_step(i, j, per, k):
            return i * (2 * per) + (j * per + k)

        chunk_order = [range(TC), range(TC - 1, -1, -1)]
        PASSES = HEADS // 2
        heads = by_name["heads"]

        def head_passes(eng):
            with eng.Fori(0, PASSES - 1) as i:
                yield i, False
            yield PASSES - 1, True

        def flat(ap):
            return ap.rearrange("p t n -> p (t n)")

        def head_block(i, j, n, extra):
            return count(heads, i, 4 * j + n, extra)

        def head_acc(i, j, n, extra=0):
            return acc_number(heads, i, 4 * j + n, 0, ACCS + 1 + extra)

        def pe_heads(pe):
            def project(i, j, n, part, parts):
                slot, bank = (first_block["heads"] + 4 * j + n) % RING, 4 + n % 2
                if part == 0:
                    pe.wait_ge(lo_ready, head_block(i, j, n, RING + 1))
                    pe.wait_ge(acc_free, head_acc(i, j, n, -2))
                for k in range(part * DC // parts, (part + 1) * DC // parts):
                    wk = slice(k * P, (k + 1) * P)
                    pe.matmul(psum[:, bank, :], whi[:, slot, wk], ah[:, k, :], start=k == 0, stop=False)
                    pe.matmul(psum[:, bank, :], whi[:, slot, wk], al[:, k, :], start=False, stop=False)
                    mm = pe.matmul(psum[:, bank, :], wlo[:, slot, wk], ah[:, k, :], start=False, stop=k == DC - 1)
                if part == parts - 1:
                    mm.then_inc(block_used, 1)

            def lengths(i, j):
                for n in range(2):
                    pe.wait_ge(S("l2_sq"), head_step(i, j, 2, n + 1))
                    pe.wait_ge(acc_free, head_acc(i, j, 2 + n))
                    pe.matmul(psum[:, 4 + n, :], ones[:], sq[:, n, :], start=True, stop=True).then_inc(S("l2_sum"), 1)

            def start(i, j, before, after):
                w = lambda name, per, k: pe.wait_ge(S(name), head_step(i, j, per, k))
                w1 = lambda name, per, k: pe.wait_ge(S(name), head_step(i, j - 1, per, k))
                w("hc_ready", 1, 1)
                for d in range(DIRS):
                    for t in range(TC):
                        mm = pe.matmul(psum[:, d, t * P:(t + 1) * P], hc[:, 0, t, d:d + 1].to_broadcast([P, P]),
                                       incl[:, d, :], start=True, stop=True)
                    mm.then_inc(S("g_bc"), 1)
                for d in range(DIRS):
                    for t in range(TC):
                        mm = pe.matmul(psum[:, 2 + d, t * P:(t + 1) * P], hc[:, 1, t, d:d + 1].to_broadcast([P, P]),
                                       eye[:], start=True, stop=True)
                    mm.then_inc(S("b_bc"), 1)
                w("qk_scaled", 2, 2)
                if before:
                    w1("o_both", 1, 1)
                for n in range(2):
                    for t in range(TC):
                        tk = slice(t * P, (t + 1) * P)
                        mm = pe.matmul(psum[:, 4 + n, tk], stg[:, 1, tk], stg[:, n, tk], start=True, stop=True)
                    mm.then_inc(S("kq_ready"), 1)
                w("qkv_silu", 3, 3)
                if before:
                    w1("s_ready", 2 * TC, 2 * TC)
                for n in range(2):
                    for t in range(TC):
                        mm = pe.transpose(psum[:, 6 + n, t * P:(t + 1) * P], stg[:, 1 + n, t * P:(t + 1) * P], eye[:])
                    mm.then_inc(S("kv_turned"), 1)
                if before:
                    w("tok_ready", 2, 2)
                    w1("o_sq", 1, 1)
                    pe.matmul(psum[:, 7, :], ones[:], sq[:, 0, :], start=True, stop=True).then_inc(S("o_sum"), 1)
                if after:
                    w("qk_masked", 4, 4)
                    project(i, j + 1, 0, 0, 1)
                for d in range(DIRS):
                    w("mt0_ready", 2, d + 1)
                    w("tok_ready", 2, 2)
                    if before and d == 1:
                        w1("o_ln", 1, 1)
                    for t in range(TC):
                        mm = pe.transpose(psum[:, 6 + d, t * P:(t + 1) * P], MT[:, d, t, :], eye[:])
                    mm.then_inc(S("m0_turned"), 1)
                if after:
                    project(i, j + 1, 1, 0, 1)

            def solve(i, j, after):
                w = lambda name, per, k: pe.wait_ge(S(name), head_step(i, j, per, k))
                for l in range(LEVELS):
                    for d in range(DIRS):
                        w("lev_ready", 2 * LEVELS, 2 * l + d + 1)
                        w("m_ready", 2 * LEVELS, 2 * l + d + 1)
                        if l:
                            w("mt_ready", 2 * LEVELS, 2 * l + d - 1)
                        for t in range(TC):
                            mm = pe.matmul(psum[:, 6 + d, t * P:(t + 1) * P], E_[:, d, t, :], Mi[:, d, t, :],
                                           start=True, stop=True)
                        mm.then_inc(S("p_ready"), 1)
                    if after and l < 4:
                        project(i, j + 1, 2 + l // 2, l % 2, 2)
                    if after and l == 4:
                        lengths(i, j + 1)
                    for d in range(DIRS):
                        w("q_ready", 2 * LEVELS, 2 * l + d + 1)
                        if l == 0:
                            w("kb_ready", 2, d + 1)
                        for t in range(TC):
                            if l < LEVELS - 1:
                                mm = pe.matmul(psum[:, d, t * P:(t + 1) * P], MT[:, d, t, :], EG[:, d, t, :],
                                               start=True, stop=True)
                        if l < LEVELS - 1:
                            mm.then_inc(S("m_new"), 1)
                        for t in range(TC):
                            mm = pe.matmul(psum[:, 2 + d, t * P:(t + 1) * P], EG[:, d, t, :], MT[:, d, t, :],
                                           start=True, stop=True)
                        mm.then_inc(S("mt_new"), 1)

            def recur(i, j, after):
                w = lambda name, per, k: pe.wait_ge(S(name), head_step(i, j, per, k))
                for n in range(TC):
                    for d in range(DIRS):
                        t = chunk_order[d][n]
                        if n:
                            w("s_ready", 2 * TC, 2 * (n - 1) + d + 1)
                            pe.matmul(psum[:, 6 + d, 0:P], KB[:, d, t, :], St[:, d, :], start=True, stop=True)\
                              .then_inc(S("r_mm"), 1)
                    for d in range(DIRS):
                        t = chunk_order[d][n]
                        if n:
                            w("v_ready", 2 * (TC - 1), 2 * (n - 1) + d + 1)
                            v = vnew[:, d, 0, :]
                        else:
                            w("vb_ready", 2, d + 1)
                            w("mt_ready", 2 * LEVELS, 2 * (LEVELS - 1) + d + 1)
                            v = AT[:, d, t, :]
                        pe.matmul(psum[:, 6 + d, P:2 * P], MT[:, d, t, :], v, start=True, stop=True)\
                          .then_inc(S("vn_mm"), 1)
                    for d in range(DIRS):
                        t = chunk_order[d][n]
                        o = psum[:, 4 + d, t * P:(t + 1) * P]
                        if n:
                            pe.matmul(o, St[:, d, :], QD[:, d, t, :], start=True, stop=False)
                        w("vn_ready", 2 * TC, 2 * n + d + 1)
                        if n == 0:
                            w("kt_ready", 2, d + 1)
                            if after:
                                pe.wait_ge(S("l2_ln"), head_step(i, j + 1, 2, 2))
                            else:
                                w("qk_masked", 4, 4)
                        pe.matmul(psum[:, 6 + d, 2 * P:3 * P], E_[:, d, t, :], vnew[:, d, 1, :], start=True, stop=True)\
                          .then_inc(S("s_mm"), 1)
                        mm = pe.matmul(o, vnew[:, d, 1, :], QK[:, d, t, :], start=n == 0, stop=True)
                        if n == TC - 1:
                            mm.then_inc(S("o_ready"), 1)
                        else:
                            mm.then_inc(S("o_part"), 1)

            pe.wait_ge(acc_free, first_acc["heads"] + ACCS)
            for n in range(4):
                project(0, 0, n, 0, 1)
            lengths(0, 0)
            start(0, 0, False, True)
            for i, last in head_passes(pe):
                for j in range(2):
                    after = not (last and j == 1)
                    solve(i, j, after)
                    recur(i, j, after)
                    if after:
                        start(i, j + 1, True, not last)
            pe.wait_ge(S("o_sq"), HEADS)
            pe.matmul(psum[:, 7, :], ones[:], sq[:, 0, :], start=True, stop=True).then_inc(S("o_sum"), 1)

        def act_heads(act):
            def take(i, j, n):
                b = 4 * j + n
                act_round(act, count(heads, i, b, LEAD), first_block["heads"] + b + LEAD, i * 2)
                act.wait_ge(block_used, head_block(i, j, n, RING + 1))
                bank = 4 + n % 2
                if n < 3:
                    act.wait_ge(S("raw_free"), head_step(i, j, 1, 1))
                    a = act.activation(raw3[:, n, SHORT_PAD:SHORT_PAD + T], psum[:, bank, :], ACT.Copy)
                else:
                    a = act.activation(of[:, bass.ds(i * 2 + j, 1), :], psum[:, bank:bank + 1, :], ACT.Silu)
                a.then_inc(acc_free, 1)

            def silu(i, j, n):
                act.wait_ge(S("conv3"), head_step(i, j, 3, n + 1))
                act.activation(stg[:, n, :], stg[:, n, :], ACT.Silu).then_inc(S("qkv_silu"), 1)

            def squares(i, j):
                for n in range(2):
                    act.wait_ge(S("qkv_silu"), head_step(i, j, 3, n + 1))
                    act.activation(sq[:, n, :], stg[:, n, :], ACT.Square).then_inc(S("l2_sq"), 1)

            def inverse_lengths(i, j):
                for n in range(2):
                    act.wait_ge(S("l2_sum"), head_step(i, j, 2, n + 1))
                    act.activation(nt[:, n, :], psum[:, 4 + n, :], ACT.Ln, bias=eps[:, 0:1]).then_inc(S("l2_ln"), 1)
                for n in range(2):
                    act.wait_ge(S("l2_ln"), head_step(i, j, 2, n + 1))
                    act.activation(nt[:, n, :], nt[:, n, :], ACT.Exp, scale=-0.5).then_inc(S("l2_r"), 1)

            def o_squares(i, j):
                act.wait_ge(S("o_both"), head_step(i, j, 1, 1))
                act.activation(sq[:, 0, :], stg[:, 3, :], ACT.Square).then_inc(S("o_sq"), 1)

            def o_inverse(i, j):
                act.wait_ge(S("o_sum"), head_step(i, j, 1, 1))
                act.activation(lnt[:], psum[:, 7, :], ACT.Ln, scale=1.0 / P, bias=eps[:, 0:1]).then_inc(S("o_ln"), 1)
                act.wait_ge(S("o_ln"), head_step(i, j, 1, 1))
                act.activation(rbc[:], lnt[:], ACT.Exp, scale=-0.5).then_inc(S("o_r"), 1)

            def start(i, j, before, after):
                w = lambda name, per, k: act.wait_ge(S(name), head_step(i, j, per, k))
                for d in range(DIRS):
                    w("e_arg", 2, d + 1)
                    act.activation(E_[:, d], E_[:, d], ACT.Exp).then_inc(S("e_ready"), 1)
                for d in range(DIRS):
                    act.activation(flat(EG[:, d]), psum[:, d, :], ACT.Exp).then_inc(S("eg_ready"), 1)
                for n in range(2):
                    w("kv_turned", 2, n + 1)
                    act.activation(flat(tok[:, n]), psum[:, 6 + n, :], ACT.Copy).then_inc(S("tok_ready"), 1)
                if before:
                    o_squares(i, j - 1)
                    o_inverse(i, j - 1)
                if after:
                    take(i, j + 1, 0)
                for d in range(DIRS):
                    w("m0_turned", 2, d + 1)
                    act.activation(flat(Mi[:, d]), psum[:, 6 + d, :], ACT.Copy).then_inc(S("m_ready"), 1)
                if after:
                    take(i, j + 1, 1)

            def solve(i, j, after):
                w = lambda name, per, k: act.wait_ge(S(name), head_step(i, j, per, k))
                for l in range(LEVELS):
                    if after and l == 1:
                        take(i, j + 1, 2)
                    if after and l == 2:
                        silu(i, j + 1, 0)
                        silu(i, j + 1, 1)
                        squares(i, j + 1)
                    if after and l == 3:
                        take(i, j + 1, 3)
                    if after and l == 4:
                        silu(i, j + 1, 2)
                    if after and l == 5:
                        inverse_lengths(i, j + 1)
                    for d in range(DIRS):
                        w("mt_new", 2 * LEVELS, 2 * l + d + 1)
                        if l < LEVELS - 1:
                            w("m_new", 2 * (LEVELS - 1), 2 * l + d + 1)
                            act.activation(flat(Mi[:, d]), psum[:, d, :], ACT.Copy).then_inc(S("m_ready"), 1)
                        act.activation(flat(MT[:, d]), psum[:, 2 + d, :], ACT.Copy).then_inc(S("mt_ready"), 1)

            def recur(i, j):
                w = lambda name, per, k: act.wait_ge(S(name), head_step(i, j, per, k))
                for n in range(TC):
                    for d in range(DIRS):
                        w("vn_mm", 2 * TC, 2 * n + d + 1)
                        if n:
                            w("s_mm", 2 * TC, 2 * (n - 1) + d + 1)
                            w("o_part", 2 * (TC - 1), 2 * (n - 1) + d + 1)
                        act.activation(vnew[:, d, 1, :], psum[:, 6 + d, P:2 * P], ACT.Copy).then_inc(S("vn_ready"), 1)

            for n in range(4):
                take(0, 0, n)
            for n in range(3):
                silu(0, 0, n)
            squares(0, 0)
            inverse_lengths(0, 0)
            start(0, 0, False, True)
            for i, last in head_passes(act):
                for j in range(2):
                    after = not (last and j == 1)
                    solve(i, j, after)
                    recur(i, j)
                    if after:
                        start(i, j + 1, True, not last)
            o_squares(PASSES - 1, 1)
            o_inverse(PASSES - 1, 1)

        def dve_heads(dve, mine):
            g0 = vec_at["delta_norm_g_2"]
            cb = vec_at["conv_dw_b_2"]
            eyes = eye[:].rearrange("p (a n) -> p a n", a=1).to_broadcast([P, TC, P])

            def banked(b):
                return psum[:, b, :].rearrange("p (t n) -> p t n", t=TC)

            conv_step = [None, None]

            def conv_tap(i, k):
                for n in range(2):
                    conv_step[n] = chunk_tap(i * 2 + n, k, conv_step[n])

            def chunk_tap(head, k, before):
                dst = cc[:, bass.ds(head, 1), :]
                src, tap = cp[:, bass.ds(head, 1), k:k + T], conv_w[:, bass.ds(head + 8 * k, 1)]
                if k == 0:
                    return mine.did(dve.tensor_scalar(dst, src, tap, vec[:, bass.ds(head + cb, 1)], ALU.mult, ALU.add))
                mine.wait(before)
                ins_ = dve.scalar_tensor_tensor(out=dst, in0=src, scalar=tap, in1=dst, op0=ALU.mult, op1=ALU.add)
                if k < CONV_K - 1:
                    return mine.did(ins_)
                ins_.then_inc(S("conv_done"), 1)

            def convolve(i, j, first, last, short=None):
                taps = range(first, last)
                if short is not None:
                    head = i * 2 + (j + 1)
                    dve.wait_ge(acc_free, head_acc(i, j + 1, short))
                for k in range(max(len(taps), 0 if short is None else SHORT_K)):
                    if short is not None and k < SHORT_K:
                        tap = short_w[:, bass.ds(head + (k * 24 + short * 8), 1)]
                        src, dst = raw3[:, short, k:k + T], stg[:, short, :]
                        if k == 0:
                            own = mine.did(dve.tensor_scalar(dst, src, tap, None, ALU.mult))
                        else:
                            mine.wait(own)
                            ins_ = dve.scalar_tensor_tensor(out=dst, in0=src, scalar=tap, in1=dst, op0=ALU.mult, op1=ALU.add)
                            if k < SHORT_K - 1:
                                own = mine.did(ins_)
                            else:
                                ins_.then_inc(S("conv3"), 1)
                    if k < len(taps):
                        conv_tap(i, taps[k])
                if short == 2:
                    dve.wait_ge(S("conv3"), head_step(i, j + 1, 3, 3))
                    dve.sem_inc(S("raw_free"), 1)

            def rest_of_taps(i, j):
                convolve(i, j, j * TAPS_FIRST + TAPS_SOLVE, TAPS_FIRST if j == 0 else CONV_K)

            def start(i, j, before):
                w = lambda name, per, k: dve.wait_ge(S(name), head_step(i, j, per, k))
                head = i * 2 + j
                dve.tensor_copy(hc[:].rearrange("p k t d -> p (k t) d"),
                                coef[:].rearrange("p k t (d h) -> p (k t) d h", d=DIRS)[:, :, :, bass.ds(head, 1)]
                                .rearrange("p a d h -> p a (d h)")).then_inc(S("hc_ready"), 1)
                for n in range(2):
                    w("l2_r", 2, n + 1)
                    w("qkv_silu", 3, n + 1)
                    dve.scalar_tensor_tensor(out=stg[:, n, :], in0=stg[:, n, :], scalar=P ** -0.5 if n == 0 else 1.0,
                                             in1=nt[:, n, :], op0=ALU.mult, op1=ALU.mult).then_inc(S("qk_scaled"), 1)
                w("hc_ready", 1, 1)
                for d in range(DIRS):
                    w("g_bc", 2, d + 1)
                    for t in range(TC):
                        ins_ = dve.tensor_scalar(E_[:, d, t, :], psum[:, d, t * P:(t + 1) * P], hc[:, 2, t, d:d + 1], 0.0,
                                                 ALU.add, ALU.min)
                    ins_.then_inc(S("e_arg"), 1)
                if before:
                    o_sum_up(i, j - 1)
                for d in range(DIRS):
                    w("e_ready", 2, d + 1)
                    masked = mine.did(dve.tensor_tensor(E_[:, d], E_[:, d], incl[:, d:d + 1, :].to_broadcast([P, TC, P]), ALU.mult))
                w("kq_ready", 2, 2)
                mine.wait(masked)
                for d in range(DIRS):
                    dve.tensor_tensor(QK[:, d], E_[:, d], banked(4), ALU.mult).then_inc(S("qk_masked"), 1)
                    dve.tensor_tensor(AT[:, d], E_[:, d], banked(5), ALU.mult).then_inc(S("qk_masked"), 1)
                for d in range(DIRS):
                    w("qk_masked", 4, 2 * d + 2)
                    w("b_bc", 2, d + 1)
                    lower = mine.did(dve.tensor_tensor(AT[:, d], AT[:, d], banked(2 + d), ALU.mult))
                for d in range(DIRS):
                    mine.wait(lower)
                    mine.wait(mine.did(dve.tensor_tensor(E_[:, d], AT[:, d], level[:, d, 0:1, :].to_broadcast([P, TC, P]), ALU.mult)))
                    dve.tensor_tensor(MT[:, d], eyes, E_[:, d], ALU.subtract).then_inc(S("mt0_ready"), 1)
                for d in range(DIRS):
                    w("mt0_ready", 2, d + 1)
                    dve.tensor_tensor(E_[:, d], AT[:, d], level[:, d, 1:2, :].to_broadcast([P, TC, P]), ALU.mult)\
                       .then_inc(S("lev_ready"), 1)
                for d in range(DIRS):
                    w("eg_ready", 2, d + 1)
                    q_ = stg[:, 0, :].rearrange("p (t n) -> p t n", t=TC)
                    k_ = stg[:, 1, :].rearrange("p (t n) -> p t n", t=TC)
                    w("qk_scaled", 2, 2)
                    decayed = mine.did(dve.tensor_tensor(KB[:, d], k_, EG[:, d], ALU.mult))
                    decayed_q = mine.did(dve.tensor_tensor(QD[:, d], q_, EG[:, d], ALU.mult))
                    mine.wait(decayed)
                    dve.tensor_tensor(KB[:, d], KB[:, d], banked(2 + d), ALU.mult).then_inc(S("kb_ready"), 1)
                if before:
                    o_gate(i, j - 1)
                    rest_of_taps(i, j - 1)
                w("kb_ready", 2, 2)
                mine.wait(decayed_q)

            def solve(i, j, after):
                w = lambda name, per, k: dve.wait_ge(S(name), head_step(i, j, per, k))
                tap = j * TAPS_FIRST
                for l in range(LEVELS):
                    for d in range(DIRS):
                        w("p_ready", 2 * LEVELS, 2 * l + d + 1)
                        dve.tensor_tensor(EG[:, d], eyes, banked(6 + d), ALU.subtract).then_inc(S("q_ready"), 1)
                        if l < LEVELS - 1:
                            dve.tensor_tensor(E_[:, d], AT[:, d], level[:, d, l + 2:l + 3, :].to_broadcast([P, TC, P]),
                                              ALU.mult).then_inc(S("lev_ready"), 1)
                        else:
                            w("lev_ready", 2 * LEVELS, 2 * LEVELS)
                            w("tok_ready", 2, 2)
                            for t in range(TC):
                                ins_ = dve.tensor_scalar(E_[:, d, t, :], tok[:, 0, t, :], hc[:, 3, t, d:d + 1], None, ALU.mult)
                            ins_.then_inc(S("kt_ready"), 1)
                            for t in range(TC):
                                ins_ = dve.tensor_scalar(AT[:, d, t, :], tok[:, 1, t, :], hc[:, 1, t, d:d + 1], None, ALU.mult)
                            ins_.then_inc(S("vb_ready"), 1)
                    taps, short = LEVEL_FILL[l]
                    convolve(i, j, tap, tap + taps, short if after else None)
                    tap += taps
                w("vb_ready", 2, 2)

            def recur(i, j):
                w = lambda name, per, k: dve.wait_ge(S(name), head_step(i, j, per, k))
                for n in range(TC):
                    if n:
                        for d in range(DIRS):
                            t = chunk_order[d][n]
                            w("r_mm", 2 * (TC - 1), 2 * (n - 1) + d + 1)
                            dve.tensor_tensor(vnew[:, d, 0, :], AT[:, d, t, :], psum[:, 6 + d, 0:P], ALU.subtract)\
                               .then_inc(S("v_ready"), 1)
                    for d in range(DIRS):
                        t = chunk_order[d][n]
                        w("s_mm", 2 * TC, 2 * n + d + 1)
                        if n == 0:
                            ins_ = dve.tensor_copy(St[:, d, :], psum[:, 6 + d, 2 * P:3 * P])
                        else:
                            w("s_ready", 2 * TC, 2 * (n - 1) + d + 1)
                            ins_ = dve.scalar_tensor_tensor(out=St[:, d, :], in0=St[:, d, :], scalar=hc[:, 4, t, d:d + 1],
                                                            in1=psum[:, 6 + d, 2 * P:3 * P], op0=ALU.mult, op1=ALU.add)
                        ins_.then_inc(S("s_ready"), 1)
                w("s_ready", 2 * TC, 2 * TC)

            def o_sum_up(i, j):
                dve.wait_ge(S("o_ready"), head_step(i, j, 2, 2))
                mine.wait(mine.did(dve.tensor_copy(stg[:, 3, :], psum[:, 4, :])))
                dve.tensor_tensor(stg[:, 3, :], stg[:, 3, :], psum[:, 5, :], ALU.add).then_inc(S("o_both"), 1)

            def o_gate(i, j):
                dve.wait_ge(S("o_r"), head_step(i, j, 1, 1))
                mine.wait(mine.did(dve.scalar_tensor_tensor(out=stg[:, 3, :], in0=stg[:, 3, :], scalar=vec[:, g0:g0 + 1],
                                                            in1=rbc[:], op0=ALU.mult, op1=ALU.mult)))
                o_ = of[:, bass.ds(i * 2 + j, 1), :]
                dve.tensor_tensor(o_, stg[:, 3:4, :], o_, ALU.mult).then_inc(S("o_gated"), 1)
                dve.wait_ge(S("o_gated"), head_step(i, j, 1, 1))

            mine.did(dve.memset(raw3[:, :, 0:SHORT_PAD], 0.0))
            mine.did(dve.memset(raw3[:, :, SHORT_PAD + T:], 0.0))
            mine.wait()
            dve.wait_ge(S("coef_exp"), 2)
            dve.wait_ge(S("beta_ready"), 1)
            dve.sem_inc(S("raw_free"), 1)
            for n in range(3):
                convolve(0, -1, 0, 0, n)
            start(0, 0, False)
            for i, last in head_passes(dve):
                if not last:
                    mine.enter(i, HEAD_STEPS)
                for j in range(2):
                    after = not (last and j == 1)
                    solve(i, j, after)
                    recur(i, j)
                    if after:
                        start(i, j + 1, True)
                if not last:
                    mine.leave(PASSES - 1)
            o_sum_up(PASSES - 1, 1)
            rest_of_taps(PASSES - 1, 1)
            o_gate(PASSES - 1, 1)

        slopes = alibi_slopes()
        block = ctx.enter_context(nc.Block())

        @block.sync
        def _(sp):
            sp.dma_start(eye[:], ins["eye"]).then_inc(S("eye_in"), 16)
            for n in range(X_PARTS):
                cols = slice(n * D // X_PARTS, (n + 1) * D // X_PARTS)
                sp.dma_start(xin[:, :, cols], ins["x"].rearrange("a (c p) d -> p (a c) d", p=P)[:, :, cols])\
                  .then_inc(S(f"x_in{n}"), 16)
            for name, rows in VECTORS:
                v = ins[name]
                v = v.rearrange("a n -> (a n)") if len(v.shape) == 2 else v
                sp.dma_start(vrows[vec_at[name]:vec_at[name] + rows, :], v.rearrange("(c p) -> c p", p=P))\
                  .then_inc(S("vrows_in"), 16)
            for s in stages:
                w = weight(s.w)
                if s.name == "vv":
                    sp.wait_ge(S("x_turned"), 8)
                    sp.wait_ge(S("vec_ready"), 1)
                    sp.dma_start(dist2[:], ins["dist2"]).then_inc(S("attn_in"), 16)
                    sp.dma_start(upper[:], ins["upper"]).then_inc(S("attn_in"), 16)
                    sp.dma_start(wsp[:], ins["w_sgu_spatial"].rearrange("a g t s -> t (a g) s")).then_inc(S("attn_in"), 16)
                    sp.dma_start(brow[:], ins["b_sgu_spatial"].rearrange("a g t -> a (g t)").to_broadcast([P, 4 * P])
                                 .rearrange("p (g t) -> p g t", g=4)).then_inc(S("attn_in"), 16)
                    sp.wait_ge(S("r_ready"), 1)
                    sp.dma_start(grow[:], ins["g_sgu"].to_broadcast([P, 512])).then_inc(S("attn_in"), 16)
                for i in passes(sp, s):
                    for j, (k0, col) in enumerate(s.body):
                        q = first_block[s.name] + j
                        slot = q % RING
                        cols = bass.ds(i * s.cstep + col, s.cols) if s.loops > 1 else slice(col, col + s.cols)
                        sp.wait_ge(lo_ready, count(s, i, j, 1))
                        sp.dma_start(raw[:, slot, :].rearrange("p (c n) -> p c n", c=s.kc),
                                     w[:, k0:k0 + s.kc, cols]).then_inc(raw_loaded[slot], 16)
            for n in range(2 * TC):
                half, t = divmod(n, TC)
                sp.wait_ge(S("out_ready"), n + 1)
                sp.dma_start(out.rearrange("a (c p) d -> p (a c) d", p=P)[:, t, half * 512:(half + 1) * 512],
                             outt[:, t, half * 512:(half + 1) * 512]).then_inc(S("out_done"), 16)
            sp.wait_ge(S("out_done"), 16 * 2 * TC)

        @block.gpsimd
        def _(pool):
            pool.sem_inc(lo_ready, RING)
            whole, rest = divmod(NB, RING)

            def low(b, slot, i):
                pool.wait_ge(hi_ready, b + 1)
                pool.tensor_tensor(wlo[:, slot, :], raw[:, slot, :], whi[:, slot, :].bitcast(F32),
                                   ALU.subtract).then_inc(lo_ready, 1)

            with pool.Fori(0, whole) as i:
                for j in range(RING):
                    low(i * RING + j, j, i)
            for j in range(rest):
                low(whole * RING + j, j, whole)

        @block.tensor
        def _(pe):
            pe.sem_inc(block_used, RING)
            pe.wait_ge(S("eye_in"), 16)
            pe.wait_ge(S("vrows_in"), 16 * len(VECTORS))
            pe.transpose(psum[:, 5, 0:NVEC], vrows[0:NVEC, :], eye[0:NVEC, 0:NVEC]).then_inc(S("vec_turned"), 1)
            for c in range(DC):
                pe.wait_ge(S(f"x_in{c * X_PARTS // DC}"), 16)
                if c >= 2:
                    pe.wait_ge(S("x_turned"), c - 1)
                for t in range(TC):
                    mm = pe.transpose(psum[:, 6 + c % 2, t * P:(t + 1) * P], xin[:, t, c * P:(c + 1) * P], eye[:])
                mm.then_inc(S("x_tp"), 1)
            pe.wait_ge(S("ones_ready"), 1)
            pe_norm(pe, 0)
            pe_stage(pe, "u", ah, al, normed=0)
            pe_stage(pe, "vv", ah, al, cols_of=lambda t: slice(t * P, (t + 1) * P))
            pe.wait_ge(S("attn_in"), 16 * 5)
            for g in range(4):
                mm = pe.transpose(psum[:, 4, g * P:(g + 1) * P], wsp[:, g, :], eye[:])
            mm.then_inc(S("wsp_turned"), 1)
            pe_stage(pe, "qk", ah, al)
            pe.wait_ge(S("wspT_ready"), 1)
            pe.wait_ge(S("vv_normed"), TC)
            for g in range(4):
                for n in range(TC):
                    mm = pe.matmul(psum[:, 4 + g, n * P:(n + 1) * P], vv[:, n, g * P:(g + 1) * P], wspT[:, g, :],
                                   start=True, stop=True)
                mm.then_inc(S("mixed"), 1)
            pe_stage(pe, "v", ah, al, cols_of=lambda r: slice(r, T, 4))

            pe.wait_ge(S("sgu_done"), 4)
            pe.wait_ge(acc_free, first_acc["branch_attn"] + ACCS)

            def scores(u):
                h, r = divmod(u, 4)
                if u >= 2:
                    pe.wait_ge(S("scored"), u - 1)
                bank = 4 + 2 * (u % 2)
                at = slice(64 * (h % 2), 64 * (h % 2) + 64)
                for gi in range(3):
                    q, k = qk[at, 2 * gi + h // 2, r::4], qk[at, 6 + 2 * gi + h // 2, :]
                    o = psum[:, bank, :] if gi == 0 else psum[:, bank + 1, (gi - 1) * P:gi * P]
                    mm = pe.matmul(o, q, k if gi == 0 else k[:, r::4], start=True, stop=True)
                mm.then_inc(S("scores"), 1)

            def turn(u):
                pe.wait_ge(S("probs"), u + 1)
                s_ = sc[:, u % 2, :]
                if u >= 1:
                    pe.wait_ge(S("pT_ready"), 2 * u)
                for c in range(4):
                    pe.transpose(psum[:, 0, c * P:(c + 1) * P], s_[:, c:T:4], eye[:])
                for c in range(2):
                    mm = pe.transpose(psum[:, 1, c * P:(c + 1) * P], s_[:, T + c * P:T + (c + 1) * P], eye[:])
                mm.then_inc(S("p_turned"), 1)

            def values(u):
                h, r = divmod(u, 4)
                pe.wait_ge(S("pT_ready"), 2 * u + 2)
                if u >= 2:
                    pe.wait_ge(S("y_ready"), u - 1)
                for c in range(6):
                    gi, tile = (0, c) if c < 4 else (c - 3, r)
                    v0 = (gi * 4 + h) * HD
                    mm = pe.matmul(psum[:, 2 + u % 2, 0:HD], pT[:, c * P:(c + 1) * P], vt[:, tile, v0:v0 + HD],
                                   start=c == 0, stop=c == 5)
                mm.then_inc(S("attended"), 1)

            scores(0)
            scores(1)
            for u in range(16):
                turn(u)
                if u < 14:
                    scores(u + 2)
                values(u)
            pe.wait_ge(S("y_ready"), 16)
            for c in range(2):
                for r in range(4):
                    mm = pe.transpose(psum[:, 4 + c, r * P:(r + 1) * P], ya[:, r, c * P:(c + 1) * P], eye[:])
            mm.then_inc(S("y_turned"), 1)
            pe.wait_ge(S("yT_ready"), 2)
            pe_stage(pe, "branch_attn", yh, yl)
            pe_stage(pe, "gate_attn", ah, al)
            pe_stage(pe, "branch_sgu", yh[:, 2:6, :], yl[:, 2:6, :])
            pe_stage(pe, "gate_sgu", ah, al)
            pe.wait_ge(S("merge_split"), 8)

            def turn_memory():
                pe.wait_ge(S("mem_in"), 16)
                for c in range(DC):
                    for t in range(2):
                        at = (c % 2) * NM + t * P
                        mm = pe.transpose(psum[:, 4 + c // 2, at:at + P], memin[:, t, c * P:(c + 1) * P], eye[:])
                    mm.then_inc(S("mem_tp"), 1)

            pe_stage(pe, "out", ah, al, between={4: turn_memory})
            pe.wait_ge(S("mem_turned"), DC)
            pe_norm(pe, 1)
            pe_stage(pe, "cross_q", ah, al, normed=8, between={1: lambda: pe_norm(pe, 2, NM)})
            pe_stage(pe, "mem_k", mh, ml, NM, normed=16)
            pe_stage(pe, "mem_v", mh, ml, NM, cols_of=lambda t: slice(t * P, (t + 1) * P))
            pe.wait_ge(acc_free, first_acc["cross_o"] + ACCS)

            def cscores(u):
                h, t = divmod(u, 4)
                if u >= 2:
                    pe.wait_ge(S("cprobs"), u - 1)
                pe.matmul(psum[:, 4 + u % 2, 0:NM], cq[:, h, t * P:(t + 1) * P], ckT[:, h, :], start=True, stop=True)\
                  .then_inc(S("cscores"), 1)

            def cturn(u):
                h, t = divmod(u, 4)
                pe.wait_ge(S("cnormed"), u + 1)
                if t == 0 and h >= 1:
                    pe.wait_ge(S("cpT_ready"), 2 * h)
                for c in range(2):
                    mm = pe.transpose(psum[:, 6 + c, t * P:(t + 1) * P], cs[:, u % 4, c * P:(c + 1) * P], eye[:])
                mm.then_inc(S("cturned"), 1)

            def cout(h):
                pe.wait_ge(S("cpT_ready"), 2 * h + 2)
                for c in range(2):
                    mm = pe.matmul(psum[:, h, :], cv[:, c, h * P:(h + 1) * P], cpT[:, c, :], start=c == 0, stop=c == 1)
                mm.then_inc(S("cattended"), 1)

            for u in range(18):
                if u < 16:
                    cscores(u)
                if u >= 2:
                    cturn(u - 2)
                    if u % 4 == 1:
                        cout(u // 4 - 1)
            pe.wait_ge(S("co_split"), 4)
            pe_stage(pe, "cross_o", yh, yl)
            pe_norm(pe, 3)
            pe_stage(pe, "gate_up", ah, al, normed=24)
            pe.wait_ge(S("hid_split"), FC)
            pe_stage(pe, "down", hh, hl)
            pe_norm(pe, 4)
            pe_norm(pe, 5)
            pe_stage(pe, "glu", ah, al, normed=32)
            pe.wait_ge(S("crows_in"), 48)
            for k, rows in enumerate((P, CONV_K * 8 - P, SHORT_K * 24)):
                mm = pe.transpose(psum[:, 7, k * P:k * P + rows], crows[0:rows, k, :], eye[0:rows, 0:rows])
            mm.then_inc(S("crows_turned"), 1)
            pe.wait_ge(S("ab_split"), 1)
            for t in range(TC):
                o = psum[:, 5, t * 32:(t + 1) * 32]
                for k in range(DC):
                    tk = slice(t * P, (t + 1) * P)
                    pe.matmul(o, ah[:, k, tk], abh[:, k, :], start=k == 0, stop=False)
                    pe.matmul(o, ah[:, k, tk], abl[:, k, :], start=False, stop=False)
                    mm = pe.matmul(o, al[:, k, tk], abh[:, k, :], start=False, stop=k == DC - 1)
            mm.then_inc(S("ab_ready"), 1)
            pe.wait_ge(S("g_ready"), 1)
            for d in range(DIRS):
                pe.matmul(psum[:, 6, d * 64:(d + 1) * 64], incl[:, d, :], coef[:, 0, :, :].rearrange("p t u -> p (t u)"),
                          start=True, stop=True)
            pe.matmul(psum[:, 6, 128:192], ones[:], coef[:, 0, :, :].rearrange("p t u -> p (t u)"), start=True, stop=True)\
              .then_inc(S("cum_ready"), 1)
            pe_heads(pe)
            pe_stage(pe, "gate_a", ah, al)
            for c in range(DC):
                pe.wait_ge(S("conv_done"), c + 1)
                mm = pe.matmul(psum[:, 4, :], ones[:], cc[:, c, :], start=c == 0, stop=c == DC - 1)
            mm.then_inc(S("conv_sum"), 1)
            pe_stage(pe, "gate_b", ah, al)
            for c in range(DC):
                pe.wait_ge(S("csq_ready"), c + 1)
                pe.matmul(psum[:, 5, :], ones[:], sq[:, c % 2, :], start=c == 0, stop=c == DC - 1).then_inc(S("csq_used"), 1)
            pe.wait_ge(S("of_split"), DC)
            pe_stage(pe, "delta_out", zh, zl)
            pe.wait_ge(S("c_split"), DC)
            pe_stage(pe, "conv_out", ah, al)
            pe.wait_ge(S("y_split"), DC)
            pe_stage(pe, "o2", zh, zl)
            pe_norm(pe, 6)
            pe_stage(pe, "gate_up2", ah, al, normed=40)
            pe.wait_ge(S("hid_split"), 2 * FC)
            pe_stage(pe, "down2", hh, hl)
            pe_norm(pe, 7)
            pe.wait_ge(S("p_in"), 16)
            for c in range(2):
                for t in range(TC):
                    mm = pe.transpose(psum[:, 6 + c, t * P:(t + 1) * P], pin[:, t, c * P:(c + 1) * P], eye[:])
                mm.then_inc(S("pp_turned"), 1)
            pe.wait_ge(S("pp_split"), 2)
            pe_stage(pe, "pl_proj", ph, pl)
            pe_norm(pe, 8)
            pe.wait_ge(S("normed"), 56)
            pe_stage(pe, "pl_gate", ah, al)
            pe_norm(pe, 9)
            for n in range(2 * TC):
                half, t = divmod(n, TC)
                pe.wait_ge(S("n_ready"), 72 + 4 * (half + 1))
                if n >= 4:
                    pe.wait_ge(S("out_ready"), n - 3)
                for c in range(4):
                    mm = pe.transpose(psum[:, n % 4, c * P:(c + 1) * P], X[:, 4 * half + c, t * P:(t + 1) * P], eye[:])
                mm.then_inc(S("o_turned"), 1)

        @block.scalar
        def _(act):
            mine = Steps(act, S("act_own"))
            act.sem_inc(acc_free, ACCS)
            for b in range(LEAD):
                act_round(act, b, b, 0)
            for c in range(DC):
                act.wait_ge(S("x_turned"), c + 1)
                act_square(act, 0, c, X)
            act_inverse(act, mine, 0)
            act_norm_hi(act, 0, ah)
            act_stage(act, "u", lambda i, g, m, a, bank: act.activation(
                uu[:, g, :], psum[:, bank, :], ACT.Gelu_apprx_tanh))
            act_stage(act, "vv", lambda i, g, m, a, bank: act.activation(
                vv[:, 2 * m:2 * m + 2, g * 256:(g + 1) * 256], psum[:, bank, :].rearrange("p (t n) -> p t n", t=2),
                ACT.Gelu_apprx_tanh))
            act.wait_ge(acc_free, first_acc["qk"] + ACCS)
            for t in range(TC):
                if t:
                    act.wait_ge(S("ss_ready"), t)
                act.activation(sq[:, 0, :], vv[:, t, :], ACT.Square, accum_out=ss[:, t:t + 1]).then_inc(S("ss_ready"), 1)
            act.wait_ge(S("ss_ready"), TC)
            mine.did(act.activation(ss[:, 8:12], ss[:, 0:4], ACT.Ln, scale=1.0 / 512, bias=eps[:, 0:1]))
            mine.wait()
            act.activation(rs[:, 0:4], ss[:, 8:12], ACT.Exp, scale=-0.5).then_inc(S("rs_ready"), 1)
            act_stage(act, "qk", lambda i, g, m, a, bank: act.activation(
                qk[:, bass.ds(i * 4 + g, 1), :], psum[:, bank:bank + 1, :], ACT.Copy))
            for g in range(4):
                act.wait_ge(S("sgu_done"), g + 1)
                act.activation(yh[:, 2 + g, :], nt[:, g % 2, :], ACT.Copy).then_inc(S("sgu_hi"), 1)
            act.wait_ge(S("mixed"), 4)
            act.dma_start(dist[:], ins["dist"]).then_inc(S("dist_in"), 16)
            act_stage(act, "v", lambda i, g, m, a, bank: act.activation(
                vt[:, 2 * m:2 * m + 2, g * 256:(g + 1) * 256], psum[:, bank, :].rearrange("p (r n) -> p r n", r=2), ACT.Copy))

            def soft(u):
                act.wait_ge(S("scored"), u + 1)
                act.activation(sc[:, u % 2, :], sc[:, u % 2, :], ACT.Exp, scale=HD ** -0.5, bias=nmx[:, u:u + 1],
                               accum_out=den[:, u:u + 1]).then_inc(S("probs"), 1)

            def pT_copy(u):
                act.wait_ge(S("p_turned"), u + 1)
                if u:
                    act.wait_ge(S("attended"), u)
                act.activation(pT[:, 0:T], psum[:, 0, :], ACT.Copy).then_inc(S("pT_ready"), 1)
                act.activation(pT[:, T:768], psum[:, 1, 0:256], ACT.Copy).then_inc(S("pT_ready"), 1)

            soft(0)
            soft(1)
            for u in range(16):
                pT_copy(u)
                if u < 14:
                    soft(u + 2)
            act.wait_ge(S("y_turned"), 1)
            for c in range(2):
                act.activation(yh[:, c, :].rearrange("p (j r) -> p r j", r=4),
                               psum[:, 4 + c, :].rearrange("p (r j) -> p r j", r=4), ACT.Copy).then_inc(S("y_hi"), 1)

            act.wait_ge(S("y_ready"), 16)
            act.wait_ge(S("yT_ready"), 2)
            act_stage(act, "branch_attn", lambda i, g, m, a, bank: act.activation(
                m1[:, 4 * g + m, :], psum[:, bank, :], ACT.Copy))

            def stage_out(name, staged0, func, bias_of=None, after=None):
                s = by_name[name]
                a0 = first_acc[name]

                def empty(i, g, m, a, bank):
                    per = len(s.body) // s.kblocks * s.width
                    act.wait_ge(stage_used, i * per + (staged0 + a - a0 + 1))
                    kw = {} if bias_of is None else {"bias": bias_of(i, a - a0)}
                    return act.activation(stg[:, (staged0 + a - a0) % 4, :], psum[:, bank, :], func, **kw)

                act_stage(act, name, empty, after)

            def residual_out(name, staged0, n):
                def square(c):
                    act.wait_ge(stage_used, 4 + staged0 + c + 1)
                    act_square(act, n, c, X)

                stage_out(name, staged0, ACT.Copy, after=lambda c: square(c - 1) if c else None)
                square(DC - 1)

            bg = vec_at["b_gate"]
            stage_out("gate_attn", 0, ACT.Sigmoid, lambda i, k: vec[:, bass.ds(i * 4 + (bg + k), 1)])
            act_stage(act, "branch_sgu", lambda i, g, m, a, bank: act.activation(
                m2[:, 2 * g + m, :], psum[:, bank, :], ACT.Copy))
            stage_out("gate_sgu", 8, ACT.Sigmoid, lambda i, k: vec[:, bass.ds(i * 4 + (bg + 8 + k), 1)])
            act_split(act, "merged", 8, m1, ah, "merge_hi", 8)
            act.wait_ge(S("merge_split"), 8)
            act.dma_start(memin[:], ins["mem"].rearrange("a (c p) d -> p (a c) d", p=P)).then_inc(S("mem_in"), 16)
            residual_out("out", 16, 1)
            act_inverse(act, mine, 1)
            act_norm_hi(act, 1, ah)
            for c in range(DC):
                act.wait_ge(S("mem_turned"), c + 1)
                act_square(act, 2, c, memT, NM)
            act_stage(act, "cross_q", lambda i, g, m, a, bank: act.activation(
                cq[:, g, :], psum[:, bank, :], ACT.Copy), after=lambda k: act_inverse(act, mine, 2, NM) if k == 1 else None)
            act_norm_hi(act, 2, mh, NM)
            act_stage(act, "mem_k", lambda i, g, m, a, bank: act.activation(
                ckT[:, g, :], psum[:, bank, 0:NM], ACT.Copy))
            act_stage(act, "mem_v", lambda i, g, m, a, bank: act.activation(
                cv[:, :, g * 256:(g + 1) * 256], psum[:, bank, :].rearrange("p (t n) -> p t n", t=2), ACT.Copy))

            def csoft(u):
                act.wait_ge(S("cmaxed"), u + 1)
                if u >= 4:
                    act.wait_ge(S("cturned"), u - 3)
                act.activation(cs[:, u % 4, :], psum[:, 4 + u % 2, 0:NM], ACT.Exp, scale=P ** -0.5,
                               bias=cmx[:, u:u + 1], accum_out=cden[:, u:u + 1]).then_inc(S("cprobs"), 1)

            def cpT_copy(h):
                act.wait_ge(S("cturned"), 4 * h + 4)
                if h:
                    act.wait_ge(S("cattended"), h)
                for c in range(2):
                    act.activation(cpT[:, c, :], psum[:, 6 + c, :], ACT.Copy).then_inc(S("cpT_ready"), 1)

            def co_hi(h):
                act.wait_ge(S("cattended"), h + 1)
                act.activation(yh[:, h, :], psum[:, h, :], ACT.Copy).then_inc(S("co_hi"), 1)

            for u in range(16):
                csoft(u)
                if u % 4 == 0 and u > 0:
                    cpT_copy(u // 4 - 1)
                if u % 4 == 2 and u > 4:
                    co_hi(u // 4 - 1)
            cpT_copy(3)
            co_hi(3)
            residual_out("cross_o", 24, 3)
            act_inverse(act, mine, 3)
            act_norm_hi(act, 3, ah)

            def swiglu(name, staged, hid0):
                s = by_name[name]
                a0 = first_acc[name]
                act.wait_ge(stage_used, 4 + staged)

                def empty(i, g, m, a, bank):
                    act.wait_ge(S("hid"), i * 2 + (hid0 + g // 2 + 1))
                    return act.activation(stg[:, g, :], psum[:, bank, :], ACT.Silu if g % 2 == 0 else ACT.Copy)

                for i in passes(act, s):
                    for j in range(4):
                        q = first_block[name] + j + LEAD
                        act_round(act, count(s, i, j, LEAD), q, i)
                        act.wait_ge(block_used, count(s, i, j, RING + 1))
                        empty(i, j, 0, a0 + j, (a0 + j) % ACCS).then_inc(acc_free, 1)
                        if j % 2 == 1:
                            act.wait_ge(S("hid"), i * 2 + (hid0 + j // 2 + 3))
                            act.activation(hh[:, bass.ds(i * 2 + j // 2, 1), :], nt[:, j // 2:j // 2 + 1, :], ACT.Copy)\
                               .then_inc(S("hid_hi"), 1)

            swiglu("gate_up", 32, 0)
            residual_out("down", 32, 4)
            act_inverse(act, mine, 4)
            for c in range(DC):
                act.wait_ge(S("n_ready"), 32 + c + 1)
                act_square(act, 5, c, X)
            act_inverse(act, mine, 5)
            act_norm_hi(act, 5, ah)
            act.dma_start(level[:], ins["level"]).then_inc(S("masks_in"), 16)
            act.dma_start(incl[:], ins["incl"]).then_inc(S("masks_in"), 16)
            cw = ins["conv_dw_w_2"].rearrange("a k (c p) -> (a k c) p", p=P)
            act.dma_start(crows[:, 0, :], cw[0:P, :]).then_inc(S("crows_in"), 16)
            act.dma_start(crows[0:CONV_K * 8 - P, 1, :], cw[P:CONV_K * 8, :]).then_inc(S("crows_in"), 16)
            act.dma_start(crows[0:SHORT_K * 24, 2, :], ins["qkv_conv_w_2"].rearrange("a k (c p) -> (a k c) p", p=P))\
               .then_inc(S("crows_in"), 16)
            act.dma_start(abw[:], ins["w_in_2"].rearrange("a (c p) n -> p (a c) n", p=P)[:, :, 6 * D:6 * D + 32])\
               .then_inc(S("ab_in"), 16)
            act.dma_start(arow[:, 0, :], ins["a_log_2"].rearrange("a d h -> a (d h)").to_broadcast([P, 16])).then_inc(S("arow_in"), 16)
            act.dma_start(arow[:, 1, :], ins["dt_bias_2"].rearrange("a d h -> a (d h)").to_broadcast([P, 16])).then_inc(S("arow_in"), 16)
            act.dma_start(spill, X[:]).then_inc(S("spilled"), 16)
            act.wait_ge(S("ab_in"), 16)
            act.activation(abh[:], abw[:], ACT.Copy).then_inc(S("ab_hi"), 1)

            def glu_empty(i, g, m, a, bank):
                act.wait_ge(S("glu_done"), i * 2 + (g // 2 + 1))
                return act.activation(stg[:, g % 4, :], psum[:, bank, :], ACT.Sigmoid if g % 2 else ACT.Copy)

            act.wait_ge(stage_used, 4 + 40)
            act_stage(act, "glu", glu_empty)
            act.wait_ge(S("arow_in"), 32)
            act.activation(arow[:, 0, :], arow[:, 0, :], ACT.Exp).then_inc(S("alog_exp"), 1)
            act.wait_ge(S("ab_sum"), 1)
            act.activation(tmp[:, 1], tmp[:, 0], ACT.Abs).then_inc(S("ab_abs"), 1)
            act.wait_ge(S("ab_abs"), 1)
            act.activation(tmp[:, 2], tmp[:, 1], ACT.Exp, scale=-1.0).then_inc(S("ab_abs"), 1)
            act.wait_ge(S("ab_abs"), 2)
            act.activation(tmp[:, 1], tmp[:, 2], ACT.Ln, bias=1.0).then_inc(S("ab_abs"), 1)
            act.activation(coef[:, 1], ab[:, :, 16:32], ACT.Sigmoid).then_inc(S("beta_ready"), 1)
            act.wait_ge(S("tail_arg"), 1)
            act.activation(coef[:, 3], coef[:, 3], ACT.Exp).then_inc(S("coef_exp"), 1)
            act.activation(coef[:, 4], coef[:, 4], ACT.Exp).then_inc(S("coef_exp"), 1)
            act_heads(act)
            for c in range(DC):
                act.wait_ge(S("o_gated"), HEADS)
                act.wait_ge(S("conv_done"), DC)
                act.activation(zh[:, c, :], of[:, c, :], ACT.Copy).then_inc(S("of_hi"), 1)
            for name, dst in (("gate_a", ga), ("gate_b", gb)):
                act_stage(act, name, lambda i, g, m, a, bank, dst=dst: act.activation(
                    dst[:, bass.ds(i * 4 + g, 1), :], psum[:, bank:bank + 1, :], ACT.Sigmoid))
            for c in range(DC):
                act.wait_ge(S("centred"), c + 1)
                if c >= 2:
                    act.wait_ge(S("csq_used"), c - 1)
                act.activation(sq[:, c % 2, :], cc[:, c, :], ACT.Square).then_inc(S("csq_ready"), 1)
            act.wait_ge(S("csq_used"), DC)
            mine.did(act.activation(lnt[:], psum[:, 5, :], ACT.Ln, scale=1.0 / D, bias=eps[:, 1:2]))
            mine.wait()
            act.activation(rbc[:], lnt[:], ACT.Exp, scale=-0.5).then_inc(S("c_r"), 1)
            lb = vec_at["conv_ln_b_2"]
            for c in range(DC):
                act.wait_ge(S("c_scaled"), c + 1)
                mine.did(act.activation(cc[:, c, :], cc[:, c, :], ACT.Silu, bias=vec[:, lb + c:lb + c + 1]))
                mine.wait()
                act.activation(ah[:, c, :], cc[:, c, :], ACT.Copy).then_inc(S("c_hi"), 1)
            stage_out("delta_out", 40, ACT.Copy)
            stage_out("conv_out", 48, ACT.Copy)
            act.wait_ge(S("y_sum"), DC)
            act.dma_start(X[:], spill).then_inc(S("x_back"), 16)
            act_split(act, "y_sum", 0, gb, zh, "y_hi2", DC)
            residual_out("o2", 56, 6)
            act_inverse(act, mine, 6)
            act_norm_hi(act, 6, ah)
            swiglu("gate_up2", 64, FC)
            residual_out("down2", 64, 7)
            act.wait_ge(block_used, RING + first_block["pl_proj"])
            act.dma_start(pin[:], ins["p_2"].rearrange("a b (c p) d -> p (a b c) d", p=P)).then_inc(S("p_in"), 16)
            act_inverse(act, mine, 7)
            for c in range(2):
                act.wait_ge(S("pp_turned"), c + 1)
                act.activation(ph[:, c, :], psum[:, 6 + c, :], ACT.Copy).then_inc(S("pp_hi"), 1)
            act_norm_hi(act, 7, ah)
            act_stage(act, "pl_proj", lambda i, g, m, a, bank: act.activation(
                PL[:, 4 * g + m, :], psum[:, bank, :], ACT.Copy))
            act.wait_ge(acc_free, ACCS + first_acc["pl_proj"] + DC)
            for c in range(DC):
                act_square(act, 8, c, PL)
            act_inverse(act, mine, 8)

            def x_square(c):
                act.wait_ge(S("x_final"), c + 1)
                act_square(act, 9, c, X)

            stage_out("pl_gate", 72, ACT.Sigmoid, after=lambda c: x_square(c - 1) if c else None)
            x_square(DC - 1)
            act_inverse(act, mine, 9)
            for n in range(2 * TC):
                half, t = divmod(n, TC)
                act.wait_ge(S("o_turned"), n + 1)
                act.activation(outt[:, t, half * 512:(half + 1) * 512], psum[:, n % 4, :], ACT.Copy).then_inc(S("out_ready"), 1)

        @block.vector
        def _(dve):
            mine = Steps(dve, S("dve_own"))
            mine.did(dve.memset(ones[:], 1.0))
            mine.did(dve.memset(eps[:, 0:1], EPS))
            mine.did(dve.memset(eps[:, 1:2], LN_EPS))
            mine.wait()
            dve.wait_ge(S("vec_turned"), 1)
            dve.tensor_copy(vec[:], psum[:, 5, 0:NVEC]).then_inc(S("vec_ready"), 1)
            dve.sem_inc(S("ones_ready"), 1)
            dve.sem_inc(stage_used, 4)
            dve.sem_inc(S("hid"), 2)
            dve.sem_inc(S("glu_done"), 2)
            for c in range(DC):
                dve.wait_ge(S("x_tp"), c + 1)
                dve.tensor_copy(X[:, c, :], psum[:, 6 + c % 2, :]).then_inc(S("x_turned"), 1)
                if c >= 2:
                    dve_sum(dve, 0, c - 1)
            dve_sum(dve, 0, DC - 1)
            dve.wait_ge(S("vec_ready"), 1)
            dve_norm(dve, 0, 0, X, "g_mix", T, (ah, al))

            dve.wait_ge(S("attn_in"), 16 * 5)
            dve.wait_ge(S("wsp_turned"), 1)
            for g in range(4):
                ins_ = dve.tensor_tensor(wspT[:, g, :], psum[:, 4, g * P:(g + 1) * P], upper[:], ALU.mult)
            ins_.then_inc(S("wspT_ready"), 1)
            dve.wait_ge(S("rs_ready"), 1)
            for t in range(TC):
                dve.scalar_tensor_tensor(out=vv[:, t, :], in0=vv[:, t, :], scalar=rs[:, t:t + 1], in1=grow[:],
                                         op0=ALU.mult, op1=ALU.mult).then_inc(S("vv_normed"), 1)
            for g in range(4):
                dve.wait_ge(S("mixed"), g + 1)
                if g >= 2:
                    dve.wait_ge(S("sgu_lo"), g - 1)
                b_ = brow[:, g:g + 1, :].to_broadcast([P, TC, P])
                n_ = nt[:, g % 2, :].rearrange("p (t s) -> p t s", t=TC)
                mine.did(dve.tensor_tensor(n_, psum[:, 4 + g, :].rearrange("p (t s) -> p t s", t=TC), b_, ALU.add))
                mine.wait()
                dve.tensor_tensor(nt[:, g % 2, :], nt[:, g % 2, :], uu[:, g, :], ALU.mult).then_inc(S("sgu_done"), 1)
                dve.wait_ge(S("sgu_hi"), g + 1)
                dve.tensor_tensor(yl[:, 2 + g, :], nt[:, g % 2, :], yh[:, 2 + g, :].bitcast(F32), ALU.subtract)\
                   .then_inc(S("sgu_lo"), 1)

            def score(u):
                h, r = divmod(u, 4)
                bank = 4 + 2 * (u % 2)
                dve.wait_ge(S("scores"), u + 1)
                if u >= 2:
                    dve.wait_ge(S("p_turned"), u - 1)
                for gi in range(3):
                    k = -float(slopes[gi, h]) * HD ** 0.5
                    d_ = dist[:, r, :] if gi == 0 else dist2[:, gi - 1, :]
                    src = psum[:, bank, :] if gi == 0 else psum[:, bank + 1, (gi - 1) * P:gi * P]
                    dst = sc[:, u % 2, 0:T] if gi == 0 else sc[:, u % 2, T + (gi - 1) * P:T + gi * P]
                    mine.did(dve.scalar_tensor_tensor(out=dst, in0=d_, scalar=k, in1=src, op0=ALU.mult, op1=ALU.add))
                mine.wait()
                mine.did(dve.tensor_reduce(mx[:, u:u + 1], sc[:, u % 2, :], AX_X, ALU.max))
                mine.wait()
                dve.tensor_scalar(nmx[:, u:u + 1], mx[:, u:u + 1], -(HD ** -0.5), None, ALU.mult).then_inc(S("scored"), 1)

            def attend(u):
                h, r = divmod(u, 4)
                dve.wait_ge(S("probs"), u + 1)
                mine.did(dve.reciprocal(rden[:, u:u + 1], den[:, u:u + 1]))
                mine.wait()
                dve.wait_ge(S("attended"), u + 1)
                dve.tensor_scalar(ya[:, r, h * HD:(h + 1) * HD], psum[:, 2 + u % 2, 0:HD], rden[:, u:u + 1], None,
                                  ALU.mult).then_inc(S("y_ready"), 1)

            dve.wait_ge(S("dist_in"), 16)
            score(0)
            score(1)
            for u in range(16):
                if u < 14:
                    score(u + 2)
                attend(u)
            for c in range(2):
                dve.wait_ge(S("y_hi"), c + 1)
                dve.tensor_tensor(yl[:, c, :].rearrange("p (j r) -> p r j", r=4),
                                  psum[:, 4 + c, :].rearrange("p (r j) -> p r j", r=4),
                                  yh[:, c, :].rearrange("p (j r) -> p r j", r=4).bitcast(F32), ALU.subtract)\
                   .then_inc(S("yT_ready"), 1)

            def per_stage(name, fn):
                s = by_name[name]
                per = len(s.body) // s.kblocks * s.width
                for i in passes(dve, s):
                    for k in range(per):
                        dve.wait_ge(acc_free, i * per + (first_acc[name] + k + 1 + ACCS))
                        fn(i, k, per)

            def gate1(i, k, per):
                c = bass.ds(i * per + k, 1)
                dve.tensor_tensor(m1[:, c, :], stg[:, k:k + 1, :], m1[:, c, :], ALU.mult).then_inc(stage_used, 1)

            def gate2(i, k, per):
                c = bass.ds(i * per + k, 1)
                dve.tensor_tensor(m2[:, c, :], stg[:, k:k + 1, :], m2[:, c, :], ALU.mult).then_inc(stage_used, 1)
                dve.wait_ge(stage_used, i * per + (4 + 8 + k + 1))
                dve.tensor_tensor(m1[:, c, :], m1[:, c, :], m2[:, c, :], ALU.add).then_inc(S("merged"), 1)

            per_stage("gate_attn", gate1)
            dve.sem_inc(S("merged"), 8)
            per_stage("gate_sgu", gate2)
            for c in range(8):
                dve.wait_ge(S("merge_hi"), c + 1)
                dve.tensor_tensor(al[:, c, :], m1[:, c, :], ah[:, c, :].bitcast(F32), ALU.subtract)\
                   .then_inc(S("merge_split"), 1)

            def residual(name, staged0, n):
                def add(i, k, per):
                    c = bass.ds(i * per + k, 1) if per < 8 else slice(k, k + 1)
                    sl = (staged0 + k) % 4
                    dve.tensor_tensor(X[:, c, :], X[:, c, :], stg[:, sl:sl + 1, :], ALU.add).then_inc(stage_used, 1)
                    if k >= 2:
                        dve_sum(dve, n, k - 1)
                per_stage(name, add)
                dve_sum(dve, n, DC - 1)

            residual("out", 16, 1)
            for c in range(DC):
                dve.wait_ge(S("mem_tp"), c + 1)
                dve.tensor_copy(memT[:, c, :], psum[:, 4 + c // 2, (c % 2) * NM:(c % 2 + 1) * NM]).then_inc(S("mem_turned"), 1)
            dve_norm(dve, 1, 1, X, "g_cross", T, (ah, al))
            for c in range(1, DC):
                dve_sum(dve, 2, c, NM)
            dve_norm(dve, 2, 2, memT, "g_mem", NM, (mh, ml))

            def cmaxes(u):
                dve.wait_ge(S("cscores"), u + 1)
                mine.did(dve.tensor_reduce(crd[:, u:u + 1], psum[:, 4 + u % 2, 0:NM], AX_X, ALU.max))
                mine.wait()
                dve.tensor_scalar(cmx[:, u:u + 1], crd[:, u:u + 1], -(P ** -0.5), None, ALU.mult).then_inc(S("cmaxed"), 1)

            def cnorm(u):
                dve.wait_ge(S("cprobs"), u + 1)
                mine.did(dve.reciprocal(crd[:, u:u + 1], cden[:, u:u + 1]))
                mine.wait()
                dve.tensor_scalar(cs[:, u % 4, :], cs[:, u % 4, :], crd[:, u:u + 1], None, ALU.mult)\
                   .then_inc(S("cnormed"), 1)

            def co_lo(h):
                dve.wait_ge(S("co_hi"), h + 1)
                dve.tensor_tensor(yl[:, h, :], psum[:, h, :], yh[:, h, :].bitcast(F32), ALU.subtract)\
                   .then_inc(S("co_split"), 1)

            cmaxes(0)
            for u in range(16):
                if u < 15:
                    cmaxes(u + 1)
                cnorm(u)
            for h in range(4):
                co_lo(h)
            residual("cross_o", 24, 3)
            dve_norm(dve, 3, 3, X, "g_ffn", T, (ah, al))

            def swiglu(name, staged, hid0):
                s = by_name[name]
                for i in passes(dve, s):
                    for k in range(2):
                        dve.wait_ge(acc_free, i * 4 + (first_acc[name] + 2 * k + 2 + ACCS))
                        dve.tensor_tensor(nt[:, k, :], stg[:, 2 * k, :], stg[:, 2 * k + 1, :], ALU.mult).then_inc(S("hid"), 1)
                        dve.wait_ge(S("hid_hi"), i * 2 + (hid0 + k + 1))
                        dve.tensor_tensor(hl[:, bass.ds(i * 2 + k, 1), :], nt[:, k:k + 1, :],
                                          hh[:, bass.ds(i * 2 + k, 1), :].bitcast(F32), ALU.subtract)\
                           .then_inc(S("hid_split"), 1)

            swiglu("gate_up", 32, 0)
            residual("down", 32, 4)
            dve_norm(dve, 4, 0, X, "g_final", after=lambda c: dve_sum(dve, 5, c - 1) if c >= 2 else None)
            dve_sum(dve, 5, DC - 1)
            dve_norm(dve, 5, 4, X, "g_mix_2", T, (ah, al))
            dve.wait_ge(S("ab_hi"), 1)
            dve.tensor_tensor(abl[:], abw[:], abh[:].bitcast(F32), ALU.subtract).then_inc(S("ab_split"), 1)
            mine.did(dve.memset(cp[:, :, 0:CONV_PAD], 0.0))
            mine.did(dve.memset(cp[:, :, CONV_PAD + T:], 0.0))

            s = by_name["glu"]
            for i in passes(dve, s):
                for k in range(2):
                    dve.wait_ge(acc_free, i * 4 + (first_acc["glu"] + 2 * k + 2 + ACCS))
                    dve.tensor_tensor(cp[:, bass.ds(i * 2 + k, 1), CONV_PAD:CONV_PAD + T], stg[:, 2 * k:2 * k + 1, :],
                                      stg[:, 2 * k + 1:2 * k + 2, :], ALU.mult).then_inc(S("glu_done"), 1)
            dve.wait_ge(S("crows_turned"), 1)
            dve.tensor_copy(conv_w[:], psum[:, 7, 0:CONV_K * 8])
            dve.tensor_copy(short_w[:], psum[:, 7, 2 * P:2 * P + SHORT_K * 24]).then_inc(S("taps_ready"), 1)
            dve.wait_ge(S("taps_ready"), 1)
            dve.wait_ge(S("spilled"), 16)
            mine.wait()
            dve.wait_ge(S("glu_done"), 2 + 8)
            dve.wait_ge(S("ab_ready"), 1)
            mine.did(dve.tensor_copy(ab[:], psum[:, 5, 0:128].rearrange("p (t u) -> p t u", t=TC)))
            mine.wait()
            dtb = arow[:, 1:2, :].to_broadcast([P, TC, 16])
            dve.wait_ge(S("arow_in"), 32)
            dve.tensor_tensor(tmp[:, 0], ab[:, :, 0:16], dtb, ALU.add).then_inc(S("ab_sum"), 1)
            dve.wait_ge(S("ab_abs"), 3)
            mine.did(dve.scalar_tensor_tensor(out=tmp[:, 2], in0=tmp[:, 0], scalar=0.0, in1=tmp[:, 1], op0=ALU.max, op1=ALU.add))
            mine.wait()
            dve.wait_ge(S("alog_exp"), 1)
            dve.scalar_tensor_tensor(out=coef[:, 0], in0=tmp[:, 2], scalar=-1.0, in1=arow[:, 0:1, :].to_broadcast([P, TC, 16]),
                                     op0=ALU.mult, op1=ALU.mult).then_inc(S("g_ready"), 1)
            dve.wait_ge(S("masks_in"), 32)
            dve.wait_ge(S("cum_ready"), 1)
            cum = [psum[:, 6, d * 64:(d + 1) * 64].rearrange("p (t u) -> p t u", t=TC) for d in range(3)]
            for d in range(DIRS):
                u = slice(8 * d, 8 * d + 8)
                mine.did(dve.tensor_scalar(coef[:, 2, :, u], cum[d][:, :, u], -1.0, None, ALU.mult))
            mine.wait()
            mine.did(dve.tensor_tensor(coef[:, 3], cum[2], coef[:, 2], ALU.add))
            mine.did(dve.tensor_copy(coef[:, 4], cum[2]))
            mine.wait()
            dve.tensor_scalar(coef[:, 3], coef[:, 3], 0.0, None, ALU.min).then_inc(S("tail_arg"), 1)

            dve_heads(dve, mine)
            for c in range(8):
                dve.wait_ge(S("of_hi"), c + 1)
                dve.tensor_tensor(zl[:, c, :], of[:, c, :], zh[:, c, :].bitcast(F32), ALU.subtract).then_inc(S("of_split"), 1)
            dve.wait_ge(S("conv_sum"), 1)
            mine.did(dve.tensor_scalar(mu, psum[:, 4, :], 1.0 / D, None, ALU.mult))
            mine.wait()
            for c in range(DC):
                dve.tensor_tensor(cc[:, c, :], cc[:, c, :], mu, ALU.subtract).then_inc(S("centred"), 1)
            dve.wait_ge(S("c_r"), 1)
            lg = vec_at["conv_ln_g_2"]
            for c in range(DC):
                dve.scalar_tensor_tensor(out=cc[:, c, :], in0=cc[:, c, :], scalar=vec[:, lg + c:lg + c + 1], in1=rbc[:],
                                         op0=ALU.mult, op1=ALU.mult).then_inc(S("c_scaled"), 1)
            for c in range(DC):
                dve.wait_ge(S("c_hi"), c + 1)
                dve.tensor_tensor(al[:, c, :], cc[:, c, :], ah[:, c, :].bitcast(F32), ALU.subtract).then_inc(S("c_split"), 1)

            def gate_delta(i, k, per):
                c = bass.ds(i * per + k, 1)
                dve.tensor_tensor(gb[:, c, :], stg[:, k:k + 1, :], gb[:, c, :], ALU.mult).then_inc(stage_used, 1)

            def gate_conv(i, k, per):
                c = bass.ds(i * per + k, 1)
                dve.tensor_tensor(ga[:, c, :], stg[:, k:k + 1, :], ga[:, c, :], ALU.mult).then_inc(stage_used, 1)
                dve.wait_ge(stage_used, i * per + (4 + 48 + k + 1))
                dve.tensor_tensor(gb[:, c, :], gb[:, c, :], ga[:, c, :], ALU.add).then_inc(S("y_sum"), 1)

            per_stage("delta_out", gate_delta)
            per_stage("conv_out", gate_conv)
            for c in range(8):
                dve.wait_ge(S("y_hi2"), c + 1)
                dve.tensor_tensor(zl[:, c, :], gb[:, c, :], zh[:, c, :].bitcast(F32), ALU.subtract).then_inc(S("y_split"), 1)
            dve.wait_ge(S("x_back"), 16)
            residual("o2", 56, 6)
            dve_norm(dve, 6, 5, X, "g_ffn_2", T, (ah, al))
            swiglu("gate_up2", 64, FC)
            residual("down2", 64, 7)
            for c in range(2):
                dve.wait_ge(S("pp_hi"), c + 1)
                dve.tensor_tensor(pl[:, c, :], psum[:, 6 + c, :], ph[:, c, :].bitcast(F32), ALU.subtract)\
                   .then_inc(S("pp_split"), 1)
            dve_norm(dve, 7, 6, X, "g_pl_2", T, (ah, al))
            for c in range(1, DC):
                dve_sum(dve, 8, c)
            dve_norm(dve, 8, 0, PL, "g_pl_proj_2")

            def gate_pl(i, k, per):
                c = i * per + k
                dve.tensor_tensor(PL[:, c, :], stg[:, k % 4, :], PL[:, c, :], ALU.mult).then_inc(stage_used, 1)
                dve.wait_ge(stage_used, 4 + 72 + c + 1)
                dve.tensor_tensor(X[:, c, :], X[:, c, :], PL[:, c, :], ALU.add).then_inc(S("x_final"), 1)
                if c >= 2:
                    dve_sum(dve, 9, c - 1)

            dve.wait_ge(S("n_ready"), 72)
            per_stage("pl_gate", gate_pl)
            dve_sum(dve, 9, DC - 1)
            dve.wait_ge(S("x_final"), 8)
            dve_norm(dve, 9, 0, X, "g_final_2")


_INS = ["x", "mem", "g_mix", "w_in", "b_gate", "w_sgu_spatial", "b_sgu_spatial", "g_sgu", "w_branch_attn",
        "w_branch_sgu", "w_out", "g_cross", "g_mem", "w_q_cross", "w_kv_cross", "w_o_cross", "g_ffn", "w_gate_up",
        "w_down", "g_final", "p_2", "g_mix_2", "w_in_2", "conv_dw_w_2", "conv_dw_b_2", "conv_ln_g_2", "conv_ln_b_2",
        "w_conv_out_2", "qkv_conv_w_2", "a_log_2", "dt_bias_2", "delta_norm_g_2", "w_delta_out_2", "w_o_2",
        "g_ffn_2", "w_gate_up_2", "w_down_2", "g_pl_2", "w_pl_gate_2", "w_pl_proj_2", "g_pl_proj_2", "g_final_2"]


def kernel(**inputs):
    import concourse.bacc as bacc
    from concourse.bass_utils import run_bass_kernel_spmd

    nc = bacc.Bacc("TRN2", target_bir_lowering=False, num_devices=1)
    arrays, aps = {}, {}
    for name, a in [(n, inputs[n]) for n in _INS] + list(shape_constants().items()):
        a = np.ascontiguousarray(a)
        arrays[f"in_{name}"] = a
        aps[name] = nc.dram_tensor(f"in_{name}", a.shape, mybir.dt.from_np(a.dtype), kind="ExternalInput").ap()
    out = nc.dram_tensor("out_0", (1, T, D), F32, kind="ExternalOutput").ap()
    build(nc, aps, out)
    r = run_bass_kernel_spmd(nc, [arrays], core_ids=[0])
    return r.results[0]["out_0"]
```
